# Optimizing a Trainium2 kernel written in Bass

```python
import math
import jax, jax.numpy as jnp
from jax import lax
import numpy as np

D_MODEL = 1024
BATCH = 1
SEQ = 1024
DEPTH = 1
DEC_BATCH = 1
DEC_SEQ = 64
PAST_LEN = 128

CHUNK = 64
D_MIX = D_MODEL
H_A = 4
DK_A = 128
DV_A = 128
CONV_W = 4
CONV_DIM = H_A * (2 * DK_A + DV_A)
A_WIDTH = H_A * DV_A
H_B = 8
DH_B = 64
B_WIDTH = H_B * DH_B
Q_BLOCK = 128
OFF1 = CONV_DIM
OFF2 = OFF1 + H_A
OFF3 = OFF2 + H_A
OFF4 = OFF3 + A_WIDTH
OFF5 = OFF4 + 3 * B_WIDTH
IN_COLS = OFF5 + H_B
N_KEYS = 128
N_EXPERTS = N_KEYS * N_KEYS
PEER_HEADS = 8
PEER_DQ = 256
PEER_TOPK = 16
PEER_TB = 128
PLE_DIM = 256
EPS = 1e-6

kernel_name = "hymba_gdn_fox_peer_stream_step"

def rmsnorm(x, g):
    x32 = x.astype(jnp.float32)
    y = x32 * lax.rsqrt(jnp.mean(x32 * x32, axis=-1, keepdims=True) + EPS)
    return (y * g.astype(jnp.float32)).astype(x.dtype)

def l2norm(x):
    x32 = x.astype(jnp.float32)
    return x32 * lax.rsqrt(jnp.sum(x32 * x32, axis=-1, keepdims=True) + EPS)

def causal_conv_silu(u, prefix, w):
    T = u.shape[1]
    full = jnp.concatenate([prefix.astype(u.dtype), u], axis=1)
    y = full[:, 0:T] * w[0]
    for j in range(1, CONV_W):
        y = y + full[:, j:j + T] * w[j]
    return jax.nn.silu(y), full[:, T:]

def gdn_chunk(S, q, k, v, beta, la):
    L = q.shape[2]
    g = jnp.cumsum(la, axis=-1)
    causal = jnp.tril(jnp.ones((L, L), dtype=bool))
    strict = jnp.tril(jnp.ones((L, L), dtype=bool), -1)
    decay = jnp.exp(jnp.where(causal, g[..., :, None] - g[..., None, :], -jnp.inf))
    kb = k * beta[..., None]
    M = jnp.where(strict, jnp.einsum('bhtd,bhsd->bhts', kb, k) * decay, 0.0)
    eg = jnp.exp(g)[..., None]
    rhs = jnp.concatenate([v * beta[..., None], kb * eg], axis=-1)
    sol = lax.linalg.triangular_solve(M, rhs, left_side=True, lower=True, unit_diagonal=True)
    u = sol[..., :DV_A] - jnp.einsum('bhtk,bhkv->bhtv', sol[..., DV_A:], S)
    attn = jnp.einsum('bhtd,bhsd->bhts', q, k) * decay
    o = jnp.einsum('bhtk,bhkv->bhtv', q * eg, S) + jnp.einsum('bhts,bhsv->bhtv', attn, u)
    gL = g[..., -1]
    S_new = jnp.exp(gL)[..., None, None] * S + jnp.einsum(
        'bhsk,bhsv->bhkv', k * jnp.exp(gL[..., None] - g)[..., None], u)
    return S_new, o

def gdn_recurrence(S0, q, k, v, beta, la):
    Bn, Hn, T = q.shape[:3]
    C = min(CHUNK, T)
    n = T // C

    def split(a):
        return jnp.moveaxis(a.reshape((Bn, Hn, n, C) + a.shape[3:]), 2, 0)

    S, o = lax.scan(lambda s, xs: gdn_chunk(s, *xs), S0,
                    (split(q), split(k), split(v), split(beta), split(la)))
    return jnp.moveaxis(o, 0, 2).reshape(Bn, Hn, T, DV_A), S

def gdn_mixer(z_qkv, z_b, z_a, z_g, conv_prefix, S0, conv_w, a_log, dt_bias, onorm):
    Bn, T, _ = z_qkv.shape
    c, conv_state = causal_conv_silu(z_qkv, conv_prefix, conv_w)
    c = c.astype(jnp.float32)
    q = l2norm(c[..., :H_A * DK_A].reshape(Bn, T, H_A, DK_A)) * (DK_A ** -0.5)
    k = l2norm(c[..., H_A * DK_A:2 * H_A * DK_A].reshape(Bn, T, H_A, DK_A))
    v = c[..., 2 * H_A * DK_A:].reshape(Bn, T, H_A, DV_A)
    beta = jax.nn.sigmoid(z_b.astype(jnp.float32))
    la = -jnp.exp(a_log.astype(jnp.float32)) * jax.nn.softplus(
        z_a.astype(jnp.float32) + dt_bias.astype(jnp.float32))
    tr = lambda t: jnp.swapaxes(t, 1, 2)
    o, S = gdn_recurrence(S0.astype(jnp.float32), tr(q), tr(k), tr(v), tr(beta), tr(la))
    o = rmsnorm(tr(o), onorm) * jax.nn.silu(z_g.reshape(Bn, T, H_A, DV_A).astype(jnp.float32))
    return o.reshape(Bn, T, A_WIDTH).astype(z_qkv.dtype), conv_state, S

def fox_attend(q, k, v, logf):
    Bn, T = q.shape[:2]
    Tk = k.shape[1]
    c = jnp.swapaxes(jnp.cumsum(logf.astype(jnp.float32), axis=1), 1, 2)
    qb = min(Q_BLOCK, T)
    nb = T // qb
    q_blocks = jnp.moveaxis(q.reshape(Bn, nb, qb, H_B, DH_B), 1, 0)
    c_q = jnp.moveaxis(c[:, :, Tk - T:].reshape(Bn, H_B, nb, qb), 2, 0)
    pos_q = (Tk - T + jnp.arange(T)).reshape(nb, qb)
    pos_k = jnp.arange(Tk)

    def block(args):
        qi, cqi, pqi = args
        s = jnp.einsum('bqhd,bkhd->bhqk', qi, k).astype(jnp.float32) * (DH_B ** -0.5)
        s = s + cqi[..., None] - c[:, :, None, :]
        s = jnp.where(pqi[:, None] >= pos_k[None, :], s, -jnp.inf)
        p = jax.nn.softmax(s, axis=-1)
        return jnp.einsum('bhqk,bkhd->bqhd', p.astype(v.dtype), v)

    o = lax.map(block, (q_blocks, c_q, pos_q))
    return jnp.moveaxis(o, 0, 1).reshape(Bn, T, H_B, DH_B)

def fox_mixer(z_qkv, z_f, past_k, past_v, past_logf, b_f, onorm):
    Bn, T, _ = z_qkv.shape
    q = z_qkv[..., :B_WIDTH].reshape(Bn, T, H_B, DH_B)
    k = z_qkv[..., B_WIDTH:2 * B_WIDTH].reshape(Bn, T, H_B, DH_B)
    v = z_qkv[..., 2 * B_WIDTH:].reshape(Bn, T, H_B, DH_B)
    logf = jax.nn.log_sigmoid(z_f.astype(jnp.float32) + b_f.astype(jnp.float32))
    if past_k is None:
        k_all, v_all, lf_all = k, v, logf
    else:
        k_all = jnp.concatenate([past_k.astype(k.dtype), k], axis=1)
        v_all = jnp.concatenate([past_v.astype(v.dtype), v], axis=1)
        lf_all = jnp.concatenate([past_logf.astype(jnp.float32), logf], axis=1)
    o = rmsnorm(fox_attend(q, k_all, v_all, lf_all), onorm)
    return o.reshape(Bn, T, B_WIDTH), k, v, logf

def peer(x, w_q, sub_keys, u_tab, v_tab):
    Bn, T, D = x.shape
    n = Bn * T
    nb = -(-n // PEER_TB)
    xt = jnp.pad(x.reshape(n, D), ((0, nb * PEER_TB - n), (0, 0))).reshape(nb, PEER_TB, D)
    keys32 = sub_keys.astype(jnp.float32)

    def block(xb):
        q = (xb @ w_q).reshape(PEER_TB, PEER_HEADS, 2, PEER_DQ // 2).astype(jnp.float32)
        s = jnp.einsum('thcd,cnd->thcn', q, keys32)
        sv, si = lax.top_k(s, PEER_TOPK)
        cand = sv[:, :, 0, :, None] + sv[:, :, 1, None, :]
        cv, ci = lax.top_k(cand.reshape(PEER_TB, PEER_HEADS, PEER_TOPK * PEER_TOPK), PEER_TOPK)
        i1 = jnp.take_along_axis(si[:, :, 0, :], ci // PEER_TOPK, axis=-1)
        i2 = jnp.take_along_axis(si[:, :, 1, :], ci % PEER_TOPK, axis=-1)
        e = i1 * N_KEYS + i2
        gate = jax.nn.softmax(cv, axis=-1)
        a = jnp.einsum('thkd,td->thk', jnp.take(u_tab, e, axis=0), xb).astype(jnp.float32)
        wgt = (gate * jax.nn.gelu(a, approximate=False)).astype(xb.dtype)
        return jnp.einsum('thk,thkd->td', wgt, jnp.take(v_tab, e, axis=0))

    y = lax.map(block, xt).reshape(nb * PEER_TB, D)[:n]
    return y.reshape(Bn, T, D)

def layer(h, p, conv_prefix, s0, past_k, past_v, past_logf, w):
    (w_in, conv_w, a_log, dt_bias, gdn_onorm, b_f, fox_onorm, w_out, norm_mix, norm_ffn,
     peer_wq, peer_keys, peer_u, peer_v, norm_ple, w_ple_proj, w_ple_gate) = w
    Bn = h.shape[0]
    a = rmsnorm(h, norm_mix)
    z = a @ w_in
    za_qkv, za_b, za_a, za_g, zb_qkv, zb_f = jnp.split(z, [OFF1, OFF2, OFF3, OFF4, OFF5], axis=-1)
    if conv_prefix is None:
        conv_prefix = jnp.zeros((Bn, CONV_W - 1, CONV_DIM), h.dtype)
    if s0 is None:
        s0 = jnp.zeros((Bn, H_A, DK_A, DV_A), jnp.float32)
    o_a, conv_state, S = gdn_mixer(za_qkv, za_b, za_a, za_g, conv_prefix, s0,
                                   conv_w, a_log, dt_bias, gdn_onorm)
    o_b, k_new, v_new, lf_new = fox_mixer(zb_qkv, zb_f, past_k, past_v, past_logf, b_f, fox_onorm)
    h = h + jnp.concatenate([o_a, o_b.astype(o_a.dtype)], axis=-1) @ w_out
    h = h + peer(rmsnorm(h, norm_ffn), peer_wq, peer_keys, peer_u, peer_v)
    gate = jax.nn.sigmoid((rmsnorm(h, norm_ple) @ w_ple_gate).astype(jnp.float32))
    h = h + ((p @ w_ple_proj).astype(jnp.float32) * gate).astype(h.dtype)
    return h, conv_state, S, k_new, v_new, lf_new

def setup_inputs(seed: int = 0) -> dict:
    key = jax.random.key(seed)
    ks = jax.random.split(key, 32)
    f32 = jnp.float32
    nrm = lambda k, shape, s=1.0: jax.random.normal(k, shape, f32) * s
    gain = lambda k, shape: 1.0 + 0.05 * jax.random.normal(k, shape, f32)
    dt = jnp.exp(jax.random.uniform(ks[10], (DEPTH, H_A), f32, math.log(1e-3), math.log(1e-1)))
    return {
        "x_prompt": nrm(ks[0], (BATCH, SEQ, D_MODEL)),
        "x_sample": nrm(ks[1], (DEC_BATCH, DEC_SEQ, D_MODEL)),
        "p_prompt": nrm(ks[2], (DEPTH, BATCH, SEQ, PLE_DIM)),
        "p_sample": nrm(ks[3], (DEPTH, DEC_BATCH, DEC_SEQ, PLE_DIM)),
        "cache_conv": nrm(ks[4], (DEPTH, DEC_BATCH, CONV_W - 1, CONV_DIM)),
        "state_gdn": nrm(ks[5], (DEPTH, DEC_BATCH, H_A, DK_A, DV_A), 0.1),
        "cache_fox_k": nrm(ks[6], (DEPTH, DEC_BATCH, PAST_LEN, H_B, DH_B)),
        "cache_fox_v": nrm(ks[7], (DEPTH, DEC_BATCH, PAST_LEN, H_B, DH_B)),
        "cache_fox_logf": jax.nn.log_sigmoid(nrm(ks[8], (DEPTH, DEC_BATCH, PAST_LEN, H_B)) + 3.0),
        "w_in": nrm(ks[9], (DEPTH, D_MODEL, IN_COLS), D_MODEL ** -0.5),
        "conv_w": jax.random.uniform(ks[11], (DEPTH, CONV_W, CONV_DIM), f32, -0.5, 0.5),
        "a_log": jnp.log(jax.random.uniform(ks[12], (DEPTH, H_A), f32, 1.0, 16.0)),
        "dt_bias": dt + jnp.log(-jnp.expm1(-dt)),
        "gdn_onorm": gain(ks[13], (DEPTH, DV_A)),
        "b_f": jax.random.uniform(ks[14], (DEPTH, H_B), f32, 1.0, 5.0),
        "fox_onorm": gain(ks[15], (DEPTH, DH_B)),
        "w_out": nrm(ks[16], (DEPTH, D_MIX, D_MODEL), D_MIX ** -0.5),
        "norm_mix": gain(ks[17], (DEPTH, D_MODEL)),
        "norm_ffn": gain(ks[18], (DEPTH, D_MODEL)),
        "peer_wq": nrm(ks[19], (DEPTH, D_MODEL, PEER_HEADS * PEER_DQ), D_MODEL ** -0.5),
        "peer_keys": nrm(ks[20], (DEPTH, 2, N_KEYS, PEER_DQ // 2), (PEER_DQ // 2) ** -0.5),
        "peer_u": nrm(ks[21], (DEPTH, N_EXPERTS, D_MODEL), D_MODEL ** -0.5),
        "peer_v": nrm(ks[22], (DEPTH, N_EXPERTS, D_MODEL), 0.5),
        "norm_ple": gain(ks[23], (DEPTH, D_MODEL)),
        "w_ple_proj": nrm(ks[24], (DEPTH, PLE_DIM, D_MODEL), PLE_DIM ** -0.5),
        "w_ple_gate": nrm(ks[25], (DEPTH, D_MODEL, D_MODEL), D_MODEL ** -0.5),
        "norm_final": gain(ks[26], (D_MODEL,)),
    }

def reference(x_prompt, x_sample, p_prompt, p_sample, cache_conv, state_gdn, cache_fox_k,
              cache_fox_v, cache_fox_logf, w_in, conv_w, a_log, dt_bias, gdn_onorm, b_f,
              fox_onorm, w_out, norm_mix, norm_ffn, peer_wq, peer_keys, peer_u, peer_v,
              norm_ple, w_ple_proj, w_ple_gate, norm_final):
    hp, hs = x_prompt, x_sample
    cp, sp, kp, vp, lp = [], [], [], [], []
    cs, ss, ksm, vs, ls = [], [], [], [], []
    for i in range(DEPTH):
        w = (w_in[i], conv_w[i], a_log[i], dt_bias[i], gdn_onorm[i], b_f[i], fox_onorm[i],
             w_out[i], norm_mix[i], norm_ffn[i], peer_wq[i], peer_keys[i], peer_u[i],
             peer_v[i], norm_ple[i], w_ple_proj[i], w_ple_gate[i])
        hp, c1, s1, k1, v1, l1 = layer(hp, p_prompt[i], None, None, None, None, None, w)
        hs, c2, s2, k2, v2, l2 = layer(hs, p_sample[i], cache_conv[i], state_gdn[i],
                                       cache_fox_k[i], cache_fox_v[i], cache_fox_logf[i], w)
        cp.append(c1); sp.append(s1); kp.append(k1); vp.append(v1); lp.append(l1)
        cs.append(c2); ss.append(s2); ksm.append(k2); vs.append(v2); ls.append(l2)
    y_prompt = rmsnorm(hp, norm_final)
    y_sample = rmsnorm(hs, norm_final)
    return (y_prompt, y_sample,
            jnp.stack(cp), jnp.stack(sp), jnp.stack(kp), jnp.stack(vp), jnp.stack(lp),
            jnp.stack(cs), jnp.stack(ss), jnp.stack(ksm), jnp.stack(vs), jnp.stack(ls))


_drawn_inputs = setup_inputs


def setup_inputs(seed=0):
    import zlib

    import numpy as np

    out = dict(_drawn_inputs(seed))
    spreads = {}
    factors = {'norm_ple': 7.733}
    for name, (base, spread) in spreads.items():
        noise = np.random.default_rng([zlib.crc32(name.encode()), seed]).standard_normal(out[name].shape)
        drawn = base * np.exp(spread * noise) if base else spread * noise
        out[name] = __import__('jax').numpy.asarray(drawn.astype(out[name].dtype))
    for name, factor in factors.items():
        out[name] = (out[name] * factor).astype(out[name].dtype)
    return out
```

```python
from contextlib import ExitStack

import concourse.bass as bass
from concourse import mybir

F32 = mybir.dt.float32
U32 = mybir.dt.uint32
ALU = mybir.AluOpType
ACT = mybir.ActivationFunctionType
AX = mybir.AxisListType

P = 128
D = 1024
DK = D // P
SEQ, DEC, PAST = 1024, 64, 128
TILES = SEQ // P
HA, HB, DHB = 4, 8, 64
CONV = 3 * HA * P
CB = CONV // P
CW = 4
COL_BA = CONV
COL_G = COL_BA + 2 * HA
COL_Q = COL_G + HA * P
COL_K = COL_Q + HB * DHB
COL_V = COL_K + HB * DHB
COL_F = COL_V + HB * DHB
COLS = COL_F + HB
HP, KEYS, TOP = 8, 128, 16
EXPERTS = KEYS * KEYS
PICKS = HP * TOP
PLE = 256
EPS = 1e-6
NEG = -1e30
LEVELS = 7

WCOLS = 264
WRING = 2
RING = 6
PER_SLOT = 4
LAG = TOP // PER_SLOT
SLOTS = PICKS // PER_SLOT + LAG

TAIL_PIECES = [("gate", c, 256) for c in range(0, D, 256)] + [("proj", 0, D)]
IN_PIECES = (
    [("conv", c, 256) for c in range(0, CONV, 256)]
    + [("ba_g", COL_BA, 264), ("g", COL_BA + 264, 256)]
    + [("fox_q", COL_Q, 256), ("fox_q", COL_Q + 256, 256)]
    + [("fox_k", COL_K, 256), ("fox_k", COL_K + 256, 256)]
    + [("fox_v", COL_V, 256), ("fox_v_f", COL_V + 256, 264)]
)
OUT_PIECES = [("out", c, 256) for c in range(0, D, 256)]
WQ_PIECES = [("wq", c, 256) for c in range(0, 2 * HP * P, 256)]
SIGNALS = """
x_loaded prefix_loaded p_loaded past_loaded const_loaded stored
rms_mix ms_mix a_ready a_tr aT_ready
zba_out conv_in silu_go c_silu c_tr ctok_v ss_gdn rms_gdn qkb_ready qkb_tr qT_out kT_out kbT_out
y_gate e_gate gates_ready latri_ready dec_mm dec_exp dec_ready kk_mm mt_ready inv_ct x_mm x_out d_mm t_out
state_mm r_ready u_mm u_out o_mm au_out o_ready s_ready ssn_gdn rmsn_gdn oA_ready
lf_ready c_mm aux_ready k_out k_tr kT_done past_k_tr past_kT
s_mm s_max p_exp p_tr pt_act pt_dve o_fox fox_o ss_fox rms_fox oB_ready mix_tr mixT_ready h1_ready
ms_ffn rms_ffn xn_ready xn_tr xnT_ready q_ready sc_mm sc_out top_v gate_e gate_done idx_done
h2_ready ms_ple rms_ple t_ready t_tr tT_ready pT_tr pT_ready sig_out h3_ready ms_fin rms_fin y_ready y_stored
proj_done out_even out_odd w_even w_odd dve_step act_step pool_step
w_gelu w_ready diag_ready handed setup_pe setup_ev setup_pool setup_dve halo_done lf_past_ready
""".split()


def peer_order():
    order = []
    for s in range(SLOTS):
        own = []
        for j in range(PER_SLOT):
            if s < SLOTS - LAG:
                own.append(("u", PER_SLOT * s + j))
            if s >= LAG:
                own.append(("v", PER_SLOT * (s - LAG) + j))
        order.append(own)
    return order


ORDER = peer_order()
NUMBER = {e: n for n, e in enumerate(e for own in ORDER for e in own)}


def on_tensor(pick):
    return pick % 2 == 0


def build(nc, t, out):
    ctx = ExitStack()
    with ctx:
        def sb(name, shape, dt=F32):
            return ctx.enter_context(nc.sbuf_tensor(name, shape, dt))

        ident = sb("ident", [P, P])
        tri_le = sb("tri_le", [P, P])
        tri_gt = sb("tri_gt", [P, P])
        ones = sb("ones", [P, P])
        level_mask = sb("level_mask", [P, LEVELS, P])
        keysT = sb("keysT", [P, 2, KEYS])
        g_ffn = sb("g_ffn", [P, D])
        g_fin = sb("g_fin", [P, D])
        g_mix = sb("g_mix", [P, DK])
        g_ple = sb("g_ple", [P, DK])
        taps = sb("taps", [P, CW, CB])
        g_gdn = sb("g_gdn", [P, P])
        g_fox = sb("g_fox", [P, DHB])
        bias12 = sb("bias12", [P, HA + HB])
        neg_a = sb("neg_a", [P, HA])
        key_minus_q = sb("key_minus_q", [P, SEQ])
        iota16 = sb("iota16", [P, TOP])
        pos = sb("pos", [P, 1])
        eps = sb("eps", [P, 1])
        valid = sb("valid", [P, 1])
        sel = sb("sel", [P, HB])
        x = sb("x", [P, D])
        an = sb("an", [P, D])
        aT = sb("aT", [P, DK, P])
        zT = sb("zT", [P, CB, CW - 1 + P])
        cT = sb("cT", [P, CB, P])
        ctok = sb("ctok", [P, CB, P])
        tmp = sb("tmp", [P, D])
        mix = sb("mix", [P, D])
        state = sb("state", [P, HA, P])
        zg = sb("zg", [P, HA * P])
        zba = sb("zba", [P, 2 * HA])
        zf = sb("zf", [P, HB])
        kst = sb("kst", [P, HB * DHB])
        fqT = sb("fqT", [P, HB, P])
        kTc = sb("kTc", [P, HB // 2, SEQ])
        vc = sb("vc", [P, TILES, HB * DHB])
        aux = sb("aux", [P, SEQ])
        y12 = sb("y12", [P, 12])
        e12 = sb("e12", [P, 12])
        l12 = sb("l12", [P, 12])
        beta = sb("beta", [P, HA])
        bex = sb("bex", [P, HA])
        la = sb("la", [P, HA])
        logf = sb("logf", [P, HB])
        lf40 = sb("lf40", [P, P])
        c40 = sb("c40", [P, P])
        carry = sb("carry", [P, 1])
        ge = sb("ge", [P, 12])
        neg_eg = sb("neg_eg", [P, HA])
        st = sb("st", [P, 16])
        fst = sb("fst", [P, 4])
        st2 = sb("st2", [P, 8])
        fmax = sb("fmax", [P, HB])
        fneg = sb("fneg", [P, HB])
        fsum = sb("fsum", [P, HB])
        finv = sb("finv", [P, HB])
        si = sb("si", [P, 2 * HP, TOP], U32)
        idx_n = sb("idx_n", [P, PICKS], U32)
        gate_n = sb("gate_n", [P, PICKS])
        arena = sb("arena", [P, 38 * 256])

        def part(kb, size, **shape):
            v = arena[:, kb * 256:kb * 256 + size]
            return v.rearrange("p (a b) -> p a b", **shape) if shape else v

        dec = part(0, 512, a=HA)
        mt = part(2, 512, a=HA)
        latri = mt
        attnT = part(4, 512, a=HA)
        ct = [part(6, 512, a=HA), part(8, 512, a=HA)]
        tinv = part(10, 512, a=HA)
        ttinv = part(12, 512, a=HA)
        xx = part(14, 512, a=HA)
        kb = part(16, 512, a=HA)
        rr, uu = ct[0], ct[1]
        pbuf = [part(18, 1024), part(22, 1024)]
        pts = part(26, 1024, a=TILES)
        cm = part(30, 1024)
        faux = part(34, 1024, a=HB)
        qTp = part(0, 2048, a=2 * HP)
        sc = part(8, 2048, a=2 * HP)
        cand = part(16, 2048, a=HP)
        eq = part(24, 2048, a=HP)
        sc2 = part(32, 256)
        sif = part(33, 256, a=2 * HP)
        cd = part(34, 128, a=HP).bitcast(U32)
        cf = arena[:, 34 * 256 + 128:35 * 256].rearrange("p (a b) -> p a b", a=HP)
        ci = part(35, 128, a=HP).bitcast(U32)
        cv = arena[:, 35 * 256 + 128:36 * 256].rearrange("p (a b) -> p a b", a=HP)
        ef = part(36, 256).rearrange("p (c a b) -> p c a b", c=2, a=HP)
        sv = part(37, 256, a=2 * HP)
        tn = part(18, 1024)
        tT = part(22, 1024, a=DK)
        sg = part(26, 1024)
        prow = part(30, PLE)
        pT = part(31, 256, a=2)
        wring = sb("wring", [P, WRING, DK * WCOLS])
        ring = sb("ring", [P, RING, D])
        diag = sb("diag", [P, 4, P])
        xn_c = sb("xn_c", [P, D])
        h_c = sb("h_c", [P, D])
        idx_c = sb("idx_c", [P, PICKS], U32)
        gate_c = sb("gate_c", [P, PICKS])
        dots = sb("dots", [P, PICKS])
        wgt = sb("wgt", [P, PICKS])
        yacc = sb("yacc", [P, D])
        h2 = sb("h2", [P, D])

        bank = [ctx.enter_context(nc.psum_tensor(f"bank{i}", [P, 512], F32)) for i in range(8)]
        YB, AB, SB, TB = bank[0:2], bank[2:4], bank[4:6], bank[6:8]

        names = SIGNALS + [f"landed{r}" for r in range(RING)] + [f"consumed{r}" for r in range(RING)]
        sems = [ctx.enter_context(nc.semaphore(n)) for n in names]
        S = dict(zip(names, sems))
        landed = [S[f"landed{r}"] for r in range(RING)]
        consumed = [S[f"consumed{r}"] for r in range(RING)]
        numbers = sorted(s.num for s in sems)
        assert numbers == list(range(numbers[0], numbers[-1] + 1))
        proj_out = [S["out_even"], S["out_odd"]]
        w_loaded = [S["w_even"], S["w_odd"]]

        def bcast(ap, n):
            return ap.unsqueeze(2).to_broadcast([ap.shape[0], ap.shape[1], n])

        def over(ap, n):
            return ap.unsqueeze(1).to_broadcast([ap.shape[0], n, ap.shape[1]])

        class Chain:
            def __init__(self, eng, sem):
                self.eng, self.sem, self.n = eng, sem, 0

            def __call__(self, ins):
                self.n += 1
                ins.then_inc(self.sem, 1)
                self.eng.wait_ge(self.sem, self.n)

        with nc.Block() as block:
            @block.sync
            def _(sp):
                rows = lambda a, w: a.rearrange("(o d) -> o d", o=1).to_broadcast([P, w])
                loads = [
                    (g_ffn[:], rows(t["norm_ffn"][0], D)), (g_fin[:], rows(t["norm_final"], D)),
                    (g_gdn[:], rows(t["gdn_onorm"][0], P)), (g_fox[:], rows(t["fox_onorm"][0], DHB)),
                    (bias12[:, 0:HA], rows(t["dt_bias"][0], HA)), (bias12[:, HA:], rows(t["b_f"][0], HB)),
                    (neg_a[:], rows(t["a_log"][0], HA)),
                    (g_mix[:], t["norm_mix"][0].rearrange("(k p) -> p k", p=P)),
                    (g_ple[:], t["norm_ple"][0].rearrange("(k p) -> p k", p=P)),
                    (tmp[:, 0:P], t["peer_keys"][0, 0]), (tmp[:, P:2 * P], t["peer_keys"][0, 1]),
                ] + [(taps[:, j, :], t["conv_w"][0, j].rearrange("(b p) -> p b", p=P)) for j in range(CW)]
                for dst, src in loads:
                    sp.dma_start(dst, src, allow_slow_non_contiguous=True).then_inc(S["const_loaded"], 16)
                sp.wait_ge(S["const_loaded"], 16 * len(loads))

            @block.gpsimd
            def _(pool):
                step = Chain(pool, S["pool_step"])
                step(pool.memset(ones[:], 1.0))
                step(pool.memset(ident[:], 0.0))
                step(pool.affine_select(out=ident[:], in_=ident[:], compare_op=ALU.not_equal, fill=1.0,
                                        base=0, pattern=[[-1, P]], channel_multiplier=1))
                step(pool.affine_select(out=tri_le[:], in_=ones[:], compare_op=ALU.is_ge, fill=0.0,
                                        base=0, pattern=[[1, P]], channel_multiplier=-1))
                step(pool.affine_select(out=tri_gt[:], in_=ones[:], compare_op=ALU.is_ge, fill=0.0,
                                        base=-1, pattern=[[-1, P]], channel_multiplier=1))
                step(pool.memset(level_mask[:], 0.0))
                for l in range(LEVELS):
                    b = 1 << l
                    n = P // (2 * b)
                    v = level_mask[:, l, :].rearrange("p (n c) -> p n c", n=n)[:, :, b:2 * b]
                    o = ones[:, 0:n * b].rearrange("p (n c) -> p n c", n=n)
                    step(pool.affine_select(out=v, in_=o, compare_op=ALU.is_ge, fill=0.0,
                                            base=0, pattern=[[-2 * b, n], [0, b]], channel_multiplier=1))
                    step(pool.affine_select(out=v, in_=v, compare_op=ALU.is_ge, fill=0.0,
                                            base=b - 1, pattern=[[2 * b, n], [0, b]], channel_multiplier=-1))
                step(pool.memset(sel[:], 0.0))
                for r in (0, 32):
                    step(pool.affine_select(out=sel[:], in_=sel[:], compare_op=ALU.not_equal, fill=1.0,
                                            base=-r, pattern=[[-1, HB]], channel_multiplier=1))
                step(pool.iota(key_minus_q[:], pattern=[[1, SEQ]], base=0, channel_multiplier=-1,
                               allow_small_or_imprecise_dtypes=True))
                step(pool.iota(iota16[:], pattern=[[1, TOP]], base=0, channel_multiplier=0,
                               allow_small_or_imprecise_dtypes=True))
                step(pool.memset(kTc[:], 0.0))
                step(pool.memset(vc[:], 0.0))
                pool.engine_nop().then_inc(S["setup_pool"], 1)

            @block.vector
            def _(v):
                step = Chain(v, S["dve_step"])
                step(v.memset(aux[:], 0.0))
                step(v.memset(aux[32:40, :], 1.0))
                step(v.memset(lf40[:], 0.0))
                step(v.memset(carry[:], 0.0))
                step(v.memset(zT[:, :, 0:CW - 1], 0.0))
                step(v.memset(state[:], 0.0))
                step(v.memset(pos[:], 0.0))
                step(v.memset(eps[:], EPS))
                step(v.memset(fqT[:], 0.0))
                step(v.memset(valid[:], 1.0))
                step(v.memset(valid[DEC:P, :], 0.0))
                v.wait_ge(S["setup_pe"], 1)
                step(v.tensor_copy(keysT[:], SB[0][:, 0:2 * KEYS].rearrange("p (c n) -> p c n", c=2)))
                v.wait_ge(S["setup_ev"], 1)
                step(v.tensor_scalar(neg_a[:], neg_a[:], -1.0, None, ALU.mult))

            @block.scalar
            def _(act):
                act.wait_ge(S["const_loaded"], 16 * 15)
                act.activation(neg_a[:], neg_a[:], ACT.Exp).then_inc(S["setup_ev"], 1)

            @block.tensor
            def _(pe):
                pe.wait_ge(S["const_loaded"], 16 * 15)
                pe.wait_ge(S["pool_step"], 3)
                for c in range(2):
                    last = pe.transpose(SB[0][:, c * KEYS:(c + 1) * KEYS], tmp[:, c * P:(c + 1) * P], ident[:])
                last.then_inc(S["setup_pe"], 1)
        nc.all_engine_barrier(sems_to_clear=range(numbers[0], numbers[-1] + 1))

        def body(front=None, peer=None, tail=None):
            pieces = (TAIL_PIECES if tail else []) + (IN_PIECES + OUT_PIECES + WQ_PIECES if front else [])
            first = {}
            for n, (what, c, w) in enumerate(pieces):
                first.setdefault(what, n)
            if front:
                f_i, f_rows, f_blk, f_sample = front
                f_src = t["x_sample"][0] if f_sample else t["x_prompt"][0][bass.ds(f_i * P, P), :]
                f_key = bass.ds(f_blk * P, P)
            if tail:
                t_i, t_rows, t_sample = tail
                t_p = t["p_sample"][0, 0] if t_sample else t["p_prompt"][0, 0][bass.ds(t_i * P, P), :]
                t_y = out["y_sample"][0] if t_sample else out["y_prompt"][0][bass.ds(t_i * P, P), :]
            mats = {"gate": t["w_ple_gate"], "proj": t["w_ple_proj"], "out": t["w_out"], "wq": t["peer_wq"]}
            n_store = [0]

            def blocks(ps2, n):
                return [b[:].rearrange("p (a c) -> p a c", a=4) for b in ps2][:n]

            with nc.Block() as block:
                @block.sync
                def _(sp):
                    if tail:
                        sp.dma_start(prow[0:t_rows, :], t_p).then_inc(S["p_loaded"], 16)
                    if front:
                        sp.dma_start(x[0:f_rows, :], f_src).then_inc(S["x_loaded"], 16)
                        if f_sample:
                            for j in range(CW - 1):
                                sp.dma_start(out["conv_prompt"][0, 0, j].rearrange("(b p) -> p b", p=P), zT[:, :, j],
                                             allow_slow_non_contiguous=True).then_inc(S["stored"], 16)
                            sp.dma_start(out["gdn_prompt"][0, 0].rearrange("h k v -> k h v"),
                                         state[:]).then_inc(S["stored"], 16)
                            sp.wait_ge(S["stored"], 16 * CW)
                            n_store[0] = CW
                            for j in range(CW - 1):
                                sp.dma_start(zT[:, :, j], t["cache_conv"][0, 0, j].rearrange("(b p) -> p b", p=P),
                                             allow_slow_non_contiguous=True).then_inc(S["prefix_loaded"], 16)
                            sp.dma_start(state[:], t["state_gdn"][0, 0].rearrange("h k v -> k h v"))\
                              .then_inc(S["prefix_loaded"], 16)
                            sp.dma_start(kst[:], t["cache_fox_k"][0, 0].rearrange("t h d -> t (h d)"))\
                              .then_inc(S["past_loaded"], 16)
                            sp.dma_start(vc[:, 0, :], t["cache_fox_v"][0, 0].rearrange("t h d -> t (h d)"))\
                              .then_inc(S["past_loaded"], 16)
                            sp.dma_start(logf[:], t["cache_fox_logf"][0, 0]).then_inc(S["past_loaded"], 16)
                    for n, (what, c, w) in enumerate(pieces):
                        if n >= WRING:
                            sp.wait_ge(S["proj_done"], n - WRING + 1)
                        src = mats.get(what, t["w_in"])[0].rearrange("(k p) n -> p k n", p=P)
                        k = src.shape[1]
                        sp.dma_start(wring[:, n % WRING, 0:k * w].rearrange("p (k n) -> p k n", k=k),
                                     src[:, :, c:c + w]).then_inc(w_loaded[n % WRING], 16)
                    if front:
                        o = "_sample" if f_sample else "_prompt"
                        rows = slice(0, DEC) if f_sample else bass.ds(f_i * P, P)
                        sp.wait_ge(S["kT_done"], 1)
                        sp.dma_start(out["k" + o][0, 0].rearrange("t h d -> t (h d)")[rows, :],
                                     kst[0:f_rows, :]).then_inc(S["stored"], 16)
                        sp.wait_ge(proj_out[(first["fox_v_f"]) % 2], first["fox_v_f"] // 2 + 1)
                        sp.wait_ge(proj_out[(first["fox_v"]) % 2], first["fox_v"] // 2 + 1)
                        vrow = vc[0:f_rows, f_blk, :] if isinstance(f_blk, int) else \
                            vc[:, bass.ds(f_blk, 1), :].rearrange("p a b -> p (a b)")
                        sp.dma_start(out["v" + o][0, 0].rearrange("t h d -> t (h d)")[rows, :],
                                     vrow).then_inc(S["stored"], 16)
                        sp.wait_ge(S["lf_ready"], 1)
                        sp.dma_start(out["logf" + o][0, 0][rows, :], logf[0:f_rows, :]).then_inc(S["stored"], 16)
                        n_store[0] += 3
                        if f_sample:
                            sp.wait_ge(S["s_ready"], 1)
                            sp.dma_start(out["gdn_sample"][0, 0].rearrange("h k v -> k h v"),
                                         state[:]).then_inc(S["stored"], 16)
                            for j in range(CW - 1):
                                sp.dma_start(out["conv_sample"][0, 0, j].rearrange("(b p) -> p b", p=P),
                                             zT[:, :, DEC + j], allow_slow_non_contiguous=True)\
                                  .then_inc(S["stored"], 16)
                            n_store[0] += CW
                    if tail:
                        sp.wait_ge(S["y_stored"], 16)
                    if n_store[0]:
                        sp.wait_ge(S["stored"], 16 * n_store[0])

                @block.gpsimd
                def _(pool):
                    def inv_masks(l):
                        if l == 0:
                            pool.wait_ge(S["mt_ready"], 1)
                        if l >= 2:
                            pool.wait_ge(S["x_mm"], l - 1)
                        pool.tensor_tensor(ct[l % 2], mt, over(level_mask[:, l, :], HA), ALU.mult)\
                            .then_inc(S["inv_ct"], 1)

                    plan = {"inv%d" % l: (lambda l=l: inv_masks(l)) for l in range(LEVELS)}
                    for s in range(SLOTS):
                        if front:
                            for name in PLAN[s]:
                                if name in plan:
                                    plan[name]()
                        if peer:
                            for kind, k in ORDER[s]:
                                n = NUMBER[kind, k]
                                r = n % RING
                                if n >= RING:
                                    pool.wait_ge(consumed[r], n // RING)
                                pool.indirect_dma_start(
                                    out=ring[0:peer, r, :], out_offset=None, in_=t["peer_" + kind],
                                    in_offset=bass.IndirectOffsetOnAxis(ap=idx_c[0:peer, k:k + 1], axis=0),
                                ).then_inc(landed[r], 16)
                    if peer:
                        for n in range(2 * PICKS - RING, 2 * PICKS):
                            pool.wait_ge(consumed[n % RING], n // RING + 1)
                        pool.dma_reset(range(landed[0].num, landed[-1].num + 1))

                def wait_used(eng, kind, k):
                    n = NUMBER[kind, k]
                    eng.wait_ge(consumed[n % RING], n // RING + 1)

                @block.scalar
                def _(act):
                    step = Chain(act, S["act_step"])

                    def rms(src, rows, c, junk, done):
                        step(act.activation(junk[0:rows, :], src, ACT.Square, accum_out=st[0:rows, c + 1:c + 2]))
                        act.activation(st[0:rows, c:c + 1], st[0:rows, c + 1:c + 2], ACT.Sqrt, bias=eps[0:rows, :],
                                       scale=1.0 / D).then_inc(done, 1)

                    def evac(n, pairs, func=ACT.Copy, scale=1.0):
                        act.wait_ge(S["proj_done"], n + 1)
                        for dst, src in pairs:
                            last = act.activation(dst, src, func, scale=scale)
                        last.then_inc(proj_out[n % 2], 1)

                    def tail_norm():
                        rms(h2[0:t_rows, :], t_rows, 8, tn, S["rms_ple"])

                    def tail_gate():
                        for j in range(4):
                            n = first["gate"] + j
                            act.wait_ge(S["proj_done"], n + 1)
                            act.activation(sg[0:t_rows, 256 * j:256 * j + 256], AB[n % 2][0:t_rows, 0:256],
                                           ACT.Sigmoid).then_inc(proj_out[n % 2], 1)

                    def tail_fin():
                        act.wait_ge(S["h3_ready"], 2)
                        rms(h2[0:t_rows, :], t_rows, 12, tn, S["rms_fin"])

                    def tail_store():
                        act.wait_ge(S["y_ready"], 1)
                        act.dma_start(t_y, tn[0:t_rows, :]).then_inc(S["y_stored"], 16)

                    def norm_mix():
                        act.wait_ge(S["x_loaded"], 16)
                        if f_sample:
                            act.wait_ge(S["halo_done"], 1)
                        rms(x[:], P, 0, tmp, S["rms_mix"])

                    def in_proj(j):
                        n = first["conv"] + j
                        what, c, w = pieces[n]
                        b = AB[n % 2]
                        if what == "conv":
                            if j == 0 and f_sample:
                                act.wait_ge(S["prefix_loaded"], 16 * CW)
                            evac(n, [(zT[:, c // P:c // P + 2, CW - 1:], b[:, 0:256].rearrange("p (a c) -> p a c", a=2))])
                        elif what == "ba_g":
                            evac(n, [(zba[:], b[:, 0:8]), (zg[:, 0:256], b[:, 8:264])])
                        elif what == "g":
                            evac(n, [(zg[:, 256:512], b[:, 0:256])])
                        elif what == "fox_q":
                            m = (c - COL_Q) // P
                            heads = fqT[:].rearrange("p (m o) c -> p m o c", o=2)
                            b3 = b[:, 0:256].rearrange("p (a c) -> p a c", a=2)
                            evac(n, [(heads[DHB * o:DHB * o + DHB, m:m + 2, o, :], b3[DHB * o:DHB * o + DHB])
                                     for o in range(2)], scale=DHB ** -0.5)
                        elif what == "fox_k":
                            if f_sample and c == COL_K:
                                act.wait_ge(S["past_k_tr"], 1)
                            evac(n, [(kst[:, c - COL_K:c - COL_K + 256], b[:, 0:256])])
                        else:
                            m = c - COL_V
                            dst = vc[:, bass.ds(f_blk, 1), m:m + 256].rearrange("p a b -> p (a b)")
                            if what == "fox_v_f":
                                evac(n, [(dst, b[:, 0:256]), (zf[:], b[:, 256:264])])
                            else:
                                evac(n, [(dst, b[:, 0:256])])

                    def silu():
                        act.wait_ge(S["conv_in"], 1)
                        act.activation(cT[:], cT[:], ACT.Silu).then_inc(S["c_silu"], 1)
                        act.activation(zg[:], zg[:], ACT.Silu).then_inc(S["silu_go"], 1)

                    def gates():
                        act.wait_ge(S["y_gate"], 1)
                        step(act.activation(e12[:], y12[:], ACT.Abs))
                        step(act.activation(e12[:], e12[:], ACT.Exp, scale=-1.0))
                        act.activation(l12[:], e12[:], ACT.Ln, bias=1.0)
                        act.activation(bex[:], zba[:, 0:HA], ACT.Exp, scale=-1.0).then_inc(S["e_gate"], 1)

                    def gdn_v():
                        act.wait_ge(S["c_tr"], 1)
                        act.activation(ctok[:, 8:12, :], TB[0][:].rearrange("p (a c) -> p a c", a=4), ACT.Copy)\
                            .then_inc(S["ctok_v"], 1)
                        act.wait_ge(S["ss_gdn"], 1)
                        act.activation(st2[:], st2[:], ACT.Sqrt, bias=eps[:]).then_inc(S["rms_gdn"], 1)

                    def gdn_qk():
                        act.wait_ge(S["qkb_tr"], 1)
                        act.activation(cT[:, 0:4, :], SB[0][:].rearrange("p (a c) -> p a c", a=4), ACT.Copy)
                        act.activation(cT[:, 4:8, :], SB[1][:].rearrange("p (a c) -> p a c", a=4), ACT.Copy)\
                            .then_inc(S["qT_out"], 1)

                    def decay():
                        act.wait_ge(S["dec_mm"], 1)
                        act.activation(dec, TB[0][:].rearrange("p (a c) -> p a c", a=4), ACT.Exp)
                        act.activation(ge[:], TB[1][:, 0:12], ACT.Exp).then_inc(S["dec_exp"], 1)

                    def inverse(l):
                        act.wait_ge(S["x_mm"], l + 1)
                        if l >= 1:
                            act.wait_ge(S["d_mm"], l)
                        act.activation(xx, TB[0][:].rearrange("p (a c) -> p a c", a=4), ACT.Copy)\
                            .then_inc(S["x_out"], 1)

                    def state_u():
                        act.wait_ge(S["u_mm"], 1)
                        act.activation(uu, SB[0][:].rearrange("p (a c) -> p a c", a=4), ACT.Copy)\
                            .then_inc(S["u_out"], 1)
                        act.wait_ge(S["o_mm"], 1)
                        act.activation(xx, SB[1][:].rearrange("p (a c) -> p a c", a=4), ACT.Copy)\
                            .then_inc(S["au_out"], 1)

                    def gdn_norm():
                        act.wait_ge(S["ssn_gdn"], 1)
                        act.activation(st2[:, 0:4], st2[:, 0:4], ACT.Sqrt, bias=eps[:], scale=1.0 / P)\
                            .then_inc(S["rmsn_gdn"], 1)

                    def fox_keys():
                        if f_sample:
                            act.wait_ge(S["past_k_tr"], 1)
                            act.activation(kTc[:, :, 0:P], TB[0][:].rearrange("p (a c) -> p a c", a=4), ACT.Copy)\
                                .then_inc(S["past_kT"], 1)

                    def fox_kT():
                        act.wait_ge(S["k_tr"], 1)
                        act.activation(kTc[:, :, f_key], TB[0][:].rearrange("p (a c) -> p a c", a=4), ACT.Copy)\
                            .then_inc(S["kT_done"], 1)

                    def fox(h):
                        act.wait_ge(S["s_max"], h + 1)
                        step(act.activation(fneg[:, h:h + 1], fmax[:, h:h + 1], ACT.Copy, scale=-1.0))
                        act.activation(pbuf[h % 2], pbuf[h % 2], ACT.Exp, bias=fneg[:, h:h + 1],
                                       accum_out=fsum[:, h:h + 1]).then_inc(S["p_exp"], 1)
                        act.wait_ge(S["p_tr"], h + 1)
                        if h >= 1:
                            act.wait_ge(S["o_fox"], h)
                        act.activation(pts[:, 0:4, :], TB[0][:].rearrange("p (a c) -> p a c", a=4), ACT.Copy)\
                            .then_inc(S["pt_act"], 1)

                    def fox_norm():
                        act.wait_ge(S["ss_fox"], 1)
                        act.activation(st2[:], st2[:], ACT.Sqrt, bias=eps[:], scale=1.0 / DHB)\
                            .then_inc(S["rms_fox"], 1)

                    def norm_ffn():
                        act.wait_ge(S["h1_ready"], 4)
                        rms(x[:], P, 4, tmp, S["rms_ffn"])

                    def wq(j):
                        n = first["wq"] + j
                        evac(n, [(qTp[:, 2 * j:2 * j + 2, :], AB[n % 2][:, 0:256].rearrange("p (a c) -> p a c", a=2))])

                    def scores():
                        for g, b in enumerate(SB + TB):
                            act.wait_ge(S["sc_mm"], g + 1)
                            act.activation(sc[:, 4 * g:4 * g + 4, :], b[:].rearrange("p (a c) -> p a c", a=4),
                                           ACT.Copy).then_inc(S["sc_out"], 1)

                    def pick_gate():
                        act.wait_ge(S["top_v"], 1)
                        act.activation(gate_n[:], gate_n[:], ACT.Exp).then_inc(S["gate_e"], 1)

                    def hand_over():
                        if peer:
                            wait_used(act, "u", PICKS - 1)
                        act.wait_ge(S["xn_ready"], 1)
                        act.activation(xn_c[:], an[:], ACT.Copy)
                        if peer:
                            act.wait_ge(S["h2_ready"], 1)
                        act.activation(h_c[:], x[:], ACT.Copy).then_inc(S["handed"], 1)

                    plan = dict(tail_norm=tail_norm, tail_gate=tail_gate, tail_fin=tail_fin, tail_store=tail_store,
                                norm_mix=norm_mix, silu=silu, gates=gates, gdn_v=gdn_v, gdn_qk=gdn_qk, decay=decay,
                                state_u=state_u, gdn_norm=gdn_norm, fox_keys=fox_keys, fox_kT=fox_kT,
                                fox_norm=fox_norm, norm_ffn=norm_ffn, scores=scores, pick_gate=pick_gate)
                    plan.update({f"in{j}": (lambda j=j: in_proj(j)) for j in range(len(IN_PIECES))})
                    plan.update({f"inv{l}": (lambda l=l: inverse(l)) for l in range(LEVELS)})
                    plan.update({f"fox{h}": (lambda h=h: fox(h)) for h in range(HB)})
                    plan.update({f"wq{j}": (lambda j=j: wq(j)) for j in range(len(WQ_PIECES))})
                    for s in range(SLOTS):
                        for name in PLAN[s]:
                            if name in plan and (tail if name.startswith("tail") else front):
                                plan[name]()
                        if peer and s >= LAG:
                            if s % LAG == 0:
                                h = s // LAG - 1
                                wait_used(act, "u", TOP * h + TOP - 1)
                                act.activation(wgt[0:peer, TOP * h:TOP * h + TOP],
                                               dots[0:peer, TOP * h:TOP * h + TOP], ACT.Gelu)\
                                    .then_inc(S["w_gelu"], 1)
                                act.wait_ge(S["w_ready"], h + 1)
                            for kind, k in ORDER[s]:
                                if kind == "v" and on_tensor(k):
                                    m = k // 2
                                    if m >= 4:
                                        wait_used(act, "v", k - 8)
                                    act.activation(diag[0:peer, m % 4, 0:peer], ident[0:peer, 0:peer], ACT.Copy,
                                                   scale=wgt[0:peer, k:k + 1]).then_inc(S["diag_ready"], 1)
                    if front:
                        hand_over()

                @block.tensor
                def _(pe):
                    def transpose8(src, rows, banks, done):
                        for k in range(DK):
                            last = pe.transpose(banks[k // 4][:, (k % 4) * P:(k % 4) * P + rows],
                                                src[0:rows, k * P:(k + 1) * P], ident[0:rows, 0:rows])
                        last.then_inc(done, 1)

                    def project(n, actT, rows, turned):
                        what, c, w = pieces[n]
                        k8 = 2 if what == "proj" else DK
                        wt = wring[:, n % WRING, 0:k8 * w].rearrange("p (k n) -> p k n", k=k8)
                        pe.wait_ge(w_loaded[n % WRING], 16 * (n // WRING + 1))
                        if n >= 2:
                            pe.wait_ge(proj_out[n % 2], n // 2)
                        b = AB[n % 2]
                        if turned:
                            for m in range(w // P):
                                for k in range(DK):
                                    last = pe.matmul(b[:, m * P:m * P + rows], wt[:, k, m * P:(m + 1) * P],
                                                     actT[:, k, 0:rows], start=(k == 0), stop=(k == DK - 1))
                        else:
                            for k in range(k8):
                                last = pe.matmul(b[0:rows, 0:w], actT[:, k, 0:rows], wt[:, k, :],
                                                 start=(k == 0), stop=(k == k8 - 1))
                        last.then_inc(S["proj_done"], 1)

                    def tail_norm():
                        pe.wait_ge(S["p_loaded"], 16)
                        for k in range(2):
                            last = pe.transpose(TB[0][:, k * P:k * P + t_rows], prow[0:t_rows, k * P:(k + 1) * P],
                                                ident[0:t_rows, 0:t_rows])
                        last.then_inc(S["pT_tr"], 1)
                        pe.wait_ge(S["t_ready"], 1)
                        transpose8(tn, t_rows, SB, S["t_tr"])

                    def tail_gate():
                        pe.wait_ge(S["tT_ready"], 2)
                        for j in range(4):
                            project(first["gate"] + j, tT, t_rows, False)
                        n = first["proj"]
                        wt = wring[:, n % WRING, 0:2 * D].rearrange("p (k n) -> p k n", k=2)
                        pe.wait_ge(w_loaded[n % WRING], 16 * (n // WRING + 1))
                        pe.wait_ge(S["pT_ready"], 1)
                        for g in range(2):
                            for k in range(2):
                                last = pe.matmul(SB[g][0:t_rows, :], pT[:, k, 0:t_rows], wt[:, k, 512 * g:512 * g + 512],
                                                 start=(k == 0), stop=(k == 1))
                        last.then_inc(S["proj_done"], 1)

                    def norm_mix():
                        pe.wait_ge(S["a_ready"], 1)
                        transpose8(an, P, TB, S["a_tr"])

                    def in_proj(j):
                        if j == 0:
                            pe.wait_ge(S["aT_ready"], 2)
                        n = first["conv"] + j
                        project(n, aT, P, pieces[n][0] in ("conv", "fox_q"))

                    def conv():
                        pe.wait_ge(S["c_silu"], 1)
                        for m in range(CB):
                            last = pe.transpose((SB + TB)[m // 4][:, (m % 4) * P:(m % 4 + 1) * P], cT[:, m, :], ident[:])
                        last.then_inc(S["c_tr"], 1)

                    def gdn_qk():
                        pe.wait_ge(S["qkb_ready"], 1)
                        for m in range(4):
                            pe.transpose(SB[0][:, m * P:(m + 1) * P], ctok[:, m, :], ident[:])
                        for m in range(4):
                            pe.transpose(SB[1][:, m * P:(m + 1) * P], ctok[:, 4 + m, :], ident[:])
                        for m in range(4):
                            last = pe.transpose(TB[1][:, m * P:(m + 1) * P], kb[:, m, :], ident[:])
                        last.then_inc(S["qkb_tr"], 1)

                    def decay():
                        pe.wait_ge(S["latri_ready"], 1)
                        pe.wait_ge(S["kbT_out"], 1)
                        pe.wait_ge(S["ctok_v"], 1)
                        for h in range(HA):
                            pe.matmul(TB[0][:, h * P:(h + 1) * P], latri[:, h, :], tri_le[:], start=True, stop=True)
                        for m, lhs in enumerate((tri_le, tri_gt, ones)):
                            last = pe.matmul(TB[1][:, 4 * m:4 * m + 4], lhs[:], la[:], start=True, stop=True)
                        last.then_inc(S["dec_mm"], 1)

                    def gram():
                        pe.wait_ge(S["qT_out"], 1)
                        for h in range(HA):
                            pe.matmul(SB[0][:, h * P:(h + 1) * P], cT[:, 4 + h, :], cT[:, 8 + h, :], start=True, stop=True)
                        for h in range(HA):
                            last = pe.matmul(SB[1][:, h * P:(h + 1) * P], cT[:, 4 + h, :], cT[:, h, :],
                                             start=True, stop=True)
                        last.then_inc(S["kk_mm"], 1)

                    def inverse(l):
                        pe.wait_ge(S["inv_ct"], l + 1)
                        if l == 0:
                            pe.wait_ge(S["dec_exp"], 1)
                            pe.wait_ge(S["mt_ready"], 1)
                        pe.wait_ge(S["t_out"], l + 1)
                        for h in range(HA):
                            last = pe.matmul(TB[0][:, h * P:(h + 1) * P], ct[l % 2][:, h, :], tinv[:, h, :],
                                             start=True, stop=True)
                        last.then_inc(S["x_mm"], 1)
                        pe.wait_ge(S["x_out"], l + 1)
                        for h in range(HA):
                            pe.matmul(SB[0][:, h * P:(h + 1) * P], ttinv[:, h, :], xx[:, h, :], start=True, stop=True)
                        for h in range(HA):
                            last = pe.matmul(SB[1][:, h * P:(h + 1) * P], xx[:, h, :], ttinv[:, h, :],
                                             start=True, stop=True)
                        last.then_inc(S["d_mm"], 1)

                    def state_u():
                        if f_sample:
                            pe.wait_ge(S["prefix_loaded"], 16 * CW)
                        pe.wait_ge(S["t_out"], LEVELS + 1)
                        for h in range(HA):
                            pe.matmul(TB[0][:, h * P:(h + 1) * P], cT[:, 4 + h, :], state[:, h, :], start=True, stop=True)
                        for h in range(HA):
                            last = pe.matmul(TB[1][:, h * P:(h + 1) * P], cT[:, h, :], state[:, h, :],
                                             start=True, stop=True)
                        last.then_inc(S["state_mm"], 1)
                        pe.wait_ge(S["r_ready"], 1)
                        for h in range(HA):
                            last = pe.matmul(SB[0][:, h * P:(h + 1) * P], ttinv[:, h, :], rr[:, h, :],
                                             start=True, stop=True)
                        last.then_inc(S["u_mm"], 1)
                        pe.wait_ge(S["u_out"], 1)
                        for h in range(HA):
                            pe.matmul(SB[1][:, h * P:(h + 1) * P], attnT[:, h, :], uu[:, h, :], start=True, stop=True)
                        for h in range(HA):
                            last = pe.matmul(TB[0][:, h * P:(h + 1) * P], kb[:, h, :], uu[:, h, :],
                                             start=True, stop=True)
                        last.then_inc(S["o_mm"], 1)

                    def fox_keys():
                        if f_sample:
                            pe.wait_ge(S["lf_past_ready"], 1)
                            pe.matmul(TB[1][:, 0:P], lf40[:], tri_le[:], start=True, stop=True).then_inc(S["c_mm"], 1)
                            pe.wait_ge(S["past_loaded"], 48)
                            for m in range(4):
                                last = pe.transpose(TB[0][:, m * P:(m + 1) * P], kst[:, m * P:(m + 1) * P], ident[:])
                            last.then_inc(S["past_k_tr"], 1)

                    def fox_kT():
                        for w in ("fox_k",):
                            for n in (first[w], first[w] + 1):
                                pe.wait_ge(proj_out[n % 2], n // 2 + 1)
                        if f_sample:
                            pe.wait_ge(S["past_kT"], 1)
                            pe.wait_ge(S["aux_ready"], 1)
                        pe.wait_ge(S["s_ready"], 1)
                        for m in range(4):
                            last = pe.transpose(TB[0][:, m * P:(m + 1) * P], kst[:, m * P:(m + 1) * P], ident[:])
                        last.then_inc(S["k_tr"], 1)
                        pe.wait_ge(S["lf_ready"], 1)
                        pe.matmul(TB[1][:, 0:P], lf40[:], tri_le[:], start=True, stop=True).then_inc(S["c_mm"], 1)

                    def fox_s(h):
                        if h == 0:
                            pe.wait_ge(S["kT_done"], 1)
                            pe.wait_ge(S["aux_ready"], 2 if f_sample else 1)
                            pe.wait_ge(S["au_out"], 1)
                        else:
                            pe.wait_ge(S["s_max"], h)
                        for g in range(2):
                            pe.matmul(SB[g][:], fqT[:, h, :], kTc[:, h // 2, 512 * g:512 * g + 512],
                                      start=True, stop=False)
                            last = pe.matmul(SB[g][:], faux[:, h, :], aux[:, 512 * g:512 * g + 512],
                                             start=False, stop=True)
                        last.then_inc(S["s_mm"], 1)

                    def fox(h):
                        if h == 0:
                            fox_s(0)
                        if h + 1 < HB:
                            fox_s(h + 1)
                        pe.wait_ge(S["p_exp"], h + 1)
                        if h >= 1:
                            pe.wait_ge(S["pt_act"], h)
                            pe.wait_ge(S["pt_dve"], h)
                        for m in range(TILES):
                            last = pe.transpose(TB[m // 4][:, (m % 4) * P:(m % 4 + 1) * P],
                                                pbuf[h % 2][:, m * P:(m + 1) * P], ident[:])
                        last.then_inc(S["p_tr"], 1)
                        pe.wait_ge(S["pt_act"], h + 1)
                        pe.wait_ge(S["pt_dve"], h + 1)
                        if h == 0:
                            for n in (first["out"] - 1, first["out"] - 2):
                                pe.wait_ge(proj_out[n % 2], n // 2 + 1)
                        for m in range(TILES):
                            last = pe.matmul(AB[0][:, h * DHB:(h + 1) * DHB], pts[:, m, :],
                                             vc[:, m, h * DHB:(h + 1) * DHB], start=(m == 0), stop=(m == TILES - 1))
                        last.then_inc(S["o_fox"], 1)

                    def mix_turn():
                        pe.wait_ge(S["oA_ready"], 1)
                        pe.wait_ge(S["oB_ready"], 1)
                        transpose8(mix, P, TB, S["mix_tr"])

                    def out_proj(j):
                        if j == 0:
                            pe.wait_ge(S["mixT_ready"], 2)
                        project(first["out"] + j, aT, P, False)

                    def norm_ffn():
                        pe.wait_ge(S["xn_ready"], 1)
                        transpose8(an, P, TB, S["xn_tr"])

                    def wq(j):
                        if j == 0:
                            pe.wait_ge(S["xnT_ready"], 2)
                        project(first["wq"] + j, aT, P, True)

                    def scores():
                        for n in (len(pieces) - 2, len(pieces) - 1):
                            pe.wait_ge(proj_out[n % 2], n // 2 + 1)
                        for g, b in enumerate(SB + TB):
                            for m in range(4):
                                last = pe.matmul(b[:, m * P:(m + 1) * P], qTp[:, 4 * g + m, :], keysT[:, m % 2, :],
                                                 start=True, stop=True)
                            last.then_inc(S["sc_mm"], 1)

                    plan = dict(tail_norm=tail_norm, tail_gate=tail_gate, norm_mix=norm_mix, conv=conv, gdn_qk=gdn_qk,
                                decay=decay, gram=gram, state_u=state_u, fox_keys=fox_keys, fox_kT=fox_kT,
                                mix_turn=mix_turn, norm_ffn=norm_ffn, scores=scores)
                    plan.update({f"in{j}": (lambda j=j: in_proj(j)) for j in range(len(IN_PIECES))})
                    plan.update({f"inv{l}": (lambda l=l: inverse(l)) for l in range(LEVELS)})
                    plan.update({f"fox{h}": (lambda h=h: fox(h)) for h in range(HB)})
                    plan.update({f"out{j}": (lambda j=j: out_proj(j)) for j in range(len(OUT_PIECES))})
                    plan.update({f"wq{j}": (lambda j=j: wq(j)) for j in range(len(WQ_PIECES))})
                    for s in range(SLOTS):
                        for name in PLAN[s]:
                            if name in plan and (tail if name.startswith("tail") else front):
                                plan[name]()
                        if peer:
                            for kind, k in ORDER[s]:
                                if kind == "v" and on_tensor(k):
                                    n = NUMBER[kind, k]
                                    r = n % RING
                                    m = k // 2
                                    pe.wait_ge(landed[r], 16 * (n // RING + 1))
                                    pe.wait_ge(S["diag_ready"], m + 1)
                                    for g in range(2):
                                        last = pe.matmul(YB[g][0:peer, :], diag[0:peer, m % 4, 0:peer],
                                                         ring[0:peer, r, 512 * g:512 * g + 512],
                                                         start=(k == 0), stop=(k == PICKS - 2))
                                        if g == 0:
                                            continue
                                        last.then_inc(consumed[r], 1)

                @block.vector
                def _(v):
                    step = Chain(v, S["dve_step"])

                    def norm(dst, src, rows, c, wait, ready, gain=None):
                        v.wait_ge(wait, 1)
                        inv = st[0:rows, c + 2:c + 3]
                        step(v.reciprocal(inv, st[0:rows, c:c + 1]))
                        if gain is None:
                            v.tensor_scalar(dst, src, inv, None, ALU.mult).then_inc(ready, 1)
                        else:
                            v.scalar_tensor_tensor(out=dst, in0=src, scalar=inv, in1=gain,
                                                   op0=ALU.mult, op1=ALU.mult).then_inc(ready, 1)

                    def turned(dst, rows, banks, wait, ready, gain=None):
                        v.wait_ge(wait, 1)
                        for g in range(2):
                            src = banks[g][:].rearrange("p (a c) -> p a c", a=4)[:, :, 0:rows]
                            d = dst[:, 4 * g:4 * g + 4, 0:rows]
                            if gain is None:
                                v.tensor_copy(d, src).then_inc(ready, 1)
                            else:
                                v.tensor_tensor(d, src, bcast(gain[:, 4 * g:4 * g + 4], rows), ALU.mult)\
                                    .then_inc(ready, 1)

                    def tail_norm():
                        v.wait_ge(S["pT_tr"], 1)
                        v.tensor_copy(pT[:, :, 0:t_rows], TB[0][:, 0:2 * P].rearrange("p (a c) -> p a c", a=2)
                                      [:, :, 0:t_rows]).then_inc(S["pT_ready"], 1)
                        norm(tn[0:t_rows, :], h2[0:t_rows, :], t_rows, 8, S["rms_ple"], S["t_ready"])
                        turned(tT, t_rows, SB, S["t_tr"], S["tT_ready"], g_ple)

                    def tail_gate():
                        n = first["proj"]
                        for j in range(4):
                            m = first["gate"] + j
                            v.wait_ge(proj_out[m % 2], m // 2 + 1)
                        v.wait_ge(S["proj_done"], n + 1)
                        for g in range(2):
                            c = slice(512 * g, 512 * g + 512)
                            step(v.tensor_tensor(sg[0:t_rows, c], SB[g][0:t_rows, :], sg[0:t_rows, c], ALU.mult))
                            v.tensor_tensor(h2[0:t_rows, c], h2[0:t_rows, c], sg[0:t_rows, c], ALU.add)\
                                .then_inc(S["h3_ready"], 1)
                        v.engine_nop().then_inc(proj_out[n % 2], 1)

                    def tail_fin():
                        norm(tn[0:t_rows, :], h2[0:t_rows, :], t_rows, 12, S["rms_fin"], S["y_ready"], g_fin[0:t_rows, :])

                    def norm_mix():
                        if f_sample:
                            v.memset(x[DEC:P, :], 0.0).then_inc(S["halo_done"], 1)
                        norm(an[:], x[:], P, 0, S["rms_mix"], S["a_ready"])
                        turned(aT, P, TB, S["a_tr"], S["aT_ready"], g_mix)

                    def conv():
                        for n in range(first["conv"], first["conv"] + 6):
                            v.wait_ge(proj_out[n % 2], n // 2 + 1)
                        scratch = arena[:, 0:CB * P].rearrange("p (a b) -> p a b", a=CB)
                        step(v.tensor_tensor(cT[:], zT[:, :, 0:P], bcast(taps[:, 0, :], P), ALU.mult))
                        for j in range(1, CW):
                            step(v.tensor_tensor(scratch, zT[:, :, j:j + P], bcast(taps[:, j, :], P), ALU.mult))
                            if j < CW - 1:
                                step(v.tensor_tensor(cT[:], cT[:], scratch, ALU.add))
                        v.tensor_tensor(cT[:], cT[:], scratch, ALU.add).then_inc(S["conv_in"], 1)
                        v.wait_ge(S["conv_in"], 1)
                        if not f_sample:
                            step(v.tensor_copy(zT[:, :, 0:CW - 1], zT[:, :, P:P + CW - 1]))

                    def gates():
                        n = first["ba_g"]
                        v.wait_ge(proj_out[n % 2], n // 2 + 1)
                        n = first["fox_v_f"]
                        v.wait_ge(proj_out[n % 2], n // 2 + 1)
                        step(v.tensor_tensor(y12[:, 0:HA], zba[:, HA:], bias12[:, 0:HA], ALU.add))
                        step(v.tensor_tensor(y12[:, HA:], zf[:], bias12[:, HA:], ALU.add))
                        v.tensor_scalar(y12[:, HA:], y12[:, HA:], -1.0, None, ALU.mult).then_inc(S["y_gate"], 1)
                        v.wait_ge(S["e_gate"], 1)
                        step(v.scalar_tensor_tensor(out=y12[:], in0=y12[:], scalar=0.0, in1=l12[:],
                                                    op0=ALU.max, op1=ALU.add))
                        step(v.tensor_tensor(la[:], y12[:, 0:HA], neg_a[:], ALU.mult))
                        if f_sample:
                            v.wait_ge(S["c_mm"], 1)
                        step(v.tensor_scalar(logf[:], y12[:, HA:], -1.0, None, ALU.mult))
                        step(v.tensor_scalar(bex[:], bex[:], 1.0, None, ALU.add))
                        step(v.reciprocal(beta[:], bex[:]))
                        if f_sample:
                            step(v.tensor_scalar(beta[:], beta[:], valid[:], None, ALU.mult))
                            step(v.tensor_scalar(la[:], la[:], valid[:], None, ALU.mult))
                        step(v.tensor_copy(lf40[:, 32:40], logf[:]))
                        v.tensor_scalar(lf40[:, 0:HB], logf[:], -1.0, None, ALU.mult).then_inc(S["lf_ready"], 1)

                    def gdn_v():
                        v.wait_ge(S["c_tr"], 1)
                        v.tensor_copy(ctok[:, 0:4, :], SB[0][:].rearrange("p (a c) -> p a c", a=4))
                        step(v.tensor_copy(ctok[:, 4:8, :], SB[1][:].rearrange("p (a c) -> p a c", a=4)))
                        sq = tmp[:].rearrange("p (a c) -> p a c", a=8)
                        step(v.tensor_tensor(sq, ctok[:, 0:8, :], ctok[:, 0:8, :], ALU.mult))
                        v.tensor_reduce(st2[:], sq, AX.X, ALU.add).then_inc(S["ss_gdn"], 1)
                        v.wait_ge(S["rms_gdn"], 1)
                        step(v.reciprocal(st2[:], st2[:]))
                        step(v.tensor_scalar(st2[:, 0:4], st2[:, 0:4], P ** -0.5, None, ALU.mult))
                        step(v.tensor_tensor(ctok[:, 0:8, :], ctok[:, 0:8, :], bcast(st2[:], P), ALU.mult))
                        v.tensor_tensor(kb, ctok[:, 4:8, :], bcast(beta[:], P), ALU.mult).then_inc(S["qkb_ready"], 1)

                    def gdn_qk():
                        v.wait_ge(S["qkb_tr"], 1)
                        v.tensor_copy(cT[:, 8:12, :], TB[1][:].rearrange("p (a c) -> p a c", a=4))\
                            .then_inc(S["kbT_out"], 1)

                    def decay():
                        v.tensor_tensor(latri, over(tri_gt[:], HA), bcast(la[:], P), ALU.mult)\
                            .then_inc(S["latri_ready"], 1)
                        v.wait_ge(S["dec_exp"], 1)
                        step(v.tensor_tensor(dec, dec, over(tri_le[:], HA), ALU.mult))
                        step(v.tensor_tensor(kb, ctok[:, 4:8, :], bcast(ge[:, 4:8], P), ALU.mult))
                        step(v.tensor_scalar(neg_eg[:], ge[:, 0:4], -1.0, None, ALU.mult))

                    def gram():
                        v.tensor_copy(tinv, over(ident[:], HA))
                        v.tensor_copy(ttinv, over(ident[:], HA)).then_inc(S["t_out"], 1)
                        v.wait_ge(S["kk_mm"], 1)
                        v.tensor_tensor(mt, SB[0][:].rearrange("p (a c) -> p a c", a=4), dec, ALU.mult)
                        v.tensor_tensor(attnT, SB[1][:].rearrange("p (a c) -> p a c", a=4), dec, ALU.mult)\
                            .then_inc(S["mt_ready"], 1)

                    def inverse(l):
                        v.wait_ge(S["d_mm"], l + 1)
                        v.wait_ge(S["t_out"], l + 1)
                        v.tensor_tensor(tinv, tinv, SB[0][:].rearrange("p (a c) -> p a c", a=4), ALU.subtract)
                        v.tensor_tensor(ttinv, ttinv, SB[1][:].rearrange("p (a c) -> p a c", a=4), ALU.subtract)\
                            .then_inc(S["t_out"], 1)

                    def state_u():
                        v.wait_ge(S["state_mm"], 1)
                        for h in range(HA):
                            last = v.scalar_tensor_tensor(out=rr[:, h, :], in0=TB[0][:, h * P:(h + 1) * P],
                                                          scalar=neg_eg[:, h:h + 1], in1=ctok[:, 8 + h, :],
                                                          op0=ALU.mult, op1=ALU.add)
                        step(last)
                        v.tensor_tensor(rr, rr, bcast(beta[:], P), ALU.mult).then_inc(S["r_ready"], 1)
                        v.wait_ge(S["au_out"], 1)
                        for h in range(HA):
                            last = v.scalar_tensor_tensor(out=mix[:, h * P:(h + 1) * P], in0=TB[1][:, h * P:(h + 1) * P],
                                                          scalar=ge[:, h:h + 1], in1=xx[:, h, :],
                                                          op0=ALU.mult, op1=ALU.add)
                        step(last)
                        for h in range(HA):
                            last = v.scalar_tensor_tensor(out=state[:, h, :], in0=state[:, h, :],
                                                          scalar=ge[:, 8 + h:9 + h], in1=TB[0][:, h * P:(h + 1) * P],
                                                          op0=ALU.mult, op1=ALU.add)
                        last.then_inc(S["s_ready"], 1)

                    def gdn_norm():
                        o = mix[:, 0:512].rearrange("p (a c) -> p a c", a=HA)
                        sq = tmp[:, 0:512].rearrange("p (a c) -> p a c", a=HA)
                        step(v.tensor_tensor(sq, o, o, ALU.mult))
                        v.tensor_reduce(st2[:, 0:4], sq, AX.X, ALU.add).then_inc(S["ssn_gdn"], 1)
                        v.wait_ge(S["rmsn_gdn"], 1)
                        step(v.reciprocal(st2[:, 0:4], st2[:, 0:4]))
                        step(v.tensor_tensor(o, o, bcast(st2[:, 0:4], P), ALU.mult))
                        step(v.tensor_tensor(o, o, over(g_gdn[:], HA), ALU.mult))
                        v.wait_ge(S["silu_go"], 1)
                        v.tensor_tensor(o, o, zg[:].rearrange("p (a c) -> p a c", a=HA), ALU.mult)\
                            .then_inc(S["oA_ready"], 1)

                    def cumulate(key, n):
                        v.wait_ge(S["c_mm"], n)
                        step(v.tensor_scalar(c40[:], TB[1][:, 0:P], carry[:], None, ALU.add))
                        step(v.tensor_copy(carry[:], c40[:, P - 1:P]))
                        return v.tensor_copy(aux[0:HB, key], c40[0:HB, :])

                    def fox_keys():
                        if f_sample:
                            v.wait_ge(S["past_loaded"], 48)
                            step(v.memset(carry[:], 0.0))
                            step(v.memset(pos[:], float(P)))
                            step(v.tensor_copy(lf40[:, 32:40], logf[:]))
                            v.tensor_scalar(lf40[:, 0:HB], logf[:], -1.0, None, ALU.mult)\
                                .then_inc(S["lf_past_ready"], 1)
                            v.wait_ge(S["lf_past_ready"], 1)
                            cumulate(slice(0, P), 1).then_inc(S["aux_ready"], 1)
                            v.wait_ge(S["aux_ready"], 1)

                    def fox_kT():
                        step(cumulate(f_key, 2 if f_sample else 1))
                        step(v.memset(c40[0:HB, :], 1.0))
                        v.tensor_tensor(faux, over(c40[:], HB), bcast(sel[:], P), ALU.mult)\
                            .then_inc(S["aux_ready"], 1)
                        step(v.tensor_scalar(cm, key_minus_q[:], pos[:], NEG, ALU.is_gt, ALU.mult))
                        step(v.tensor_scalar(pos[:], pos[:], float(P), None, ALU.add))

                    def fox_s(h):
                        v.wait_ge(S["s_mm"], h + 1)
                        if h == 0 and tail:
                            v.wait_ge(S["y_stored"], 16)
                        if h >= 2:
                            v.wait_ge(S["p_tr"], h - 1)
                        for g in range(2):
                                                        last = v.tensor_tensor_reduce(out=pbuf[h % 2][:, 512 * g:512 * g + 512], in0=SB[g][:],
                                                          in1=cm[:, 512 * g:512 * g + 512], scale=1.0, scalar=NEG * 10,
                                                          op0=ALU.add, op1=ALU.max, accum_out=fst[:, g:g + 1])
                        step(last)
                        v.tensor_tensor(fmax[:, h:h + 1], fst[:, 0:1], fst[:, 1:2], ALU.max).then_inc(S["s_max"], 1)
                        v.wait_ge(S["s_max"], h + 1)

                    def fox(h):
                        if h == 0:
                            fox_s(0)
                        if h + 1 < HB:
                            fox_s(h + 1)
                        v.wait_ge(S["p_tr"], h + 1)
                        if h >= 1:
                            v.wait_ge(S["o_fox"], h)
                        v.tensor_copy(pts[:, 4:8, :], TB[1][:].rearrange("p (a c) -> p a c", a=4))\
                            .then_inc(S["pt_dve"], 1)

                    def fox_norm():
                        v.wait_ge(S["o_fox"], HB)
                        v.wait_ge(S["p_exp"], HB)
                        step(v.reciprocal(finv[:], fsum[:]))
                        o = mix[:, 512:].rearrange("p (a c) -> p a c", a=HB)
                        sq = tmp[:, 0:512].rearrange("p (a c) -> p a c", a=HB)
                        step(v.tensor_tensor(o, AB[0][:].rearrange("p (a c) -> p a c", a=HB), bcast(finv[:], DHB), ALU.mult))
                        step(v.tensor_tensor(sq, o, o, ALU.mult))
                        v.tensor_reduce(st2[:], sq, AX.X, ALU.add).then_inc(S["ss_fox"], 1)
                        v.wait_ge(S["rms_fox"], 1)
                        step(v.reciprocal(st2[:], st2[:]))
                        step(v.tensor_tensor(o, o, bcast(st2[:], DHB), ALU.mult))
                        v.tensor_tensor(o, o, over(g_fox[:], HB), ALU.mult).then_inc(S["oB_ready"], 1)

                    def mix_turn():
                        turned(aT, P, TB, S["mix_tr"], S["mixT_ready"])

                    def out_proj(j):
                        n = first["out"] + j
                        v.wait_ge(S["proj_done"], n + 1)
                        v.tensor_tensor(x[:, 256 * j:256 * j + 256], x[:, 256 * j:256 * j + 256],
                                        AB[n % 2][:, 0:256], ALU.add).then_inc(S["h1_ready"], 1)
                        v.engine_nop().then_inc(proj_out[n % 2], 1)

                    def norm_ffn():
                        norm(an[:], x[:], P, 4, S["rms_ffn"], S["xn_ready"], g_ffn[:])
                        turned(aT, P, TB, S["xn_tr"], S["xnT_ready"])

                    def top16(values, vals, idxs, work):
                        step(v.max(vals[:, 0:8], values))
                        v.max_index(idxs[:, 0:8], vals[:, 0:8], values)
                        step(v.match_replace(work, vals[:, 0:8], values, NEG * 100))
                        step(v.max(vals[:, 8:16], work))
                        step(v.max_index(idxs[:, 8:16], vals[:, 8:16], work))

                    def pick_half(m):
                        if m % 4 == 0:
                            v.wait_ge(S["sc_out"], m // 4 + 1)
                        top16(sc[:, m, :], sv[:, m, :], si[:, m, :], sc2[:, 0:KEYS])

                    def pick_pairs(h):
                        if h == 0:
                            s1 = sv[:].rearrange("p (h c) k -> p h c k", c=2)
                            for hh in range(HP):
                                last = v.tensor_tensor(cand[:, hh, :].rearrange("p (a b) -> p a b", a=TOP),
                                                       bcast(sv[:, 2 * hh, :], TOP), over(sv[:, 2 * hh + 1, :], TOP),
                                                       ALU.add)
                            step(last)
                            step(v.tensor_copy(sif[:], si[:]))
                        top16(cand[:, h, :], cv[:, h, :], ci[:, h, :], sc2[:])

                    def pick_gate():
                        g3 = gate_n[:].rearrange("p (h k) -> p h k", h=HP)
                        v.tensor_tensor(g3, cv[:], cv[:, :, 0:1].to_broadcast([P, HP, TOP]), ALU.subtract)\
                            .then_inc(S["top_v"], 1)
                        for c in range(2):
                            if c == 0:
                                step(v.tensor_scalar(cd[:], ci[:], 4, None, ALU.logical_shift_right))
                            else:
                                step(v.tensor_scalar(cd[:], ci[:], 15, None, ALU.bitwise_and))
                            step(v.tensor_copy(cf[:], cd[:]))
                            for h in range(HP):
                                last = v.tensor_tensor(eq[:, h, :].rearrange("p (a b) -> p a b", a=TOP),
                                                       bcast(cf[:, h, :], TOP), over(iota16[:], TOP), ALU.is_equal)
                            step(last)
                            for h in range(HP):
                                e3 = eq[:, h, :].rearrange("p (a b) -> p a b", a=TOP)
                                last = v.tensor_tensor(e3, e3, over(sif[:, 2 * h + c, :], TOP), ALU.mult)
                            step(last)
                            step(v.tensor_reduce(ef[:, c, :, :], eq.rearrange("p h (a b) -> p h a b", a=TOP),
                                                 AX.X, ALU.add))
                        step(v.scalar_tensor_tensor(out=ef[:, 0, :, :], in0=ef[:, 0, :, :], scalar=float(KEYS),
                                                    in1=ef[:, 1, :, :], op0=ALU.mult, op1=ALU.add))
                        v.tensor_copy(idx_n[:].rearrange("p (h k) -> p h k", h=HP), ef[:, 0, :, :])
                        v.wait_ge(S["gate_e"], 1)
                        step(v.tensor_reduce(st2[:], g3, AX.X, ALU.add))
                        step(v.reciprocal(st2[:], st2[:]))
                        v.tensor_tensor(g3, g3, bcast(st2[:], TOP), ALU.mult).then_inc(S["gate_done"], 1)

                    plan = dict(tail_norm=tail_norm, tail_gate=tail_gate, tail_fin=tail_fin, norm_mix=norm_mix, conv=conv,
                                gates=gates, gdn_v=gdn_v, gdn_qk=gdn_qk, decay=decay, gram=gram, state_u=state_u,
                                gdn_norm=gdn_norm, fox_keys=fox_keys, fox_kT=fox_kT, fox_norm=fox_norm,
                                mix_turn=mix_turn, norm_ffn=norm_ffn, pick_gate=pick_gate)
                    plan.update({f"inv{l}": (lambda l=l: inverse(l)) for l in range(LEVELS)})
                    plan.update({f"fox{h}": (lambda h=h: fox(h)) for h in range(HB)})
                    plan.update({f"out{j}": (lambda j=j: out_proj(j)) for j in range(len(OUT_PIECES))})
                    plan.update({f"half{m}": (lambda m=m: pick_half(m)) for m in range(2 * HP)})
                    plan.update({f"pair{h}": (lambda h=h: pick_pairs(h)) for h in range(HP)})
                    last_add = None
                    for s in range(SLOTS):
                        for name in PLAN[s]:
                            if name in plan and (tail if name.startswith("tail") else front):
                                plan[name]()
                        if not peer:
                            continue
                        if s >= LAG and s % LAG == 0:
                            h = s // LAG - 1
                            v.wait_ge(S["w_gelu"], h + 1)
                            c = slice(TOP * h, TOP * h + TOP)
                            v.tensor_tensor(wgt[0:peer, c], wgt[0:peer, c], gate_c[0:peer, c], ALU.mult)\
                                .then_inc(S["w_ready"], 1)
                            v.wait_ge(S["w_ready"], h + 1)
                        for kind, k in ORDER[s]:
                            n = NUMBER[kind, k]
                            r = n % RING
                            row = ring[0:peer, r, :]
                            if kind == "u":
                                v.wait_ge(landed[r], 16 * (n // RING + 1))
                                v.tensor_tensor_reduce(out=row, in0=row, in1=xn_c[0:peer, :], scale=1.0, scalar=0.0,
                                                       op0=ALU.mult, op1=ALU.add, accum_out=dots[0:peer, k:k + 1])\
                                    .then_inc(consumed[r], 1)
                            elif not on_tensor(k):
                                v.wait_ge(landed[r], 16 * (n // RING + 1))
                                if last_add is None:
                                    ins = v.tensor_scalar(yacc[0:peer, :], row, wgt[0:peer, k:k + 1], None, ALU.mult)
                                else:
                                    wait_used(v, *last_add)
                                    ins = v.scalar_tensor_tensor(out=yacc[0:peer, :], in0=row, scalar=wgt[0:peer, k:k + 1],
                                                                 in1=yacc[0:peer, :], op0=ALU.mult, op1=ALU.add)
                                ins.then_inc(consumed[r], 1)
                                last_add = (kind, k)
                    if peer:
                        wait_used(v, *last_add)
                        wait_used(v, "v", PICKS - 2)
                        step(v.tensor_tensor(yacc[0:peer, :], yacc[0:peer, :], h_c[0:peer, :], ALU.add))
                        for g in range(2):
                            c = slice(512 * g, 512 * g + 512)
                            last = v.tensor_tensor(h2[0:peer, c], yacc[0:peer, c], YB[g][0:peer, :], ALU.add)
                        last.then_inc(S["h2_ready"], 1)
                    if front:
                        v.wait_ge(S["gate_done"], 1)
                        v.tensor_copy(idx_c[:], idx_n[:])
                        v.tensor_copy(gate_c[:], gate_n[:])
            nc.all_engine_barrier(sems_to_clear=range(numbers[0], numbers[-1] + 1))

        body(front=(0, P, 0, False))
        body(front=(1, P, 1, False), peer=P)
        with nc.Fori(2, TILES) as i:
            body(front=(i, P, i, False), peer=P, tail=(i - 2, P, False))
        body(front=(0, DEC, 1, True), peer=P, tail=(TILES - 2, P, False))
        body(peer=DEC, tail=(TILES - 1, P, False))
        body(tail=(0, DEC, True))


def make_plan():
    plan = [[] for _ in range(SLOTS)]
    plan[0] = ["tail_norm", "norm_mix", "fox_keys"]
    plan[1] = ["tail_gate", "tail_fin", "tail_store"]
    at = 2
    ins = [f"in{j}" for j in range(len(IN_PIECES))]
    for k in range(0, 14, 2):
        plan[at] += ins[k:k + 2]
        at += 1
    plan[at] += ["conv", "silu"]
    plan[at + 1] += ["gates", "gdn_v"]
    plan[at + 2] += ["gdn_qk", "decay", "gram"]
    at += 3
    for l in range(LEVELS):
        plan[at + l // 2] += [f"inv{l}"]
    at += 4
    plan[at] += ["state_u", "gdn_norm"]
    plan[at + 1] += ["fox_kT"]
    at += 2
    for h in range(HB):
        plan[at + h // 2] += [f"fox{h}"]
    at += 4
    plan[at] += ["fox_norm", "mix_turn", "out0", "out1", "out2", "out3"]
    plan[at + 1] += ["norm_ffn", "wq0", "wq1", "wq2", "wq3"]
    plan[at + 2] += ["wq4", "wq5", "wq6", "wq7", "scores"]
    at += 3
    for m in range(2 * HP):
        plan[at + m // 4] += [f"half{m}"]
    at += 4
    for h in range(HP):
        plan[at + h // 4] += [f"pair{h}"]
    at += 2
    plan[at] += ["pick_gate"]
    assert at < SLOTS
    return plan


PLAN = make_plan()

_INS = ["x_prompt", "x_sample", "p_prompt", "p_sample", "cache_conv", "state_gdn", "cache_fox_k", "cache_fox_v",
        "cache_fox_logf", "w_in", "conv_w", "a_log", "dt_bias", "gdn_onorm", "b_f", "fox_onorm", "w_out", "norm_mix",
        "norm_ffn", "peer_wq", "peer_keys", "peer_u", "peer_v", "norm_ple", "w_ple_proj", "w_ple_gate", "norm_final"]
_OUTS = [("y_prompt", (1, SEQ, D)), ("y_sample", (1, DEC, D)),
         ("conv_prompt", (1, 1, CW - 1, CONV)), ("gdn_prompt", (1, 1, HA, P, P)),
         ("k_prompt", (1, 1, SEQ, HB, DHB)), ("v_prompt", (1, 1, SEQ, HB, DHB)), ("logf_prompt", (1, 1, SEQ, HB)),
         ("conv_sample", (1, 1, CW - 1, CONV)), ("gdn_sample", (1, 1, HA, P, P)),
         ("k_sample", (1, 1, DEC, HB, DHB)), ("v_sample", (1, 1, DEC, HB, DHB)), ("logf_sample", (1, 1, DEC, HB))]


def kernel(**inputs):
    import numpy as _np
    import concourse.bacc as _bacc
    from concourse.bass_utils import run_bass_kernel_spmd as _run

    nc = _bacc.Bacc("TRN2", target_bir_lowering=False, num_devices=1)
    arrays, t, out = {}, {}, {}
    for name in _INS:
        a = _np.ascontiguousarray(inputs[name])
        arrays[name] = a
        t[name] = nc.dram_tensor(name, a.shape, F32, kind="ExternalInput").ap()
    t["peer_u"] = t["peer_u"].rearrange("a e d -> (a e) d")
    t["peer_v"] = t["peer_v"].rearrange("a e d -> (a e) d")
    for name, shape in _OUTS:
        out[name] = nc.dram_tensor("out_" + name, shape, F32, kind="ExternalOutput").ap()
    build(nc, t, out)
    r = _run(nc, [arrays], core_ids=[0])
    return tuple(r.results[0]["out_" + name] for name, _ in _OUTS)
```

```python
from contextlib import ExitStack

import concourse.bass as bass
from concourse import mybir

F32 = mybir.dt.float32
U32 = mybir.dt.uint32
ALU = mybir.AluOpType
ACT = mybir.ActivationFunctionType
AX = mybir.AxisListType

P = 128
D = 1024
DK = D // P
SEQ, DEC, PAST = 1024, 64, 128
TILES = SEQ // P
HA, HB, DHB = 4, 8, 64
CONV = 3 * HA * P
CB = CONV // P
CW = 4
COL_BA = CONV
COL_G = COL_BA + 2 * HA
COL_Q = COL_G + HA * P
COL_K = COL_Q + HB * DHB
COL_V = COL_K + HB * DHB
COL_F = COL_V + HB * DHB
COLS = COL_F + HB
HP, KEYS, TOP = 8, 128, 16
EXPERTS = KEYS * KEYS
PICKS = HP * TOP
PLE = 256
EPS = 1e-6
NEG = -1e30
LEVELS = 7

WCOLS = 264
WRING = 2
RING = 8
DIAGS = 4
PER_SLOT = 2
HEAD_SLOTS = TOP // PER_SLOT
LAG = HEAD_SLOTS + 1
SLOTS = PICKS // PER_SLOT + LAG

TAIL_PIECES = {f"gate{j}": ("gate", 256 * j, 256) for j in range(4)}
TAIL_PIECES.update({f"proj{g}": ("proj", 512 * g, 512) for g in range(2)})
IN_PIECES = {f"conv_in{j}": ("conv", 256 * j, 256) for j in range(6)}
IN_PIECES.update(ba_g=("ba_g", COL_BA, 264), g=("g", COL_BA + 264, 256))
IN_PIECES.update({f"fox_q{j}": ("fox_q", COL_Q + 256 * j, 256) for j in range(2)})
IN_PIECES.update({f"fox_k{j}": ("fox_k", COL_K + 256 * j, 256) for j in range(2)})
IN_PIECES.update(fox_v0=("fox_v", COL_V, 256), fox_v1=("fox_v_f", COL_V + 256, 264))
PIECES = {**TAIL_PIECES, **IN_PIECES}
PIECES.update({f"out{j}": ("out", 256 * j, 256) for j in range(4)})
PIECES.update({f"wq{j}": ("wq", 256 * j, 256) for j in range(HP)})
TAIL_STAGES = {"tail_norm", "tail_fin", *TAIL_PIECES}

SIGNALS = """
x_loaded prefix_loaded p_loaded past_loaded const_loaded stored
rms_mix a_ready a_tr aT_ready conv_in silu_go c_silu c_tr ctok_v ss_gdn rms_gdn qkb_ready qkb_tr qT_out kbT_out
y_gate e_gate dec_mm dec_exp kk_mm mt_ready inv_ct x_mm x_out d_mm t_out
state_mm r_ready qs_out u_mm u_out o_mm s_ready ssn_gdn rmsn_gdn oA_ready
lf_ready c_mm aux_ready cm_iota k_tr kT_done past_k_tr past_kT
s_mm s_max p_exp p_tr pt_out o_fox ss_fox rms_fox oB_ready mix_tr mixT_ready h1_ready
rms_ffn xn_ready xn_tr xnT_ready sc_mm sc_out top_v gate_e gate_done
h2_ready rms_ple t_ready t_tr tT_ready pT_tr pT_ready h3_ready rms_fin y_ready y_stored
proj_done out_even out_odd w_even w_odd dve_step act_step pool_step
w_gelu w_ready diag_ready setup_pe setup_ev setup_pool halo_done lf_past_ready
""".split()


def peer_order():
    order = []
    for s in range(SLOTS):
        own = []
        for j in range(PER_SLOT):
            if s < SLOTS - LAG:
                own.append(("u", PER_SLOT * s + j))
            if s >= LAG:
                own.append(("v", PER_SLOT * (s - LAG) + j))
        order.append(own)
    return order


ORDER = peer_order()
NUMBER = {e: n for n, e in enumerate(e for own in ORDER for e in own)}
TENSOR_PICKS = [k for k in range(PICKS) if k % 2 == 0]
TENSOR = {k: m for m, k in enumerate(TENSOR_PICKS)}


def build(nc, t, out):
    ctx = ExitStack()
    with ctx:
        def sb(name, shape, dt=F32):
            return ctx.enter_context(nc.sbuf_tensor(name, shape, dt))

        ident = sb("ident", [P, P])
        tri_le = sb("tri_le", [P, P])
        tri_gt = sb("tri_gt", [P, P])
        ones = sb("ones", [P, P])
        level_mask = sb("level_mask", [P, LEVELS, P])
        keysT = sb("keysT", [P, 2, KEYS])
        g_ffn = sb("g_ffn", [P, D])
        g_fin = sb("g_fin", [P, D])
        g_mix = sb("g_mix", [P, DK])
        g_ple = sb("g_ple", [P, DK])
        taps = sb("taps", [P, CW, CB])
        g_gdn = sb("g_gdn", [P, P])
        g_fox = sb("g_fox", [P, DHB])
        bias12 = sb("bias12", [P, HA + HB])
        neg_a = sb("neg_a", [P, HA])
        iota16 = sb("iota16", [P, TOP])
        pos = sb("pos", [P, 1])
        eps = sb("eps", [P, 1])
        valid = sb("valid", [P, 1])
        sel = sb("sel", [P, HB])
        x = sb("x", [P, D])
        an = sb("an", [P, D])
        aT = sb("aT", [P, DK, P])
        zT = sb("zT", [P, CB, CW - 1 + P])
        cT = sb("cT", [P, CB, P])
        ctok = sb("ctok", [P, CB, P])
        tmp = sb("tmp", [P, D])
        mix = sb("mix", [P, D])
        state = sb("state", [P, HA, P])
        zg = sb("zg", [P, HA * P])
        zba = sb("zba", [P, 2 * HA])
        zf = sb("zf", [P, HB])
        kst = sb("kst", [P, HB * DHB])
        fqT = sb("fqT", [P, HB, P])
        kTc = sb("kTc", [P, HB // 2, SEQ])
        vc = sb("vc", [P, TILES, HB * DHB])
        aux = sb("aux", [P, SEQ])
        y12 = sb("y12", [P, 12])
        e12 = sb("e12", [P, 12])
        l12 = sb("l12", [P, 12])
        beta = sb("beta", [P, HA])
        bex = sb("bex", [P, HA])
        la = sb("la", [P, HA])
        logf = sb("logf", [P, HB])
        lf40 = sb("lf40", [P, P])
        c40 = sb("c40", [P, P])
        carry = sb("carry", [P, 1])
        ge = sb("ge", [P, 12])
        neg_eg = sb("neg_eg", [P, HA])
        st = sb("st", [P, 16])
        fst = sb("fst", [P, 4])
        st2 = sb("st2", [P, 8])
        st4 = sb("st4", [P, HA])
        fneg = sb("fneg", [P, HB])
        fsum = sb("fsum", [P, HB])
        finv = sb("finv", [P, HB])
        si = sb("si", [P, 2 * HP, TOP], U32)
        idx_n = sb("idx_n", [P, PICKS], U32)
        gate_n = sb("gate_n", [P, PICKS])
        arena = sb("arena", [P, 38 * 256])

        def part(kb, size, **shape):
            v = arena[:, kb * 256:kb * 256 + size]
            return v.rearrange("p (a b) -> p a b", **shape) if shape else v

        dec = part(0, 512, a=HA)
        mt = part(2, 512, a=HA)
        latri = mt
        attnT = part(4, 512, a=HA)
        ct = [part(6, 512, a=HA), part(8, 512, a=HA)]
        tinv = part(10, 512, a=HA)
        ttinv = part(12, 512, a=HA)
        xx = part(14, 512, a=HA)
        kb = part(16, 512, a=HA)
        rr, uu = ct[0], ct[1]
        pbuf = [part(18, 1024), part(22, 1024)]
        pts = part(26, 1024, a=TILES)
        cm = part(30, 1024)
        faux = part(34, 1024, a=HB)
        qTp = part(0, 2048, a=2 * HP)
        sc = part(8, 2048, a=2 * HP)
        cand = part(16, 2048, a=HP)
        eq = part(24, 2048, a=HP)
        sc2 = part(32, 256)
        sif = part(33, 256, a=2 * HP)
        cd = part(34, 128, a=HP).bitcast(U32)
        cf = arena[:, 34 * 256 + 128:35 * 256].rearrange("p (a b) -> p a b", a=HP)
        ci = part(35, 128, a=HP).bitcast(U32)
        cv = arena[:, 35 * 256 + 128:36 * 256].rearrange("p (a b) -> p a b", a=HP)
        ef = part(36, 256).rearrange("p (c a b) -> p c a b", c=2, a=HP)
        sv = part(37, 256, a=2 * HP)
        tn = part(18, 1024)
        tT = part(22, 1024, a=DK)
        sg = part(26, 1024)
        prow = part(30, PLE)
        pT = part(31, 256, a=2)
        wring = sb("wring", [P, WRING, DK * WCOLS])
        ring = sb("ring", [P, RING, D])
        diag = sb("diag", [P, DIAGS, P])
        xn_c = sb("xn_c", [P, D])
        h_c = sb("h_c", [P, D])
        idx_c = sb("idx_c", [P, PICKS], U32)
        gate_c = sb("gate_c", [P, PICKS])
        dots = sb("dots", [P, PICKS])
        wgt = sb("wgt", [P, PICKS])
        h2 = sb("h2", [P, D])

        bank = [ctx.enter_context(nc.psum_tensor(f"bank{i}", [P, 512], F32)) for i in range(8)]
        YB, AB, SB, TB = bank[0:2], bank[2:4], bank[4:6], bank[6:8]

        names = SIGNALS + [f"landed{r}" for r in range(RING)] + [f"consumed{r}" for r in range(RING)]
        sems = [ctx.enter_context(nc.semaphore(n)) for n in names]
        S = dict(zip(names, sems))
        landed = [S[f"landed{r}"] for r in range(RING)]
        consumed = [S[f"consumed{r}"] for r in range(RING)]
        numbers = sorted(s.num for s in sems)
        assert numbers == list(range(numbers[0], numbers[-1] + 1))
        proj_out = [S["out_even"], S["out_odd"]]
        w_loaded = [S["w_even"], S["w_odd"]]

        def bcast(ap, n):
            return ap.unsqueeze(2).to_broadcast([ap.shape[0], ap.shape[1], n])

        def over(ap, n):
            return ap.unsqueeze(1).to_broadcast([ap.shape[0], n, ap.shape[1]])

        class Chain:
            def __init__(self, eng, sem):
                self.eng, self.sem, self.n = eng, sem, 0

            def __call__(self, ins):
                self.n += 1
                ins.then_inc(self.sem, 1)
                self.eng.wait_ge(self.sem, self.n)

        with nc.Block() as block:
            @block.sync
            def _(sp):
                rows = lambda a, w: a.rearrange("(o d) -> o d", o=1).to_broadcast([P, w])
                loads = [
                    (g_ffn[:], rows(t["norm_ffn"][0], D)), (g_fin[:], rows(t["norm_final"], D)),
                    (g_gdn[:], rows(t["gdn_onorm"][0], P)), (g_fox[:], rows(t["fox_onorm"][0], DHB)),
                    (bias12[:, 0:HA], rows(t["dt_bias"][0], HA)), (bias12[:, HA:], rows(t["b_f"][0], HB)),
                    (neg_a[:], rows(t["a_log"][0], HA)),
                    (g_mix[:], t["norm_mix"][0].rearrange("(k p) -> p k", p=P)),
                    (g_ple[:], t["norm_ple"][0].rearrange("(k p) -> p k", p=P)),
                    (tmp[:, 0:P], t["peer_keys"][0, 0]), (tmp[:, P:2 * P], t["peer_keys"][0, 1]),
                ] + [(taps[:, j, :], t["conv_w"][0, j].rearrange("(b p) -> p b", p=P)) for j in range(CW)]
                for dst, src in loads:
                    sp.dma_start(dst, src, allow_slow_non_contiguous=True).then_inc(S["const_loaded"], 16)
                sp.wait_ge(S["const_loaded"], 16 * len(loads))

            @block.gpsimd
            def _(pool):
                step = Chain(pool, S["pool_step"])
                step(pool.memset(ones[:], 1.0))
                step(pool.memset(ident[:], 0.0))
                step(pool.affine_select(out=ident[:], in_=ident[:], compare_op=ALU.not_equal, fill=1.0,
                                        base=0, pattern=[[-1, P]], channel_multiplier=1))
                step(pool.affine_select(out=tri_le[:], in_=ones[:], compare_op=ALU.is_ge, fill=0.0,
                                        base=0, pattern=[[1, P]], channel_multiplier=-1))
                step(pool.affine_select(out=tri_gt[:], in_=ones[:], compare_op=ALU.is_ge, fill=0.0,
                                        base=-1, pattern=[[-1, P]], channel_multiplier=1))
                step(pool.memset(level_mask[:], 0.0))
                for l in range(LEVELS):
                    b = 1 << l
                    n = P // (2 * b)
                    v = level_mask[:, l, :].rearrange("p (n c) -> p n c", n=n)[:, :, b:2 * b]
                    o = ones[:, 0:n * b].rearrange("p (n c) -> p n c", n=n)
                    step(pool.affine_select(out=v, in_=o, compare_op=ALU.is_ge, fill=0.0,
                                            base=0, pattern=[[-2 * b, n], [0, b]], channel_multiplier=1))
                    step(pool.affine_select(out=v, in_=v, compare_op=ALU.is_ge, fill=0.0,
                                            base=b - 1, pattern=[[2 * b, n], [0, b]], channel_multiplier=-1))
                step(pool.memset(sel[:], 0.0))
                for r in (0, 32):
                    step(pool.affine_select(out=sel[:], in_=sel[:], compare_op=ALU.not_equal, fill=1.0,
                                            base=-r, pattern=[[-1, HB]], channel_multiplier=1))
                step(pool.iota(iota16[:], pattern=[[1, TOP]], base=0, channel_multiplier=0,
                               allow_small_or_imprecise_dtypes=True))
                pool.engine_nop().then_inc(S["setup_pool"], 1)

            @block.vector
            def _(v):
                step = Chain(v, S["dve_step"])
                step(v.memset(kTc[:], 0.0))
                step(v.memset(vc[:], 0.0))
                step(v.memset(aux[:], 0.0))
                step(v.memset(aux[32:40, :], 1.0))
                step(v.memset(lf40[:], 0.0))
                step(v.memset(carry[:], 0.0))
                step(v.memset(zT[:, :, 0:CW - 1], 0.0))
                step(v.memset(state[:], 0.0))
                step(v.memset(pos[:], 0.0))
                step(v.memset(eps[:], EPS))
                step(v.memset(fqT[:], 0.0))
                step(v.memset(valid[:], 1.0))
                step(v.memset(valid[DEC:P, :], 0.0))
                v.wait_ge(S["setup_pe"], 1)
                step(v.tensor_copy(keysT[:], SB[0][:, 0:2 * KEYS].rearrange("p (c n) -> p c n", c=2)))
                v.wait_ge(S["setup_ev"], 1)
                step(v.tensor_scalar(neg_a[:], neg_a[:], -1.0, None, ALU.mult))

            @block.scalar
            def _(act):
                act.wait_ge(S["const_loaded"], 16 * 15)
                act.activation(neg_a[:], neg_a[:], ACT.Exp).then_inc(S["setup_ev"], 1)

            @block.tensor
            def _(pe):
                pe.wait_ge(S["const_loaded"], 16 * 15)
                pe.wait_ge(S["pool_step"], 3)
                for c in range(2):
                    last = pe.transpose(SB[0][:, c * KEYS:(c + 1) * KEYS], tmp[:, c * P:(c + 1) * P], ident[:])
                last.then_inc(S["setup_pe"], 1)
        nc.all_engine_barrier(sems_to_clear=range(numbers[0], numbers[-1] + 1))

        def body(front=None, peer=None, tail=None, blocks=TILES):
            names = [name for name in PIECE_ORDER if (tail if name in TAIL_PIECES else front)]
            pieces = [PIECES[name] for name in names]
            number = {name: n for n, name in enumerate(names)}
            keys = blocks * P
            n_halves = (blocks + 3) // 4
            halves = [range(4 * g, min(4 * g + 4, blocks)) for g in range(n_halves)]
            if front:
                f_i, f_rows, f_blk, f_sample = front
                f_src = t["x_sample"][0] if f_sample else t["x_prompt"][0][bass.ds(f_i * P, P), :]
                f_key = bass.ds(f_blk * P, P)
            if tail:
                t_i, t_rows, t_sample = tail
                t_p = t["p_sample"][0, 0] if t_sample else t["p_prompt"][0, 0][bass.ds(t_i * P, P), :]
                t_y = out["y_sample"][0] if t_sample else out["y_prompt"][0][bass.ds(t_i * P, P), :]
            mats = {"gate": t["w_ple_gate"], "proj": t["w_ple_proj"], "out": t["w_out"], "wq": t["peer_wq"]}
            n_store = [0]

            def four(b):
                return b[:].rearrange("p (a c) -> p a c", a=4)

            def wait_out(eng, *names):
                for name in names:
                    n = number[name]
                    eng.wait_ge(proj_out[n % 2], n // 2 + 1)

            def wait_used(eng, kind, k):
                n = NUMBER[kind, k]
                eng.wait_ge(consumed[n % RING], n // RING + 1)

            def walker(stages):
                begun = {}

                def next_part(name):
                    if name not in stages or not (tail if name in TAIL_STAGES else front):
                        return
                    if name not in begun:
                        begun[name] = stages[name]() or iter(())
                    next(begun[name], None)
                return next_part

            with nc.Block() as block:
                @block.sync
                def _(sp):
                    if tail:
                        sp.dma_start(prow[0:t_rows, :], t_p).then_inc(S["p_loaded"], 16)
                    if front:
                        sp.dma_start(x[0:f_rows, :], f_src).then_inc(S["x_loaded"], 16)
                        if f_sample:
                            for j in range(CW - 1):
                                sp.dma_start(out["conv_prompt"][0, 0, j].rearrange("(b p) -> p b", p=P), zT[:, :, j],
                                             allow_slow_non_contiguous=True).then_inc(S["stored"], 16)
                            sp.dma_start(out["gdn_prompt"][0, 0].rearrange("h k v -> k h v"),
                                         state[:]).then_inc(S["stored"], 16)
                            sp.wait_ge(S["stored"], 16 * CW)
                            n_store[0] = CW
                            for j in range(CW - 1):
                                sp.dma_start(zT[:, :, j], t["cache_conv"][0, 0, j].rearrange("(b p) -> p b", p=P),
                                             allow_slow_non_contiguous=True).then_inc(S["prefix_loaded"], 16)
                            sp.dma_start(state[:], t["state_gdn"][0, 0].rearrange("h k v -> k h v"))\
                              .then_inc(S["prefix_loaded"], 16)
                            sp.dma_start(kst[:], t["cache_fox_k"][0, 0].rearrange("t h d -> t (h d)"))\
                              .then_inc(S["past_loaded"], 16)
                            sp.dma_start(vc[:, 0, :], t["cache_fox_v"][0, 0].rearrange("t h d -> t (h d)"))\
                              .then_inc(S["past_loaded"], 16)
                            sp.dma_start(logf[:], t["cache_fox_logf"][0, 0]).then_inc(S["past_loaded"], 16)
                    for n, (what, c, w) in enumerate(pieces):
                        if n >= WRING:
                            sp.wait_ge(S["proj_done"], n - WRING + 1)
                        src = mats.get(what, t["w_in"])[0].rearrange("(k p) n -> p k n", p=P)
                        k = src.shape[1]
                        sp.dma_start(wring[:, n % WRING, 0:k * w].rearrange("p (k n) -> p k n", k=k),
                                     src[:, :, c:c + w]).then_inc(w_loaded[n % WRING], 16)
                    if front:
                        o = "_sample" if f_sample else "_prompt"
                        rows = slice(0, DEC) if f_sample else bass.ds(f_i * P, P)
                        sp.wait_ge(S["kT_done"], 1)
                        sp.dma_start(out["k" + o][0, 0].rearrange("t h d -> t (h d)")[rows, :],
                                     kst[0:f_rows, :]).then_inc(S["stored"], 16)
                        wait_out(sp, "fox_v0", "fox_v1")
                        vrow = vc[0:f_rows, f_blk, :] if isinstance(f_blk, int) else \
                            vc[:, bass.ds(f_blk, 1), :].rearrange("p a b -> p (a b)")
                        sp.dma_start(out["v" + o][0, 0].rearrange("t h d -> t (h d)")[rows, :],
                                     vrow).then_inc(S["stored"], 16)
                        sp.wait_ge(S["lf_ready"], 1)
                        sp.dma_start(out["logf" + o][0, 0][rows, :], logf[0:f_rows, :]).then_inc(S["stored"], 16)
                        n_store[0] += 3
                        if f_sample:
                            sp.wait_ge(S["s_ready"], 1)
                            sp.dma_start(out["gdn_sample"][0, 0].rearrange("h k v -> k h v"),
                                         state[:]).then_inc(S["stored"], 16)
                            for j in range(CW - 1):
                                sp.dma_start(out["conv_sample"][0, 0, j].rearrange("(b p) -> p b", p=P),
                                             zT[:, :, DEC + j], allow_slow_non_contiguous=True)\
                                  .then_inc(S["stored"], 16)
                            n_store[0] += CW
                    if tail:
                        sp.wait_ge(S["y_stored"], 16)
                    if n_store[0]:
                        sp.wait_ge(S["stored"], 16 * n_store[0])

                @block.gpsimd
                def _(pool):
                    def inv_masks(l):
                        if l == 0:
                            pool.wait_ge(S["mt_ready"], 1)
                        if l >= 2:
                            pool.wait_ge(S["t_out"], l - 1)
                        pool.tensor_tensor(ct[l % 2], mt, over(level_mask[:, l, :], HA), ALU.mult)\
                            .then_inc(S["inv_ct"], 1)

                    def fox_keys():
                        if tail:
                            pool.wait_ge(S["y_stored"], 16)
                        pool.iota(cm[:, 0:keys], pattern=[[1, keys]], base=0, channel_multiplier=-1,
                                  allow_small_or_imprecise_dtypes=True).then_inc(S["cm_iota"], 1)

                    stages = dict(fox_keys=fox_keys)
                    stages.update({f"inv{l}": (lambda l=l: inv_masks(l)) for l in range(LEVELS)})
                    next_part = walker(stages)
                    for s in range(SLOTS):
                        for name in PLAN[s]:
                            next_part(name)
                        if peer:
                            for kind, k in ORDER[s]:
                                n = NUMBER[kind, k]
                                r = n % RING
                                if n >= RING:
                                    pool.wait_ge(consumed[r], n // RING)
                                pool.indirect_dma_start(
                                    out=ring[0:peer, r, :], out_offset=None, in_=t["peer_" + kind],
                                    in_offset=bass.IndirectOffsetOnAxis(ap=idx_c[0:peer, k:k + 1], axis=0),
                                ).then_inc(landed[r], 16)
                    if peer:
                        for n in range(2 * PICKS - RING, 2 * PICKS):
                            pool.wait_ge(consumed[n % RING], n // RING + 1)
                        pool.dma_reset(range(landed[0].num, landed[-1].num + 1))

                @block.scalar
                def _(act):
                    step = Chain(act, S["act_step"])

                    def rms(src, rows, c, junk, done):
                        step(act.activation(junk[0:rows, :], src, ACT.Square, accum_out=st[0:rows, c + 1:c + 2]))
                        act.activation(st[0:rows, c:c + 1], st[0:rows, c + 1:c + 2], ACT.Sqrt, bias=eps[0:rows, :],
                                       scale=1.0 / D).then_inc(done, 1)

                    def evac(name, pairs, func=ACT.Copy, scale=1.0):
                        n = number[name]
                        act.wait_ge(S["proj_done"], n + 1)
                        for dst, src in pairs:
                            last = act.activation(dst, src, func, scale=scale)
                        last.then_inc(proj_out[n % 2], 1)

                    def tail_norm():
                        rms(h2[0:t_rows, :], t_rows, 8, tn, S["rms_ple"])

                    def tail_gate(j):
                        name = f"gate{j}"
                        evac(name, [(sg[0:t_rows, 256 * j:256 * j + 256], AB[number[name] % 2][0:t_rows, 0:256])],
                             ACT.Sigmoid)

                    def tail_fin():
                        act.wait_ge(S["h3_ready"], 2)
                        rms(h2[0:t_rows, :], t_rows, 12, tn, S["rms_fin"])
                        yield
                        yield
                        act.wait_ge(S["y_ready"], 1)
                        act.dma_start(t_y, tn[0:t_rows, :]).then_inc(S["y_stored"], 16)

                    def norm_mix():
                        act.wait_ge(S["x_loaded"], 16)
                        if f_sample:
                            act.wait_ge(S["halo_done"], 1)
                        rms(x[:], P, 0, tmp, S["rms_mix"])

                    def in_proj(name):
                        n = number[name]
                        what, c, w = PIECES[name]
                        b = AB[n % 2]
                        if what == "conv":
                            if name == "conv_in0" and f_sample:
                                act.wait_ge(S["prefix_loaded"], 16 * CW)
                            evac(name, [(zT[:, c // P:c // P + 2, CW - 1:],
                                         b[:, 0:256].rearrange("p (a c) -> p a c", a=2))])
                        elif what == "ba_g":
                            evac(name, [(zba[:], b[:, 0:8]), (zg[:, 0:256], b[:, 8:264])])
                        elif what == "g":
                            evac(name, [(zg[:, 256:512], b[:, 0:256])])
                        elif what == "fox_q":
                            m = (c - COL_Q) // P
                            heads = fqT[:].rearrange("p (m o) c -> p m o c", o=2)
                            b3 = b[:, 0:256].rearrange("p (a c) -> p a c", a=2)
                            evac(name, [(heads[DHB * o:DHB * o + DHB, m:m + 2, o, :], b3[DHB * o:DHB * o + DHB])
                                        for o in range(2)], scale=DHB ** -0.5)
                        elif what == "fox_k":
                            if f_sample:
                                act.wait_ge(S["past_k_tr"], 1)
                            evac(name, [(kst[:, c - COL_K:c - COL_K + 256], b[:, 0:256])])
                        else:
                            m = c - COL_V
                            dst = vc[:, bass.ds(f_blk, 1), m:m + 256].rearrange("p a b -> p (a b)")
                            if what == "fox_v_f":
                                evac(name, [(dst, b[:, 0:256]), (zf[:], b[:, 256:264])])
                            else:
                                evac(name, [(dst, b[:, 0:256])])

                    def conv(g):
                        act.wait_ge(S["conv_in"], g + 1)
                        act.activation(cT[:, 4 * g:4 * g + 4, :], cT[:, 4 * g:4 * g + 4, :], ACT.Silu)\
                            .then_inc(S["c_silu"], 1)
                        yield
                        if g == 2:
                            act.wait_ge(S["c_tr"], 3)
                            act.activation(ctok[:, 8:12, :], four(TB[0]), ACT.Copy).then_inc(S["ctok_v"], 1)

                    def silu_g():
                        wait_out(act, "ba_g", "g")
                        act.activation(zg[:], zg[:], ACT.Silu).then_inc(S["silu_go"], 1)

                    def gates():
                        act.wait_ge(S["y_gate"], 1)
                        step(act.activation(e12[:], y12[:], ACT.Abs))
                        step(act.activation(e12[:], e12[:], ACT.Exp, scale=-1.0))
                        act.activation(l12[:], e12[:], ACT.Ln, bias=1.0)
                        act.activation(bex[:], zba[:, 0:HA], ACT.Exp, scale=-1.0).then_inc(S["e_gate"], 1)

                    def gdn():
                        act.wait_ge(S["ss_gdn"], 1)
                        act.activation(st2[:], st2[:], ACT.Sqrt, bias=eps[:]).then_inc(S["rms_gdn"], 1)
                        yield
                        yield
                        act.wait_ge(S["qkb_tr"], 1)
                        act.activation(cT[:, 0:4, :], four(SB[0]), ACT.Copy)
                        act.activation(cT[:, 4:8, :], four(SB[1]), ACT.Copy).then_inc(S["qT_out"], 1)
                        act.wait_ge(S["dec_mm"], 1)
                        act.activation(dec, four(TB[0]), ACT.Exp).then_inc(S["dec_exp"], 1)
                        yield
                        act.wait_ge(S["dec_mm"], 2)
                        act.activation(ge[:], TB[1][:, 0:12], ACT.Exp).then_inc(S["dec_exp"], 1)

                    def inverse(l):
                        if l == 0:
                            return
                        act.wait_ge(S["x_mm"], l + 1)
                        if l >= 2:
                            act.wait_ge(S["d_mm"], l - 1)
                        act.activation(xx, four(AB[0]), ACT.Copy).then_inc(S["x_out"], 1)

                    def state_u():
                        yield
                        yield
                        act.wait_ge(S["u_mm"], 1)
                        act.activation(uu, four(AB[0]), ACT.Copy).then_inc(S["u_out"], 1)

                    def gdn_norm():
                        act.wait_ge(S["ssn_gdn"], 1)
                        act.activation(st4[:], st4[:], ACT.Sqrt, bias=eps[:], scale=1.0 / P)\
                            .then_inc(S["rmsn_gdn"], 1)

                    def fox_past():
                        if not f_sample:
                            return
                        yield
                        act.wait_ge(S["past_k_tr"], 1)
                        act.activation(kTc[:, :, 0:P], four(TB[0]), ACT.Copy).then_inc(S["past_kT"], 1)

                    def fox_keys():
                        act.wait_ge(S["k_tr"], 1)
                        act.activation(kTc[:, :, f_key], four(TB[0]), ACT.Copy).then_inc(S["kT_done"], 1)

                    def fox_s(h):
                        yield
                        act.wait_ge(S["s_max"], h + 1)
                        act.activation(pbuf[h % 2][:, 0:keys], pbuf[h % 2][:, 0:keys], ACT.Exp,
                                       bias=fneg[:, h:h + 1], accum_out=fsum[:, h:h + 1]).then_inc(S["p_exp"], 1)

                    def fox_o(h):
                        n = n_halves * h
                        act.wait_ge(S["p_tr"], n + 1)
                        if h >= 1:
                            act.wait_ge(S["o_fox"], h)
                        b = len(halves[0])
                        act.activation(pts[:, 0:b, :], four(TB[0])[:, 0:b], ACT.Copy).then_inc(S["pt_out"], 1)

                    def fox_norm():
                        act.wait_ge(S["ss_fox"], 1)
                        act.activation(st2[:], st2[:], ACT.Sqrt, bias=eps[:], scale=1.0 / DHB)\
                            .then_inc(S["rms_fox"], 1)

                    def norm_ffn():
                        act.wait_ge(S["h1_ready"], 4)
                        rms(x[:], P, 4, tmp, S["rms_ffn"])

                    def wq(j):
                        name = f"wq{j}"
                        evac(name, [(qTp[:, 2 * j:2 * j + 2, :],
                                     AB[number[name] % 2][:, 0:256].rearrange("p (a c) -> p a c", a=2))])

                    def scores(g):
                        act.wait_ge(S["sc_mm"], g + 1)
                        act.activation(sc[:, 4 * g:4 * g + 4, :], four((SB + TB)[g]), ACT.Copy)\
                            .then_inc(S["sc_out"], 1)

                    def pick_gate():
                        act.wait_ge(S["top_v"], 1)
                        act.activation(gate_n[:], gate_n[:], ACT.Exp).then_inc(S["gate_e"], 1)

                    def hand_rows():
                        if peer:
                            wait_used(act, "u", PICKS - 1)
                        act.wait_ge(S["xn_ready"], 1)
                        act.activation(xn_c[:], an[:], ACT.Copy)

                    stages = dict(tail_norm=tail_norm, tail_fin=tail_fin, norm_mix=norm_mix, silu_g=silu_g, gates=gates,
                                  gdn=gdn, state=state_u, gdn_norm=gdn_norm, fox_past=fox_past, fox_keys=fox_keys,
                                  fox_norm=fox_norm, norm_ffn=norm_ffn, pick_gate=pick_gate, hand_rows=hand_rows)
                    stages.update({f"gate{j}": (lambda j=j: tail_gate(j)) for j in range(4)})
                    stages.update({name: (lambda name=name: in_proj(name)) for name in IN_PIECES})
                    stages.update({f"conv{g}": (lambda g=g: conv(g)) for g in range(3)})
                    stages.update({f"inv{l}": (lambda l=l: inverse(l)) for l in range(LEVELS)})
                    stages.update({f"fox_s{h}": (lambda h=h: fox_s(h)) for h in range(HB)})
                    stages.update({f"fox_o{h}": (lambda h=h: fox_o(h)) for h in range(HB)})
                    stages.update({f"wq{j}": (lambda j=j: wq(j)) for j in range(HP)})
                    stages.update({f"scores{g}": (lambda g=g: scores(g)) for g in range(4)})
                    next_part = walker(stages)
                    for s in range(SLOTS):
                        if peer:
                            for k in [k for kind, k in ORDER[s] if kind == "v" and k in TENSOR]:
                                m = TENSOR[k]
                                act.wait_ge(S["w_ready"], k // TOP + 1)
                                if m >= DIAGS:
                                    wait_used(act, "v", TENSOR_PICKS[m - DIAGS])
                                act.activation(diag[0:peer, m % DIAGS, 0:peer], ident[0:peer, 0:peer], ACT.Copy,
                                               scale=wgt[0:peer, k:k + 1]).then_inc(S["diag_ready"], 1)
                            if s and s % HEAD_SLOTS == 0 and s // HEAD_SLOTS <= HP:
                                h = s // HEAD_SLOTS - 1
                                wait_used(act, "u", TOP * h + TOP - 1)
                                act.activation(wgt[0:peer, TOP * h:TOP * h + TOP],
                                               dots[0:peer, TOP * h:TOP * h + TOP], ACT.Gelu)\
                                    .then_inc(S["w_gelu"], 1)
                        for name in PLAN[s]:
                            next_part(name)
                    if front:
                        if peer:
                            act.wait_ge(S["h2_ready"], 1)
                        act.activation(h_c[:], x[:], ACT.Copy)

                @block.tensor
                def _(pe):
                    def transpose8(src, rows, banks, done):
                        for k in range(DK):
                            last = pe.transpose(banks[k // 4][:, (k % 4) * P:(k % 4) * P + rows],
                                                src[0:rows, k * P:(k + 1) * P], ident[0:rows, 0:rows])
                        last.then_inc(done, 1)

                    def transpose4(bank_, src, m0):
                        for m in range(4):
                            last = pe.transpose(bank_[:, m * P:(m + 1) * P], src[:, m0 + m, :], ident[:])
                        return last

                    def project(name, actT, rows, turned=False):
                        n = number[name]
                        what, c, w = PIECES[name]
                        k8 = 2 if what == "proj" else DK
                        wt = wring[:, n % WRING, 0:k8 * w].rearrange("p (k n) -> p k n", k=k8)
                        pe.wait_ge(w_loaded[n % WRING], 16 * (n // WRING + 1))
                        if n >= 2:
                            pe.wait_ge(proj_out[n % 2], n // 2)
                        b = AB[n % 2]
                        if turned:
                            for m in range(w // P):
                                for k in range(DK):
                                    last = pe.matmul(b[:, m * P:m * P + rows], wt[:, k, m * P:(m + 1) * P],
                                                     actT[:, k, 0:rows], start=(k == 0), stop=(k == DK - 1))
                        else:
                            for k in range(k8):
                                last = pe.matmul(b[0:rows, 0:w], actT[:, k, 0:rows], wt[:, k, :],
                                                 start=(k == 0), stop=(k == k8 - 1))
                        last.then_inc(S["proj_done"], 1)

                    def tail_norm():
                        pe.wait_ge(S["p_loaded"], 16)
                        for k in range(2):
                            last = pe.transpose(TB[0][:, k * P:k * P + t_rows], prow[0:t_rows, k * P:(k + 1) * P],
                                                ident[0:t_rows, 0:t_rows])
                        last.then_inc(S["pT_tr"], 1)
                        yield
                        pe.wait_ge(S["t_ready"], 1)
                        transpose8(tn, t_rows, SB, S["t_tr"])

                    def tail_gate(j):
                        pe.wait_ge(S["tT_ready"], 2)
                        project(f"gate{j}", tT, t_rows)

                    def tail_proj(g):
                        pe.wait_ge(S["pT_ready"], 1)
                        project(f"proj{g}", pT, t_rows)

                    def norm_mix():
                        yield
                        pe.wait_ge(S["a_ready"], 1)
                        transpose8(an, P, AB, S["a_tr"])

                    def in_proj(name):
                        if name == "conv_in0":
                            pe.wait_ge(S["aT_ready"], 2)
                        project(name, aT, P, PIECES[name][0] in ("conv", "fox_q"))

                    def conv(g):
                        yield
                        pe.wait_ge(S["c_silu"], g + 1)
                        if g == 0 and tail:
                            pe.wait_ge(S["tT_ready"], 2)
                            pe.wait_ge(S["pT_ready"], 1)
                        if g == 2 and f_sample:
                            pe.wait_ge(S["past_kT"], 1)
                        transpose4((SB + TB)[g], cT, 4 * g).then_inc(S["c_tr"], 1)

                    def gdn():
                        yield
                        yield
                        pe.wait_ge(S["qkb_ready"], 1)
                        pe.wait_ge(S["ctok_v"], 1)
                        transpose4(SB[0], ctok, 0)
                        transpose4(SB[1], ctok, 4)
                        if f_sample:
                            pe.wait_ge(S["aux_ready"], 1)
                        transpose4(TB[1], kb, 0).then_inc(S["qkb_tr"], 1)
                        for h in range(HA):
                            last = pe.matmul(TB[0][:, h * P:(h + 1) * P], latri[:, h, :], tri_le[:],
                                             start=True, stop=True)
                        last.then_inc(S["dec_mm"], 1)
                        yield
                        pe.wait_ge(S["kbT_out"], 1)
                        for m, lhs in enumerate((tri_le, tri_gt, ones)):
                            last = pe.matmul(TB[1][:, 4 * m:4 * m + 4], lhs[:], la[:], start=True, stop=True)
                        last.then_inc(S["dec_mm"], 1)
                        pe.wait_ge(S["qT_out"], 1)
                        for h in range(HA):
                            pe.matmul(SB[0][:, h * P:(h + 1) * P], cT[:, 4 + h, :], cT[:, 8 + h, :], start=True, stop=True)
                        for h in range(HA):
                            last = pe.matmul(SB[1][:, h * P:(h + 1) * P], cT[:, 4 + h, :], cT[:, h, :],
                                             start=True, stop=True)
                        last.then_inc(S["kk_mm"], 1)

                    def inverse(l):
                        pe.wait_ge(S["inv_ct"], l + 1)
                        if l == 0:
                            wait_out(pe, *[name for name in names if name in IN_PIECES][-2:])
                            transpose4(AB[0], ct[0], 0).then_inc(S["x_mm"], 1)
                            return
                        pe.wait_ge(S["t_out"], l)
                        for h in range(HA):
                            last = pe.matmul(AB[0][:, h * P:(h + 1) * P], ct[l % 2][:, h, :], tinv[:, h, :],
                                             start=True, stop=True)
                        last.then_inc(S["x_mm"], 1)
                        yield
                        pe.wait_ge(S["x_out"], l)
                        for h in range(HA):
                            pe.matmul(AB[0][:, h * P:(h + 1) * P], ttinv[:, h, :], xx[:, h, :], start=True, stop=True)
                        for h in range(HA):
                            last = pe.matmul(AB[1][:, h * P:(h + 1) * P], xx[:, h, :], ttinv[:, h, :],
                                             start=True, stop=True)
                        last.then_inc(S["d_mm"], 1)

                    def state_u():
                        if f_sample:
                            pe.wait_ge(S["prefix_loaded"], 16 * CW)
                        pe.wait_ge(S["t_out"], LEVELS)
                        for h in range(HA):
                            pe.matmul(AB[0][:, h * P:(h + 1) * P], cT[:, 4 + h, :], state[:, h, :], start=True, stop=True)
                        for h in range(HA):
                            last = pe.matmul(AB[1][:, h * P:(h + 1) * P], cT[:, h, :], state[:, h, :],
                                             start=True, stop=True)
                        last.then_inc(S["state_mm"], 1)
                        yield
                        yield
                        pe.wait_ge(S["r_ready"], 1)
                        for h in range(HA):
                            last = pe.matmul(AB[0][:, h * P:(h + 1) * P], ttinv[:, h, :], rr[:, h, :],
                                             start=True, stop=True)
                        last.then_inc(S["u_mm"], 1)
                        yield
                        pe.wait_ge(S["u_out"], 1)
                        pe.wait_ge(S["qs_out"], 1)
                        for h in range(HA):
                            pe.matmul(AB[0][:, h * P:(h + 1) * P], attnT[:, h, :], uu[:, h, :], start=True, stop=True)
                        for h in range(HA):
                            last = pe.matmul(AB[1][:, h * P:(h + 1) * P], kb[:, h, :], uu[:, h, :],
                                             start=True, stop=True)
                        last.then_inc(S["o_mm"], 1)

                    def fox_past():
                        if not f_sample:
                            return
                        yield
                        pe.wait_ge(S["lf_past_ready"], 1)
                        pe.matmul(TB[1][:, 0:P], lf40[:], tri_le[:], start=True, stop=True).then_inc(S["c_mm"], 1)
                        pe.wait_ge(S["past_loaded"], 48)
                        if tail:
                            pe.wait_ge(S["pT_ready"], 1)
                        for m in range(4):
                            last = pe.transpose(TB[0][:, m * P:(m + 1) * P], kst[:, m * P:(m + 1) * P], ident[:])
                        last.then_inc(S["past_k_tr"], 1)

                    def fox_keys():
                        wait_out(pe, "fox_k0", "fox_k1")
                        pe.wait_ge(S["dec_exp"], 2)
                        for m in range(4):
                            last = pe.transpose(TB[0][:, m * P:(m + 1) * P], kst[:, m * P:(m + 1) * P], ident[:])
                        last.then_inc(S["k_tr"], 1)
                        pe.wait_ge(S["lf_ready"], 1)
                        pe.matmul(TB[1][:, 0:P], lf40[:], tri_le[:], start=True, stop=True).then_inc(S["c_mm"], 1)

                    def fox_s(h):
                        if h == 0:
                            wait_out(pe, "fox_q0", "fox_q1")
                            pe.wait_ge(S["kT_done"], 1)
                            pe.wait_ge(S["aux_ready"], 2 if f_sample else 1)
                            pe.wait_ge(S["mt_ready"], 1)
                        else:
                            pe.wait_ge(S["s_max"], h)
                        for g, own in enumerate(halves):
                            c = slice(P * own[0], P * own[-1] + P)
                            w = P * len(own)
                            pe.matmul(SB[g][:, 0:w], fqT[:, h, :], kTc[:, h // 2, c], start=True, stop=False)
                            last = pe.matmul(SB[g][:, 0:w], faux[:, h, :], aux[:, c], start=False, stop=True)
                        last.then_inc(S["s_mm"], 1)

                    def fox_o(h):
                        pe.wait_ge(S["p_exp"], h + 1)
                        for g, own in enumerate(halves):
                            n = n_halves * h + g
                            if n >= 1:
                                pe.wait_ge(S["pt_out"], n)
                            for m in own:
                                last = pe.transpose(TB[0][:, (m % 4) * P:(m % 4 + 1) * P],
                                                    pbuf[h % 2][:, m * P:(m + 1) * P], ident[:])
                            last.then_inc(S["p_tr"], 1)
                            yield
                        if n_halves == 1:
                            yield
                        pe.wait_ge(S["pt_out"], n_halves * h + n_halves)
                        if h == 0:
                            pe.wait_ge(S["aux_ready"], 2 if f_sample else 1)
                            wait_out(pe, "fox_v0", "fox_v1")
                        for m in range(blocks):
                            last = pe.matmul(TB[1][:, h * DHB:(h + 1) * DHB], pts[:, m, :],
                                             vc[:, m, h * DHB:(h + 1) * DHB], start=(m == 0), stop=(m == blocks - 1))
                        last.then_inc(S["o_fox"], 1)

                    def mix_turn():
                        pe.wait_ge(S["oA_ready"], 1)
                        pe.wait_ge(S["oB_ready"], 1)
                        transpose8(mix, P, TB, S["mix_tr"])

                    def out_proj(j):
                        if j == 0:
                            pe.wait_ge(S["mixT_ready"], 2)
                        project(f"out{j}", aT, P)

                    def norm_ffn():
                        yield
                        yield
                        pe.wait_ge(S["xn_ready"], 1)
                        transpose8(an, P, TB, S["xn_tr"])

                    def wq(j):
                        if j == 0:
                            pe.wait_ge(S["xnT_ready"], 2)
                        project(f"wq{j}", aT, P, True)

                    def scores(g):
                        wait_out(pe, f"wq{2 * g}", f"wq{2 * g + 1}")
                        for m in range(4):
                            last = pe.matmul((SB + TB)[g][:, m * P:(m + 1) * P], qTp[:, 4 * g + m, :],
                                             keysT[:, m % 2, :], start=True, stop=True)
                        last.then_inc(S["sc_mm"], 1)

                    stages = dict(tail_norm=tail_norm, norm_mix=norm_mix, gdn=gdn, state=state_u, fox_past=fox_past,
                                  fox_keys=fox_keys, mix_turn=mix_turn, norm_ffn=norm_ffn)
                    stages.update({f"gate{j}": (lambda j=j: tail_gate(j)) for j in range(4)})
                    stages.update({f"proj{g}": (lambda g=g: tail_proj(g)) for g in range(2)})
                    stages.update({name: (lambda name=name: in_proj(name)) for name in IN_PIECES})
                    stages.update({f"conv{g}": (lambda g=g: conv(g)) for g in range(3)})
                    stages.update({f"inv{l}": (lambda l=l: inverse(l)) for l in range(LEVELS)})
                    stages.update({f"fox_s{h}": (lambda h=h: fox_s(h)) for h in range(HB)})
                    stages.update({f"fox_o{h}": (lambda h=h: fox_o(h)) for h in range(HB)})
                    stages.update({f"out{j}": (lambda j=j: out_proj(j)) for j in range(4)})
                    stages.update({f"wq{j}": (lambda j=j: wq(j)) for j in range(HP)})
                    stages.update({f"scores{g}": (lambda g=g: scores(g)) for g in range(4)})
                    next_part = walker(stages)
                    for s in range(SLOTS):
                        for name in PLAN[s]:
                            next_part(name)
                        if peer:
                            for kind, k in ORDER[s]:
                                if kind == "v" and k in TENSOR:
                                    n = NUMBER[kind, k]
                                    r = n % RING
                                    m = TENSOR[k]
                                    pe.wait_ge(landed[r], 16 * (n // RING + 1))
                                    pe.wait_ge(S["diag_ready"], m + 1)
                                    for g in range(2):
                                        last = pe.matmul(YB[g][0:peer, :], diag[0:peer, m % DIAGS, 0:peer],
                                                         ring[0:peer, r, 512 * g:512 * g + 512],
                                                         start=(m == 0), stop=(m == len(TENSOR) - 1))
                                    last.then_inc(consumed[r], 1)

                @block.vector
                def _(v):
                    step = Chain(v, S["dve_step"])

                    def norm(dst, src, rows, c, wait, ready, gain=None):
                        v.wait_ge(wait, 1)
                        inv = st[0:rows, c + 2:c + 3]
                        step(v.reciprocal(inv, st[0:rows, c:c + 1]))
                        if gain is None:
                            v.tensor_scalar(dst, src, inv, None, ALU.mult).then_inc(ready, 1)
                        else:
                            v.scalar_tensor_tensor(out=dst, in0=src, scalar=inv, in1=gain,
                                                   op0=ALU.mult, op1=ALU.mult).then_inc(ready, 1)

                    def turned(dst, rows, banks, wait, ready, gain=None):
                        v.wait_ge(wait, 1)
                        for g in range(2):
                            src = four(banks[g])[:, :, 0:rows]
                            d = dst[:, 4 * g:4 * g + 4, 0:rows]
                            if gain is None:
                                v.tensor_copy(d, src).then_inc(ready, 1)
                            else:
                                v.tensor_tensor(d, src, bcast(gain[:, 4 * g:4 * g + 4], rows), ALU.mult)\
                                    .then_inc(ready, 1)

                    def tail_norm():
                        yield
                        v.wait_ge(S["pT_tr"], 1)
                        v.tensor_copy(pT[:, :, 0:t_rows], TB[0][:, 0:2 * P].rearrange("p (a c) -> p a c", a=2)
                                      [:, :, 0:t_rows]).then_inc(S["pT_ready"], 1)
                        norm(tn[0:t_rows, :], h2[0:t_rows, :], t_rows, 8, S["rms_ple"], S["t_ready"])
                        yield
                        turned(tT, t_rows, SB, S["t_tr"], S["tT_ready"], g_ple)

                    def tail_proj(g):
                        yield
                        name = f"proj{g}"
                        n = number[name]
                        wait_out(v, f"gate{2 * g}", f"gate{2 * g + 1}")
                        v.wait_ge(S["proj_done"], n + 1)
                        c = slice(512 * g, 512 * g + 512)
                        step(v.tensor_tensor(sg[0:t_rows, c], AB[n % 2][0:t_rows, :], sg[0:t_rows, c], ALU.mult))
                        v.tensor_tensor(h2[0:t_rows, c], h2[0:t_rows, c], sg[0:t_rows, c], ALU.add)\
                            .then_inc(S["h3_ready"], 1)
                        v.engine_nop().then_inc(proj_out[n % 2], 1)

                    def tail_fin():
                        yield
                        norm(tn[0:t_rows, :], h2[0:t_rows, :], t_rows, 12, S["rms_fin"], S["y_ready"], g_fin[0:t_rows, :])

                    def norm_mix():
                        if f_sample:
                            v.memset(x[DEC:P, :], 0.0).then_inc(S["halo_done"], 1)
                        yield
                        norm(an[:], x[:], P, 0, S["rms_mix"], S["a_ready"])
                        yield
                        turned(aT, P, AB, S["a_tr"], S["aT_ready"], g_mix)

                    def conv(g):
                        wait_out(v, f"conv_in{2 * g}", f"conv_in{2 * g + 1}")
                        b = slice(4 * g, 4 * g + 4)
                        scratch = part(2 * g, 512, a=4)
                        step(v.tensor_tensor(cT[:, b, :], zT[:, b, 0:P], bcast(taps[:, 0, b], P), ALU.mult))
                        for j in range(1, CW):
                            step(v.tensor_tensor(scratch, zT[:, b, j:j + P], bcast(taps[:, j, b], P), ALU.mult))
                            if j < CW - 1:
                                step(v.tensor_tensor(cT[:, b, :], cT[:, b, :], scratch, ALU.add))
                        v.tensor_tensor(cT[:, b, :], cT[:, b, :], scratch, ALU.add).then_inc(S["conv_in"], 1)
                        if not f_sample:
                            step(v.tensor_copy(zT[:, b, 0:CW - 1], zT[:, b, P:P + CW - 1]))
                        yield
                        if g < 2:
                            yield
                            v.wait_ge(S["c_tr"], g + 1)
                            step(v.tensor_copy(ctok[:, b, :], four(SB[g])))

                    def gates():
                        wait_out(v, "ba_g", "fox_v1")
                        step(v.tensor_tensor(y12[:, 0:HA], zba[:, HA:], bias12[:, 0:HA], ALU.add))
                        step(v.tensor_tensor(y12[:, HA:], zf[:], bias12[:, HA:], ALU.add))
                        v.tensor_scalar(y12[:, HA:], y12[:, HA:], -1.0, None, ALU.mult).then_inc(S["y_gate"], 1)
                        yield
                        v.wait_ge(S["e_gate"], 1)
                        step(v.scalar_tensor_tensor(out=y12[:], in0=y12[:], scalar=0.0, in1=l12[:],
                                                    op0=ALU.max, op1=ALU.add))
                        step(v.tensor_tensor(la[:], y12[:, 0:HA], neg_a[:], ALU.mult))
                        if f_sample:
                            v.wait_ge(S["c_mm"], 1)
                        step(v.tensor_scalar(logf[:], y12[:, HA:], -1.0, None, ALU.mult))
                        step(v.tensor_scalar(bex[:], bex[:], 1.0, None, ALU.add))
                        step(v.reciprocal(beta[:], bex[:]))
                        if f_sample:
                            step(v.tensor_scalar(beta[:], beta[:], valid[:], None, ALU.mult))
                            step(v.tensor_scalar(la[:], la[:], valid[:], None, ALU.mult))
                        step(v.tensor_copy(lf40[:, 32:40], logf[:]))
                        v.tensor_scalar(lf40[:, 0:HB], logf[:], -1.0, None, ALU.mult).then_inc(S["lf_ready"], 1)

                    def gdn():
                        sq = tmp[:].rearrange("p (a c) -> p a c", a=8)
                        step(v.tensor_tensor(sq, ctok[:, 0:8, :], ctok[:, 0:8, :], ALU.mult))
                        v.tensor_reduce(st2[:], sq, AX.X, ALU.add).then_inc(S["ss_gdn"], 1)
                        yield
                        v.wait_ge(S["lf_ready"], 1)
                        step(v.tensor_tensor(latri, over(tri_gt[:], HA), bcast(la[:], P), ALU.mult))
                        v.wait_ge(S["rms_gdn"], 1)
                        step(v.reciprocal(st2[:], st2[:]))
                        step(v.tensor_scalar(st2[:, 0:4], st2[:, 0:4], P ** -0.5, None, ALU.mult))
                        step(v.tensor_tensor(ctok[:, 0:8, :], ctok[:, 0:8, :], bcast(st2[:], P), ALU.mult))
                        v.tensor_tensor(kb, ctok[:, 4:8, :], bcast(beta[:], P), ALU.mult).then_inc(S["qkb_ready"], 1)
                        yield
                        yield
                        v.wait_ge(S["qkb_tr"], 1)
                        v.tensor_copy(cT[:, 8:12, :], four(TB[1])).then_inc(S["kbT_out"], 1)
                        v.wait_ge(S["dec_exp"], 1)
                        step(v.tensor_tensor(dec, dec, over(tri_le[:], HA), ALU.mult))
                        yield
                        v.wait_ge(S["dec_exp"], 2)
                        step(v.tensor_tensor(kb, ctok[:, 4:8, :], bcast(ge[:, 4:8], P), ALU.mult))
                        step(v.tensor_scalar(neg_eg[:], ge[:, 0:4], -1.0, None, ALU.mult))
                        v.wait_ge(S["kk_mm"], 1)
                        v.tensor_tensor(mt, four(SB[0]), dec, ALU.mult)
                        v.tensor_tensor(attnT, four(SB[1]), dec, ALU.mult).then_inc(S["mt_ready"], 1)

                    def inverse(l):
                        if l == 0:
                            yield
                            v.wait_ge(S["inv_ct"], 1)
                            v.tensor_tensor(ttinv, over(ident[:], HA), ct[0], ALU.subtract)
                            v.wait_ge(S["x_mm"], 1)
                            v.tensor_tensor(tinv, over(ident[:], HA), four(AB[0]), ALU.subtract)\
                                .then_inc(S["t_out"], 1)
                            return
                        yield
                        yield
                        v.wait_ge(S["d_mm"], l)
                        v.wait_ge(S["t_out"], l)
                        v.tensor_tensor(tinv, tinv, four(AB[0]), ALU.subtract)
                        v.tensor_tensor(ttinv, ttinv, four(AB[1]), ALU.subtract).then_inc(S["t_out"], 1)

                    def state_u():
                        yield
                        v.wait_ge(S["state_mm"], 1)
                        for h in range(HA):
                            last = v.scalar_tensor_tensor(out=rr[:, h, :], in0=AB[0][:, h * P:(h + 1) * P],
                                                          scalar=neg_eg[:, h:h + 1], in1=ctok[:, 8 + h, :],
                                                          op0=ALU.mult, op1=ALU.add)
                        step(last)
                        v.tensor_tensor(rr, rr, bcast(beta[:], P), ALU.mult).then_inc(S["r_ready"], 1)
                        oA = mix[:, 0:512].rearrange("p (a c) -> p a c", a=HA)
                        v.tensor_tensor(oA, four(AB[1]), bcast(ge[:, 0:4], P), ALU.mult).then_inc(S["qs_out"], 1)
                        yield
                        yield
                        yield
                        v.wait_ge(S["o_mm"], 1)
                        v.wait_ge(S["qs_out"], 1)
                        step(v.tensor_tensor(oA, oA, four(AB[0]), ALU.add))
                        for h in range(HA):
                            last = v.scalar_tensor_tensor(out=state[:, h, :], in0=state[:, h, :],
                                                          scalar=ge[:, 8 + h:9 + h], in1=AB[1][:, h * P:(h + 1) * P],
                                                          op0=ALU.mult, op1=ALU.add)
                        last.then_inc(S["s_ready"], 1)

                    def gdn_norm():
                        o = mix[:, 0:512].rearrange("p (a c) -> p a c", a=HA)
                        sq = tmp[:, 0:512].rearrange("p (a c) -> p a c", a=HA)
                        step(v.tensor_tensor(sq, o, o, ALU.mult))
                        v.tensor_reduce(st4[:], sq, AX.X, ALU.add).then_inc(S["ssn_gdn"], 1)
                        yield
                        v.wait_ge(S["rmsn_gdn"], 1)
                        step(v.reciprocal(st4[:], st4[:]))
                        step(v.tensor_tensor(o, o, bcast(st4[:], P), ALU.mult))
                        step(v.tensor_tensor(o, o, over(g_gdn[:], HA), ALU.mult))
                        v.wait_ge(S["silu_go"], 1)
                        v.tensor_tensor(o, o, zg[:].rearrange("p (a c) -> p a c", a=HA), ALU.mult)\
                            .then_inc(S["oA_ready"], 1)

                    def cumulate(key, n):
                        v.wait_ge(S["c_mm"], n)
                        step(v.tensor_scalar(c40[:], TB[1][:, 0:P], carry[:], None, ALU.add))
                        step(v.tensor_copy(carry[:], c40[:, P - 1:P]))
                        return v.tensor_copy(aux[0:HB, key], c40[0:HB, :])

                    def fox_past():
                        if not f_sample:
                            return
                        v.wait_ge(S["past_loaded"], 48)
                        step(v.memset(carry[:], 0.0))
                        step(v.memset(pos[:], float(P)))
                        step(v.tensor_copy(lf40[:, 32:40], logf[:]))
                        v.tensor_scalar(lf40[:, 0:HB], logf[:], -1.0, None, ALU.mult)\
                            .then_inc(S["lf_past_ready"], 1)
                        yield
                        yield
                        cumulate(slice(0, P), 1).then_inc(S["aux_ready"], 1)
                        v.wait_ge(S["aux_ready"], 1)

                    def fox_keys():
                        yield
                        step(cumulate(f_key, 2 if f_sample else 1))
                        step(v.memset(c40[0:HB, :], 1.0))
                        if tail:
                            v.wait_ge(S["y_stored"], 16)
                        v.tensor_tensor(faux, over(c40[:], HB), bcast(sel[:], P), ALU.mult)\
                            .then_inc(S["aux_ready"], 1)
                        v.wait_ge(S["cm_iota"], 1)
                        step(v.tensor_scalar(cm[:, 0:keys], cm[:, 0:keys], pos[:], NEG, ALU.is_gt, ALU.mult))
                        step(v.tensor_scalar(pos[:], pos[:], float(P), None, ALU.add))

                    def fox_s(h):
                        yield
                        v.wait_ge(S["s_mm"], h + 1)
                        if h >= 2:
                            v.wait_ge(S["p_tr"], n_halves * (h - 1))
                        for g, own in enumerate(halves):
                            c = slice(P * own[0], P * own[-1] + P)
                            last = v.tensor_tensor_reduce(out=pbuf[h % 2][:, c], in0=SB[g][:, 0:P * len(own)],
                                                          in1=cm[:, c], scale=1.0, scalar=NEG * 10,
                                                          op0=ALU.add, op1=ALU.max, accum_out=fst[:, g:g + 1])
                        step(last)
                        if n_halves == 2:
                            step(v.tensor_tensor(fst[:, 0:1], fst[:, 0:1], fst[:, 1:2], ALU.max))
                        v.tensor_scalar(fneg[:, h:h + 1], fst[:, 0:1], -1.0, None, ALU.mult).then_inc(S["s_max"], 1)
                        v.wait_ge(S["s_max"], h + 1)

                    def fox_o(h):
                        if n_halves == 1:
                            return
                        yield
                        v.wait_ge(S["p_tr"], 2 * h + 2)
                        if h >= 1:
                            v.wait_ge(S["o_fox"], h)
                        b = len(halves[1])
                        v.tensor_copy(pts[:, 4:4 + b, :], four(TB[0])[:, 0:b]).then_inc(S["pt_out"], 1)

                    def fox_norm():
                        v.wait_ge(S["o_fox"], HB)
                        v.wait_ge(S["p_exp"], HB)
                        step(v.reciprocal(finv[:], fsum[:]))
                        o = mix[:, 512:].rearrange("p (a c) -> p a c", a=HB)
                        sq = tmp[:, 0:512].rearrange("p (a c) -> p a c", a=HB)
                        step(v.tensor_tensor(o, TB[1][:].rearrange("p (a c) -> p a c", a=HB), bcast(finv[:], DHB), ALU.mult))
                        step(v.tensor_tensor(sq, o, o, ALU.mult))
                        v.tensor_reduce(st2[:], sq, AX.X, ALU.add).then_inc(S["ss_fox"], 1)
                        yield
                        v.wait_ge(S["rms_fox"], 1)
                        step(v.reciprocal(st2[:], st2[:]))
                        step(v.tensor_tensor(o, o, bcast(st2[:], DHB), ALU.mult))
                        v.tensor_tensor(o, o, over(g_fox[:], HB), ALU.mult).then_inc(S["oB_ready"], 1)

                    def mix_turn():
                        yield
                        turned(aT, P, TB, S["mix_tr"], S["mixT_ready"])

                    def out_proj(j):
                        yield
                        n = number[f"out{j}"]
                        v.wait_ge(S["proj_done"], n + 1)
                        v.tensor_tensor(x[:, 256 * j:256 * j + 256], x[:, 256 * j:256 * j + 256],
                                        AB[n % 2][:, 0:256], ALU.add).then_inc(S["h1_ready"], 1)
                        v.engine_nop().then_inc(proj_out[n % 2], 1)

                    def norm_ffn():
                        yield
                        norm(an[:], x[:], P, 4, S["rms_ffn"], S["xn_ready"], g_ffn[:])
                        yield
                        yield
                        turned(aT, P, TB, S["xn_tr"], S["xnT_ready"])

                    def top16(values, vals, idxs, work):
                        step(v.max(vals[:, 0:8], values))
                        v.max_index(idxs[:, 0:8], vals[:, 0:8], values)
                        step(v.match_replace(work, vals[:, 0:8], values, NEG * 100))
                        step(v.max(vals[:, 8:16], work))
                        step(v.max_index(idxs[:, 8:16], vals[:, 8:16], work))

                    def pick_half(m):
                        if m % 4 == 0:
                            v.wait_ge(S["sc_out"], m // 4 + 1)
                        top16(sc[:, m, :], sv[:, m, :], si[:, m, :], sc2[:, 0:KEYS])

                    def pick_pairs(h):
                        step(v.tensor_tensor(cand[:, h, :].rearrange("p (a b) -> p a b", a=TOP),
                                             bcast(sv[:, 2 * h, :], TOP), over(sv[:, 2 * h + 1, :], TOP), ALU.add))
                        top16(cand[:, h, :], cv[:, h, :], ci[:, h, :], sc2[:])

                    def pick_gate():
                        g3 = gate_n[:].rearrange("p (h k) -> p h k", h=HP)
                        v.tensor_tensor(g3, cv[:], cv[:, :, 0:1].to_broadcast([P, HP, TOP]), ALU.subtract)\
                            .then_inc(S["top_v"], 1)
                        step(v.tensor_copy(sif[:], si[:]))
                        for c in range(2):
                            if c == 0:
                                step(v.tensor_scalar(cd[:], ci[:], 4, None, ALU.logical_shift_right))
                            else:
                                step(v.tensor_scalar(cd[:], ci[:], 15, None, ALU.bitwise_and))
                            step(v.tensor_copy(cf[:], cd[:]))
                            for h in range(HP):
                                last = v.tensor_tensor(eq[:, h, :].rearrange("p (a b) -> p a b", a=TOP),
                                                       bcast(cf[:, h, :], TOP), over(iota16[:], TOP), ALU.is_equal)
                            step(last)
                            yield
                            for h in range(HP):
                                e3 = eq[:, h, :].rearrange("p (a b) -> p a b", a=TOP)
                                last = v.tensor_tensor(e3, e3, over(sif[:, 2 * h + c, :], TOP), ALU.mult)
                            step(last)
                            step(v.tensor_reduce(ef[:, c, :, :], eq.rearrange("p h (a b) -> p h a b", a=TOP),
                                                 AX.X, ALU.add))
                            yield
                        step(v.scalar_tensor_tensor(out=ef[:, 0, :, :], in0=ef[:, 0, :, :], scalar=float(KEYS),
                                                    in1=ef[:, 1, :, :], op0=ALU.mult, op1=ALU.add))
                        v.tensor_copy(idx_n[:].rearrange("p (h k) -> p h k", h=HP), ef[:, 0, :, :])
                        v.wait_ge(S["gate_e"], 1)
                        step(v.tensor_reduce(st2[:], g3, AX.X, ALU.add))
                        step(v.reciprocal(st2[:], st2[:]))
                        v.tensor_tensor(g3, g3, bcast(st2[:], TOP), ALU.mult).then_inc(S["gate_done"], 1)

                    stages = dict(tail_norm=tail_norm, tail_fin=tail_fin, norm_mix=norm_mix, gates=gates, gdn=gdn,
                                  state=state_u, gdn_norm=gdn_norm, fox_past=fox_past, fox_keys=fox_keys,
                                  fox_norm=fox_norm, mix_turn=mix_turn, norm_ffn=norm_ffn, pick_gate=pick_gate)
                    stages.update({f"proj{g}": (lambda g=g: tail_proj(g)) for g in range(2)})
                    stages.update({f"conv{g}": (lambda g=g: conv(g)) for g in range(3)})
                    stages.update({f"inv{l}": (lambda l=l: inverse(l)) for l in range(LEVELS)})
                    stages.update({f"fox_s{h}": (lambda h=h: fox_s(h)) for h in range(HB)})
                    stages.update({f"fox_o{h}": (lambda h=h: fox_o(h)) for h in range(HB)})
                    stages.update({f"out{j}": (lambda j=j: out_proj(j)) for j in range(4)})
                    stages.update({f"half{m}": (lambda m=m: pick_half(m)) for m in range(2 * HP)})
                    stages.update({f"pair{h}": (lambda h=h: pick_pairs(h)) for h in range(HP)})
                    next_part = walker(stages)
                    last_add = None
                    for s in range(SLOTS):
                        for name in PLAN[s]:
                            next_part(name)
                        if not peer:
                            continue
                        if s and s % HEAD_SLOTS == 0 and s // HEAD_SLOTS <= HP:
                            h = s // HEAD_SLOTS - 1
                            v.wait_ge(S["w_gelu"], h + 1)
                            c = slice(TOP * h, TOP * h + TOP)
                            v.tensor_tensor(wgt[0:peer, c], wgt[0:peer, c], gate_c[0:peer, c], ALU.mult)\
                                .then_inc(S["w_ready"], 1)
                        for kind, k in ORDER[s]:
                            n = NUMBER[kind, k]
                            r = n % RING
                            row = ring[0:peer, r, :]
                            if kind == "u":
                                v.wait_ge(landed[r], 16 * (n // RING + 1))
                                v.tensor_tensor_reduce(out=row, in0=row, in1=xn_c[0:peer, :], scale=1.0, scalar=0.0,
                                                       op0=ALU.mult, op1=ALU.add, accum_out=dots[0:peer, k:k + 1])\
                                    .then_inc(consumed[r], 1)
                            elif k not in TENSOR:
                                v.wait_ge(landed[r], 16 * (n // RING + 1))
                                v.wait_ge(S["w_ready"], k // TOP + 1)
                                if last_add is not None:
                                    wait_used(v, *last_add)
                                v.scalar_tensor_tensor(out=h_c[0:peer, :], in0=row, scalar=wgt[0:peer, k:k + 1],
                                                       in1=h_c[0:peer, :], op0=ALU.mult, op1=ALU.add)\
                                    .then_inc(consumed[r], 1)
                                last_add = (kind, k)
                    if peer:
                        wait_used(v, *last_add)
                        wait_used(v, "v", TENSOR_PICKS[-1])
                        for g in range(2):
                            c = slice(512 * g, 512 * g + 512)
                            last = v.tensor_tensor(h2[0:peer, c], h_c[0:peer, c], YB[g][0:peer, :], ALU.add)
                        last.then_inc(S["h2_ready"], 1)
                    if front:
                        v.wait_ge(S["gate_done"], 1)
                        v.tensor_copy(idx_c[:], idx_n[:])
                        v.tensor_copy(gate_c[:], gate_n[:])
            nc.all_engine_barrier(sems_to_clear=range(numbers[0], numbers[-1] + 1))

        body(front=(0, P, 0, False), blocks=1)
        body(front=(1, P, 1, False), peer=P, blocks=2)
        with nc.Fori(2, TILES // 2) as i:
            body(front=(i, P, i, False), peer=P, tail=(i - 2, P, False), blocks=TILES // 2)
        with nc.Fori(TILES // 2, TILES) as i:
            body(front=(i, P, i, False), peer=P, tail=(i - 2, P, False), blocks=TILES)
        body(front=(0, DEC, 1, True), peer=P, tail=(TILES - 2, P, False), blocks=2)
        body(peer=DEC, tail=(TILES - 1, P, False))
        body(tail=(0, DEC, True))


def make_plan():
    plan = [[] for _ in range(SLOTS)]

    def at(slot, *names):
        plan[slot].extend(names)

    def spread(name, *slots):
        for s in slots:
            at(s, name)

    spread("tail_norm", 0, 1, 2)
    spread("norm_mix", 0, 1, 2)
    spread("fox_past", 3, 4, 5)
    for j in range(6):
        at(3 + j, f"conv_in{j}")
    for g in range(3):
        spread(f"conv{g}", 5 + 2 * g, 6 + 2 * g, 7 + 2 * g)
    at(9, "ba_g")
    at(10, "fox_v1")
    spread("gates", 11, 12)
    for j in range(4):
        at(11 + j, f"gate{j}")
    spread("gdn", 12, 13, 14, 15, 16)
    at(15, "proj0")
    at(16, "proj0", "proj1", "fox_v0")
    at(17, "proj1", "fox_k0")
    spread("tail_fin", 18, 19, 20)
    at(18, "fox_k1")
    at(19, "fox_q0")
    at(20, "fox_q1")
    spread("fox_keys", 20, 21)
    at(21, "g")
    at(22, "silu_g")
    s = 22
    spread("inv0", s, s + 1)
    for l in range(1, LEVELS):
        spread(f"inv{l}", s + 2 * l - 1, s + 2 * l, s + 2 * l + 1)
    s += 2 * LEVELS
    spread("state", s - 1 + 0, s + 1, s + 2, s + 3, s + 4)
    spread("gdn_norm", s + 5, s + 6)
    for h in range(HB):
        s = 21 + 1 + int(2.75 * h)
        spread(f"fox_s{h}", s, s + 1)
        spread(f"fox_o{h}", s + 2, s + 3, s + 4)
    s += 5
    spread("fox_norm", s, s + 1)
    spread("mix_turn", s + 1, s + 2)
    s += 2
    for j in range(4):
        spread(f"out{j}", s + j, s + j + 1)
    s += 4
    spread("norm_ffn", s, s + 1, s + 1, s + 2)
    s += 2
    for j in range(HP):
        at(s + j, f"wq{j}")
        if j % 2:
            g = j // 2
            at(s + j, f"scores{g}")
            for m in range(4):
                at(s + j + 1 + m // 2, f"half{4 * g + m}")
            for m in range(2):
                at(s + j + 2 + m, f"pair{2 * g + m}")
    s += HP + 2
    spread("pick_gate", s, s + 1, s + 2, s + 3, s + 4)
    at(HP * HEAD_SLOTS + 1, "hand_rows")
    assert s + 4 < SLOTS, s
    return plan


PLAN = make_plan()
PIECE_ORDER = list(dict.fromkeys(name for slot in PLAN for name in slot if name in PIECES))

_INS = ["x_prompt", "x_sample", "p_prompt", "p_sample", "cache_conv", "state_gdn", "cache_fox_k", "cache_fox_v",
        "cache_fox_logf", "w_in", "conv_w", "a_log", "dt_bias", "gdn_onorm", "b_f", "fox_onorm", "w_out", "norm_mix",
        "norm_ffn", "peer_wq", "peer_keys", "peer_u", "peer_v", "norm_ple", "w_ple_proj", "w_ple_gate", "norm_final"]
_OUTS = [("y_prompt", (1, SEQ, D)), ("y_sample", (1, DEC, D)),
         ("conv_prompt", (1, 1, CW - 1, CONV)), ("gdn_prompt", (1, 1, HA, P, P)),
         ("k_prompt", (1, 1, SEQ, HB, DHB)), ("v_prompt", (1, 1, SEQ, HB, DHB)), ("logf_prompt", (1, 1, SEQ, HB)),
         ("conv_sample", (1, 1, CW - 1, CONV)), ("gdn_sample", (1, 1, HA, P, P)),
         ("k_sample", (1, 1, DEC, HB, DHB)), ("v_sample", (1, 1, DEC, HB, DHB)), ("logf_sample", (1, 1, DEC, HB))]


def kernel(**inputs):
    import numpy as _np
    import concourse.bacc as _bacc
    from concourse.bass_utils import run_bass_kernel_spmd as _run

    nc = _bacc.Bacc("TRN2", target_bir_lowering=False, num_devices=1)
    arrays, t, out = {}, {}, {}
    for name in _INS:
        a = _np.ascontiguousarray(inputs[name])
        arrays[name] = a
        t[name] = nc.dram_tensor(name, a.shape, F32, kind="ExternalInput").ap()
    t["peer_u"] = t["peer_u"].rearrange("a e d -> (a e) d")
    t["peer_v"] = t["peer_v"].rearrange("a e d -> (a e) d")
    for name, shape in _OUTS:
        out[name] = nc.dram_tensor("out_" + name, shape, F32, kind="ExternalOutput").ap()
    build(nc, t, out)
    r = _run(nc, [arrays], core_ids=[0])
    return tuple(r.results[0]["out_" + name] for name, _ in _OUTS)
```

```python
from contextlib import ExitStack

import concourse.bass as bass
from concourse import mybir

F32 = mybir.dt.float32
U32 = mybir.dt.uint32
ALU = mybir.AluOpType
ACT = mybir.ActivationFunctionType
AX = mybir.AxisListType

P = 128
D = 1024
DK = D // P
SEQ, DEC, PAST = 1024, 64, 128
TILES = SEQ // P
HA, HB, DHB = 4, 8, 64
CONV = 3 * HA * P
CB = CONV // P
CW = 4
COL_BA = CONV
COL_G = COL_BA + 2 * HA
COL_Q = COL_G + HA * P
COL_K = COL_Q + HB * DHB
COL_V = COL_K + HB * DHB
COL_F = COL_V + HB * DHB
COLS = COL_F + HB
HP, KEYS, TOP = 8, 128, 16
EXPERTS = KEYS * KEYS
PICKS = HP * TOP
PLE = 256
EPS = 1e-6
NEG = -1e30
LEVELS = 7

WCOLS = 264
WRING = 3
RING = 8
AHEAD = 3
DIAGS = 4
PER_SLOT = 2
HEAD_SLOTS = TOP // PER_SLOT
LAG = HEAD_SLOTS + 1

TAIL_PIECES = {f"gate{j}": ("gate", 256 * j, 256) for j in range(4)}
TAIL_PIECES.update({f"proj{g}": ("proj", 512 * g, 512) for g in range(2)})
IN_PIECES = {f"conv_in{j}": ("conv", 256 * j, 256) for j in range(6)}
IN_PIECES.update(ba_g=("ba_g", COL_BA, 264), g=("g", COL_BA + 264, 256))
IN_PIECES.update({f"fox_q{j}": ("fox_q", COL_Q + 256 * j, 256) for j in range(2)})
IN_PIECES.update({f"fox_k{j}": ("fox_k", COL_K + 256 * j, 256) for j in range(2)})
IN_PIECES.update(fox_v0=("fox_v", COL_V, 256), fox_v1=("fox_v_f", COL_V + 256, 264))
PIECES = {**TAIL_PIECES, **IN_PIECES}
PIECES.update({f"out{j}": ("out", 256 * j, 256) for j in range(4)})
PIECES.update({f"wq{j}": ("wq", 256 * j, 256) for j in range(HP)})
FIRST_PIECES = ("conv_in0", "conv_in1", "conv_in2")
TAIL_STAGES = {"tail_norm", "tail_fin", *TAIL_PIECES}

SIGNALS = """
x_loaded prefix_loaded p_loaded past_loaded const_loaded stored
rms_mix a_ready a_tr aT_ready conv_in silu_go c_silu c_tr ctok_v ss_gdn rms_gdn qkb_ready qkb_tr qT_out kbT_out
y_gate e_gate dec_mm dec_exp kk_mm mt_ready inv_ct x_mm x_out d_mm t_out
state_mm r_ready qs_out u_mm u_out o_mm s_ready ssn_gdn rmsn_gdn oA_ready
lf_ready c_mm aux_ready cm_iota k_tr kT_done past_k_tr past_kT
s_mm s_max p_exp p_tr pt_out o_fox ss_fox rms_fox oB_ready mix_tr mixT_ready h1_ready
rms_ffn xn_ready xn_tr xnT_ready sc_mm sc_out eq2_ready eq2_times top_v gate_e gate_done
h2_ready rms_ple t_ready t_tr tT_ready pT_tr pT_ready h3_ready rms_fin y_ready y_stored
proj_done first_loaded out_even out_odd dve_step act_step pool_step
w_gelu w_ready diag_ready sum_ready folded x_twice setup_pe setup_ev setup_pool halo_done lf_past_ready
""".split()


def on_tensor(k):
    slot = k // PER_SLOT + LAG
    if 23 <= slot < 43:
        return k % 4 == 0
    if 46 <= slot < 50:
        return False
    if 53 <= slot < 65:
        return k % 4 != 3
    return k % 2 == 0


class Schedule:
    def __init__(self, picks, on_tensor):
        self.picks = picks
        self.slots = picks // PER_SLOT + LAG
        self.order = []
        for s in range(self.slots):
            own = []
            for j in range(PER_SLOT):
                if s < self.slots - LAG:
                    own.append(("u", PER_SLOT * s + j))
                if s >= LAG:
                    own.append(("v", PER_SLOT * (s - LAG) + j))
            self.order.append(own)
        self.flat = [e for own in self.order for e in own]
        self.number = {e: n for n, e in enumerate(self.flat)}
        self.tensor_picks = [k for k in range(picks) if on_tensor(k)]
        self.tensor = {k: m for m, k in enumerate(self.tensor_picks)}
        assert 2 * picks % RING == 0


FULL = Schedule(PICKS, on_tensor)
FOLDED = Schedule(PICKS // 2, lambda k: k % 2 == 0)


def build(nc, t, out):
    ctx = ExitStack()
    with ctx:
        def sb(name, shape, dt=F32):
            return ctx.enter_context(nc.sbuf_tensor(name, shape, dt))

        ident = sb("ident", [P, P])
        tri_le = sb("tri_le", [P, P])
        tri_gt = sb("tri_gt", [P, P])
        ones = sb("ones", [P, P])
        level_mask = sb("level_mask", [P, LEVELS, P])
        keysT = sb("keysT", [P, 2, KEYS])
        g_ffn = sb("g_ffn", [P, D])
        g_fin = sb("g_fin", [P, D])
        g_mix = sb("g_mix", [P, DK])
        g_ple = sb("g_ple", [P, DK])
        taps = sb("taps", [P, CW, CB])
        g_gdn = sb("g_gdn", [P, P])
        g_fox = sb("g_fox", [P, DHB])
        bias12 = sb("bias12", [P, HA + HB])
        neg_a = sb("neg_a", [P, HA])
        iota16 = sb("iota16", [P, TOP])
        pos = sb("pos", [P, 1])
        eps = sb("eps", [P, 1])
        valid = sb("valid", [P, 1])
        sel = sb("sel", [P, HB])
        x = sb("x", [P, D])
        an = sb("an", [P, D])
        tmp = an
        aT = sb("aT", [P, DK, P])
        zT = sb("zT", [P, CB, CW - 1 + P])
        cT = sb("cT", [P, CB, P])
        ctok = sb("ctok", [P, CB, P])
        state = sb("state", [P, HA, P])
        zg = sb("zg", [P, HA * P])
        zba = sb("zba", [P, 2 * HA])
        zf = sb("zf", [P, HB])
        kst = sb("kst", [P, HB * DHB])
        fqT = sb("fqT", [P, HB, P])
        kTc = sb("kTc", [P, HB // 2, SEQ])
        vc = sb("vc", [P, TILES, HB * DHB])
        aux = sb("aux", [P, SEQ])
        y12 = sb("y12", [P, 12])
        e12 = sb("e12", [P, 12])
        l12 = sb("l12", [P, 12])
        beta = sb("beta", [P, HA])
        bex = sb("bex", [P, HA])
        la = sb("la", [P, HA])
        logf = sb("logf", [P, HB])
        lf40 = sb("lf40", [P, P])
        c40 = sb("c40", [P, P])
        carry = sb("carry", [P, 1])
        ge = sb("ge", [P, 12])
        neg_eg = sb("neg_eg", [P, HA])
        st = sb("st", [P, 16])
        fst = sb("fst", [P, 4])
        st2 = sb("st2", [P, 8])
        st4 = sb("st4", [P, HA])
        fneg = sb("fneg", [P, HB])
        fsum = sb("fsum", [P, HB])
        finv = sb("finv", [P, HB])
        si = sb("si", [P, 2 * HP, TOP], U32)
        idx_n = sb("idx_n", [P, PICKS], U32)
        gate_n = sb("gate_n", [P, PICKS])
        arena = sb("arena", [P, 38 * 256])

        def part(kb, size, **shape):
            v = arena[:, kb * 256:kb * 256 + size]
            return v.rearrange("p (a b) -> p a b", **shape) if shape else v

        dec = part(0, 512, a=HA)
        mt = part(2, 512, a=HA)
        latri = mt
        attnT = part(4, 512, a=HA)
        ct = [part(6, 512, a=HA), part(8, 512, a=HA)]
        tinv = part(10, 512, a=HA)
        ttinv = part(12, 512, a=HA)
        xx = part(14, 512, a=HA)
        kb = part(16, 512, a=HA)
        rr, uu = ct[0], ct[1]
        pbuf = [part(18, 1024), part(22, 1024)]
        pts = part(26, 1024, a=TILES)
        faux = part(30, 1024, a=HB)
        cm = part(34, 1024)
        qTp = part(0, 2048, a=2 * HP)
        sc = part(8, 2048, a=2 * HP)
        cand = part(16, 2048, a=HP)
        eq = part(24, 2048, a=HP)
        sc2 = part(32, 256)
        sif = part(33, 256, a=2 * HP)
        cd = part(34, 128, a=HP).bitcast(U32)
        cf = arena[:, 34 * 256 + 128:35 * 256].rearrange("p (a b) -> p a b", a=HP)
        eq2 = cand
        ci = part(35, 128, a=HP).bitcast(U32)
        cv = arena[:, 35 * 256 + 128:36 * 256].rearrange("p (a b) -> p a b", a=HP)
        ef = part(36, 256).rearrange("p (c a b) -> p c a b", c=2, a=HP)
        sv = part(37, 256, a=2 * HP)
        tn = part(18, 1024)
        tT = part(22, 1024, a=DK)
        sg = part(26, 1024)
        prow = part(30, PLE)
        pT = part(31, 256, a=2)
        wring = sb("wring", [P, WRING, DK * WCOLS])
        ring = sb("ring", [P, RING, D])
        diag = sb("diag", [P, DIAGS, P])
        xn_c = sb("xn_c", [P, D])
        h_c = sb("h_c", [P, D])
        idx_c = sb("idx_c", [P, PICKS], U32)
        gate_c = sb("gate_c", [P, PICKS])
        dots = sb("dots", [P, PICKS])
        wgt = sb("wgt", [P, PICKS])
        h2 = sb("h2", [P, D])
        mix = h2

        bank = [ctx.enter_context(nc.psum_tensor(f"bank{i}", [P, 512], F32)) for i in range(8)]
        YB, AB, SB, TB = bank[0:2], bank[2:4], bank[4:6], bank[6:8]

        names = SIGNALS + [f"w_loaded{r}" for r in range(WRING)] + [f"landed{r}" for r in range(RING)] + ["ahead_landed"] + [f"consumed{r}" for r in range(RING)]
        sems = [ctx.enter_context(nc.semaphore(n)) for n in names]
        S = dict(zip(names, sems))
        landed = [S[f"landed{r}"] for r in range(RING)]
        consumed = [S[f"consumed{r}"] for r in range(RING)]
        numbers = sorted(s.num for s in sems)
        assert numbers == list(range(numbers[0], numbers[-1] + 1))
        proj_out = [S["out_even"], S["out_odd"]]
        w_loaded = [S[f"w_loaded{r}"] for r in range(WRING)]

        def bcast(ap, n):
            return ap.unsqueeze(2).to_broadcast([ap.shape[0], ap.shape[1], n])

        def over(ap, n):
            return ap.unsqueeze(1).to_broadcast([ap.shape[0], n, ap.shape[1]])

        class Chain:
            def __init__(self, eng, sem):
                self.eng, self.sem, self.n = eng, sem, 0

            def __call__(self, ins):
                self.n += 1
                ins.then_inc(self.sem, 1)
                self.eng.wait_ge(self.sem, self.n)

        mats = {"gate": t["w_ple_gate"], "proj": t["w_ple_proj"], "out": t["w_out"], "wq": t["peer_wq"]}

        def load_piece(sp, n, name, loaded):
            what, c, w = PIECES[name]
            src = mats.get(what, t["w_in"])[0].rearrange("(k p) n -> p k n", p=P)
            k = src.shape[1]
            sp.dma_start(wring[:, n % WRING, 0:k * w].rearrange("p (k n) -> p k n", k=k),
                         src[:, :, c:c + w]).then_inc(loaded, 16)

        def load_first(sp, names):
            for n, name in enumerate(names):
                load_piece(sp, n, name, S["first_loaded"])

        with nc.Block() as block:
            @block.sync
            def _(sp):
                rows = lambda a, w: a.rearrange("(o d) -> o d", o=1).to_broadcast([P, w])
                loads = [
                    (g_ffn[:], rows(t["norm_ffn"][0], D)), (g_fin[:], rows(t["norm_final"], D)),
                    (g_gdn[:], rows(t["gdn_onorm"][0], P)), (g_fox[:], rows(t["fox_onorm"][0], DHB)),
                    (bias12[:, 0:HA], rows(t["dt_bias"][0], HA)), (bias12[:, HA:], rows(t["b_f"][0], HB)),
                    (neg_a[:], rows(t["a_log"][0], HA)),
                    (g_mix[:], t["norm_mix"][0].rearrange("(k p) -> p k", p=P)),
                    (g_ple[:], t["norm_ple"][0].rearrange("(k p) -> p k", p=P)),
                    (tmp[:, 0:P], t["peer_keys"][0, 0]), (tmp[:, P:2 * P], t["peer_keys"][0, 1]),
                ] + [(taps[:, j, :], t["conv_w"][0, j].rearrange("(b p) -> p b", p=P)) for j in range(CW)]
                load_first(sp, FIRST_PIECES)
                for dst, src in loads:
                    sp.dma_start(dst, src, allow_slow_non_contiguous=True).then_inc(S["const_loaded"], 16)
                sp.wait_ge(S["const_loaded"], 16 * len(loads))
                sp.wait_ge(S["first_loaded"], 16 * WRING)

            @block.gpsimd
            def _(pool):
                step = Chain(pool, S["pool_step"])
                step(pool.memset(ones[:], 1.0))
                step(pool.memset(ident[:], 0.0))
                step(pool.affine_select(out=ident[:], in_=ident[:], compare_op=ALU.not_equal, fill=1.0,
                                        base=0, pattern=[[-1, P]], channel_multiplier=1))
                step(pool.affine_select(out=tri_le[:], in_=ones[:], compare_op=ALU.is_ge, fill=0.0,
                                        base=0, pattern=[[1, P]], channel_multiplier=-1))
                step(pool.affine_select(out=tri_gt[:], in_=ones[:], compare_op=ALU.is_ge, fill=0.0,
                                        base=-1, pattern=[[-1, P]], channel_multiplier=1))
                step(pool.memset(level_mask[:], 0.0))
                for l in range(LEVELS):
                    b = 1 << l
                    n = P // (2 * b)
                    v = level_mask[:, l, :].rearrange("p (n c) -> p n c", n=n)[:, :, b:2 * b]
                    o = ones[:, 0:n * b].rearrange("p (n c) -> p n c", n=n)
                    step(pool.affine_select(out=v, in_=o, compare_op=ALU.is_ge, fill=0.0,
                                            base=0, pattern=[[-2 * b, n], [0, b]], channel_multiplier=1))
                    step(pool.affine_select(out=v, in_=v, compare_op=ALU.is_ge, fill=0.0,
                                            base=b - 1, pattern=[[2 * b, n], [0, b]], channel_multiplier=-1))
                step(pool.memset(sel[:], 0.0))
                for r in (0, 32):
                    step(pool.affine_select(out=sel[:], in_=sel[:], compare_op=ALU.not_equal, fill=1.0,
                                            base=-r, pattern=[[-1, HB]], channel_multiplier=1))
                step(pool.iota(iota16[:], pattern=[[1, TOP]], base=0, channel_multiplier=0,
                               allow_small_or_imprecise_dtypes=True))
                pool.engine_nop().then_inc(S["setup_pool"], 1)

            @block.vector
            def _(v):
                step = Chain(v, S["dve_step"])
                step(v.memset(aux[:], 0.0))
                step(v.memset(aux[32:40, :], 1.0))
                step(v.memset(lf40[:], 0.0))
                step(v.memset(carry[:], 0.0))
                step(v.memset(zT[:, :, 0:CW - 1], 0.0))
                step(v.memset(state[:], 0.0))
                step(v.memset(pos[:], 0.0))
                step(v.memset(eps[:], EPS))
                step(v.memset(fqT[:], 0.0))
                step(v.memset(valid[:], 1.0))
                step(v.memset(valid[DEC:P, :], 0.0))
                v.wait_ge(S["setup_pe"], 1)
                step(v.tensor_copy(keysT[:], SB[0][:, 0:2 * KEYS].rearrange("p (c n) -> p c n", c=2)))
                v.wait_ge(S["setup_ev"], 1)
                step(v.tensor_scalar(neg_a[:], neg_a[:], -1.0, None, ALU.mult))

            @block.scalar
            def _(act):
                act.wait_ge(S["const_loaded"], 16 * 15)
                act.activation(neg_a[:], neg_a[:], ACT.Exp).then_inc(S["setup_ev"], 1)

            @block.tensor
            def _(pe):
                pe.wait_ge(S["const_loaded"], 16 * 15)
                pe.wait_ge(S["pool_step"], 3)
                for c in range(2):
                    last = pe.transpose(SB[0][:, c * KEYS:(c + 1) * KEYS], tmp[:, c * P:(c + 1) * P], ident[:])
                last.then_inc(S["setup_pe"], 1)
        nc.all_engine_barrier(sems_to_clear=range(numbers[0], numbers[-1] + 1))

        def body(front=None, peer=None, tail=None, blocks=TILES, plan=None,
                 first=FIRST_PIECES, upcoming=FIRST_PIECES, sched=FULL):
            plan = plan or PLAN[:sched.slots]
            order = dict.fromkeys(name for slot in plan for name in slot if name in PIECES)
            names = [name for name in order if (tail if name in TAIL_PIECES else front)]
            assert names[:WRING] == list(first)[:WRING]
            number = {name: n for n, name in enumerate(names)}
            keys = blocks * P
            n_halves = (blocks + 3) // 4
            halves = [range(4 * g, min(4 * g + 4, blocks)) for g in range(n_halves)]
            if front:
                f_i, f_rows, f_blk, f_sample = front
                f_src = t["x_sample"][0] if f_sample else t["x_prompt"][0][bass.ds(f_i * P, P), :]
                f_key = bass.ds(f_blk * P, P)
            if tail:
                t_i, t_rows, t_sample = tail
                t_p = t["p_sample"][0, 0] if t_sample else t["p_prompt"][0, 0][bass.ds(t_i * P, P), :]
                t_y = out["y_sample"][0] if t_sample else out["y_prompt"][0][bass.ds(t_i * P, P), :]
            n_store = [0]

            def four(b):
                return b[:].rearrange("p (a c) -> p a c", a=4)

            def wait_out(eng, *names):
                for name in names:
                    n = number[name]
                    eng.wait_ge(proj_out[n % 2], n // 2 + 1)

            def wait_landed(eng, n):
                before = 1 if n % RING < AHEAD else 0
                if n >= AHEAD:
                    eng.wait_ge(landed[n % RING], 16 * (n // RING + 1 - before))

            def wait_used(eng, kind, k):
                n = sched.number[kind, k]
                eng.wait_ge(consumed[n % RING], n // RING + 1)

            def walker(stages):
                begun = {}

                def next_part(name):
                    if name not in stages or not (tail if name in TAIL_STAGES else front):
                        return
                    if name not in begun:
                        begun[name] = stages[name]() or iter(())
                    next(begun[name], None)
                return next_part

            with nc.Block() as block:
                @block.sync
                def _(sp):
                    if tail:
                        sp.dma_start(prow[0:t_rows, :], t_p).then_inc(S["p_loaded"], 16)
                    if front:
                        sp.dma_start(x[0:f_rows, :], f_src).then_inc(S["x_loaded"], 16)
                        if f_sample:
                            for j in range(CW - 1):
                                sp.dma_start(out["conv_prompt"][0, 0, j].rearrange("(b p) -> p b", p=P), zT[:, :, j],
                                             allow_slow_non_contiguous=True).then_inc(S["stored"], 16)
                            sp.dma_start(out["gdn_prompt"][0, 0].rearrange("h k v -> k h v"),
                                         state[:]).then_inc(S["stored"], 16)
                            sp.wait_ge(S["stored"], 16 * CW)
                            n_store[0] = CW
                            for j in range(CW - 1):
                                sp.dma_start(zT[:, :, j], t["cache_conv"][0, 0, j].rearrange("(b p) -> p b", p=P),
                                             allow_slow_non_contiguous=True).then_inc(S["prefix_loaded"], 16)
                            sp.dma_start(state[:], t["state_gdn"][0, 0].rearrange("h k v -> k h v"))\
                              .then_inc(S["prefix_loaded"], 16)
                            sp.dma_start(kst[:], t["cache_fox_k"][0, 0].rearrange("t h d -> t (h d)"))\
                              .then_inc(S["past_loaded"], 16)
                            sp.dma_start(vc[:, 0, :], t["cache_fox_v"][0, 0].rearrange("t h d -> t (h d)"))\
                              .then_inc(S["past_loaded"], 16)
                            sp.dma_start(logf[:], t["cache_fox_logf"][0, 0]).then_inc(S["past_loaded"], 16)
                    for n in range(WRING, len(names)):
                        sp.wait_ge(S["proj_done"], n - WRING + 1)
                        load_piece(sp, n, names[n], w_loaded[n % WRING])
                    if front:
                        o = "_sample" if f_sample else "_prompt"
                        rows = slice(0, DEC) if f_sample else bass.ds(f_i * P, P)
                        sp.wait_ge(S["kT_done"], 1)
                        sp.dma_start(out["k" + o][0, 0].rearrange("t h d -> t (h d)")[rows, :],
                                     kst[0:f_rows, :]).then_inc(S["stored"], 16)
                        wait_out(sp, "fox_v0", "fox_v1")
                        vrow = vc[0:f_rows, f_blk, :] if isinstance(f_blk, int) else \
                            vc[:, bass.ds(f_blk, 1), :].rearrange("p a b -> p (a b)")
                        sp.dma_start(out["v" + o][0, 0].rearrange("t h d -> t (h d)")[rows, :],
                                     vrow).then_inc(S["stored"], 16)
                        sp.wait_ge(S["lf_ready"], 1)
                        sp.dma_start(out["logf" + o][0, 0][rows, :], logf[0:f_rows, :]).then_inc(S["stored"], 16)
                        n_store[0] += 3
                        if f_sample:
                            sp.wait_ge(S["s_ready"], 1)
                            sp.dma_start(out["gdn_sample"][0, 0].rearrange("h k v -> k h v"),
                                         state[:]).then_inc(S["stored"], 16)
                            for j in range(CW - 1):
                                sp.dma_start(out["conv_sample"][0, 0, j].rearrange("(b p) -> p b", p=P),
                                             zT[:, :, DEC + j], allow_slow_non_contiguous=True)\
                                  .then_inc(S["stored"], 16)
                            n_store[0] += CW
                    if upcoming:
                        sp.wait_ge(S["proj_done"], len(names))
                        load_first(sp, upcoming)
                        sp.wait_ge(S["first_loaded"], 16 * WRING)
                    if tail:
                        sp.wait_ge(S["y_stored"], 16)
                    if n_store[0]:
                        sp.wait_ge(S["stored"], 16 * n_store[0])

                @block.gpsimd
                def _(pool):
                    def gather(n, kind, k, rows, idx, done):
                        pool.indirect_dma_start(
                            out=ring[0:rows, n % RING, :], out_offset=None, in_=t["peer_" + kind],
                            in_offset=bass.IndirectOffsetOnAxis(ap=idx[0:rows, k:k + 1], axis=0),
                        ).then_inc(done, 16)

                    def inv_masks(l):
                        if l == 0:
                            pool.wait_ge(S["mt_ready"], 1)
                        if l >= 2:
                            pool.wait_ge(S["t_out"], l - 1)
                        pool.tensor_tensor(ct[l % 2], mt, over(level_mask[:, l, :], HA), ALU.mult)\
                            .then_inc(S["inv_ct"], 1)

                    def fox_keys():
                        pool.iota(cm[:, 0:keys], pattern=[[1, keys]], base=0, channel_multiplier=-1,
                                  allow_small_or_imprecise_dtypes=True).then_inc(S["cm_iota"], 1)

                    def pick_gate():
                        yield
                        yield
                        yield
                        yield
                        pool.wait_ge(S["eq2_ready"], 1)
                        for h in range(HP):
                            e3 = eq2[:, h, :].rearrange("p (a b) -> p a b", a=TOP)
                            last = pool.tensor_tensor(e3, e3, over(sif[:, 2 * h + 1, :], TOP), ALU.mult)
                        last.then_inc(S["eq2_times"], 1)

                    stages = dict(fox_keys=fox_keys, pick_gate=pick_gate)
                    stages.update({f"inv{l}": (lambda l=l: inv_masks(l)) for l in range(LEVELS)})
                    next_part = walker(stages)
                    if front and not peer:
                        pool.memset(kTc[:, :, P:], 0.0)
                        pool.memset(vc[:, 1:, :], 0.0)
                    for s in range(len(plan)):
                        for name in plan[s]:
                            next_part(name)
                        if peer:
                            for kind, k in sched.order[s]:
                                n = sched.number[kind, k]
                                if n >= AHEAD:
                                    if n >= RING:
                                        pool.wait_ge(consumed[n % RING], n // RING)
                                    gather(n, kind, k, peer, idx_c, landed[n % RING])
                    if front:
                        pool.wait_ge(S["gate_done"], 1)
                        for n, (kind, k) in enumerate(FULL.flat[:AHEAD]):
                            if peer:
                                pool.wait_ge(consumed[n], 2 * sched.picks // RING)
                            gather(n, kind, k, P, idx_n, S["ahead_landed"])
                        pool.wait_ge(S["ahead_landed"], 16 * AHEAD)
                    if peer:
                        for n in range(2 * sched.picks - RING, 2 * sched.picks):
                            pool.wait_ge(consumed[n % RING], n // RING + 1)
                    if peer or front:
                        pool.dma_reset(range(landed[0].num, S["ahead_landed"].num + 1))

                @block.scalar
                def _(act):
                    step = Chain(act, S["act_step"])

                    def rms(src, rows, c, junk, done):
                        step(act.activation(junk[0:rows, :], src, ACT.Square, accum_out=st[0:rows, c + 1:c + 2]))
                        act.activation(st[0:rows, c:c + 1], st[0:rows, c + 1:c + 2], ACT.Sqrt, bias=eps[0:rows, :],
                                       scale=1.0 / D).then_inc(done, 1)

                    def evac(name, pairs, func=ACT.Copy, scale=1.0):
                        n = number[name]
                        act.wait_ge(S["proj_done"], n + 1)
                        for dst, src in pairs:
                            last = act.activation(dst, src, func, scale=scale)
                        last.then_inc(proj_out[n % 2], 1)

                    def tail_norm():
                        rms(h2[0:t_rows, :], t_rows, 8, tn, S["rms_ple"])

                    def tail_gate(j):
                        name = f"gate{j}"
                        evac(name, [(sg[0:t_rows, 256 * j:256 * j + 256], AB[number[name] % 2][0:t_rows, 0:256])],
                             ACT.Sigmoid)

                    def tail_fin():
                        act.wait_ge(S["h3_ready"], 2)
                        rms(h2[0:t_rows, :], t_rows, 12, tn, S["rms_fin"])
                        yield
                        yield
                        act.wait_ge(S["y_ready"], 1)
                        act.dma_start(t_y, tn[0:t_rows, :]).then_inc(S["y_stored"], 16)

                    def norm_mix():
                        act.wait_ge(S["x_loaded"], 16)
                        if f_sample:
                            act.wait_ge(S["halo_done"], 1)
                        rms(x[:], P, 0, tmp, S["rms_mix"])

                    def in_proj(name):
                        n = number[name]
                        what, c, w = PIECES[name]
                        b = AB[n % 2]
                        if what == "conv":
                            if name == "conv_in0" and f_sample:
                                act.wait_ge(S["prefix_loaded"], 16 * CW)
                            evac(name, [(zT[:, c // P:c // P + 2, CW - 1:],
                                         b[:, 0:256].rearrange("p (a c) -> p a c", a=2))])
                        elif what == "ba_g":
                            evac(name, [(zba[:], b[:, 0:8]), (zg[:, 0:256], b[:, 8:264])])
                        elif what == "g":
                            evac(name, [(zg[:, 256:512], b[:, 0:256])])
                        elif what == "fox_q":
                            m = (c - COL_Q) // P
                            heads = fqT[:].rearrange("p (m o) c -> p m o c", o=2)
                            b3 = b[:, 0:256].rearrange("p (a c) -> p a c", a=2)
                            evac(name, [(heads[DHB * o:DHB * o + DHB, m:m + 2, o, :], b3[DHB * o:DHB * o + DHB])
                                        for o in range(2)], scale=DHB ** -0.5)
                        elif what == "fox_k":
                            if f_sample:
                                act.wait_ge(S["past_k_tr"], 1)
                            evac(name, [(kst[:, c - COL_K:c - COL_K + 256], b[:, 0:256])])
                        else:
                            m = c - COL_V
                            dst = vc[:, bass.ds(f_blk, 1), m:m + 256].rearrange("p a b -> p (a b)")
                            if what == "fox_v_f":
                                evac(name, [(dst, b[:, 0:256]), (zf[:], b[:, 256:264])])
                            else:
                                evac(name, [(dst, b[:, 0:256])])

                    def conv(g):
                        act.wait_ge(S["conv_in"], g + 1)
                        act.activation(cT[:, 4 * g:4 * g + 4, :], cT[:, 4 * g:4 * g + 4, :], ACT.Silu)\
                            .then_inc(S["c_silu"], 1)
                        yield
                        if g == 2:
                            act.wait_ge(S["c_tr"], 3)
                            act.activation(ctok[:, 8:12, :], four(TB[0]), ACT.Copy).then_inc(S["ctok_v"], 1)

                    def silu_g():
                        wait_out(act, "ba_g", "g")
                        act.activation(zg[:], zg[:], ACT.Silu).then_inc(S["silu_go"], 1)

                    def gates():
                        act.wait_ge(S["y_gate"], 1)
                        act.activation(bex[:], zba[:, 0:HA], ACT.Exp, scale=-1.0)
                        step(act.activation(e12[:], e12[:], ACT.Exp, scale=-1.0))
                        act.activation(l12[:], e12[:], ACT.Ln, bias=1.0).then_inc(S["e_gate"], 1)

                    def gdn():
                        act.wait_ge(S["ss_gdn"], 1)
                        act.activation(st2[:], st2[:], ACT.Sqrt, bias=eps[:]).then_inc(S["rms_gdn"], 1)
                        yield
                        yield
                        act.wait_ge(S["qkb_tr"], 1)
                        act.activation(cT[:, 0:4, :], four(SB[0]), ACT.Copy)
                        act.activation(cT[:, 4:8, :], four(SB[1]), ACT.Copy).then_inc(S["qT_out"], 1)
                        act.wait_ge(S["dec_mm"], 1)
                        act.activation(dec, four(TB[0]), ACT.Exp).then_inc(S["dec_exp"], 1)
                        yield
                        act.wait_ge(S["dec_mm"], 2)
                        act.activation(ge[:], TB[1][:, 0:12], ACT.Exp).then_inc(S["dec_exp"], 1)

                    def inverse(l):
                        if l == 0:
                            return
                        act.wait_ge(S["x_mm"], l + 1)
                        if l >= 2:
                            act.wait_ge(S["d_mm"], l - 1)
                        act.activation(xx, four(AB[0]), ACT.Copy).then_inc(S["x_out"], 1)

                    def state_u():
                        yield
                        yield
                        act.wait_ge(S["u_mm"], 1)
                        act.activation(uu, four(AB[0]), ACT.Copy).then_inc(S["u_out"], 1)

                    def gdn_norm():
                        act.wait_ge(S["ssn_gdn"], 1)
                        act.activation(st4[:], st4[:], ACT.Sqrt, bias=eps[:], scale=1.0 / P)\
                            .then_inc(S["rmsn_gdn"], 1)

                    def fox_past():
                        if not f_sample:
                            return
                        yield
                        act.wait_ge(S["past_k_tr"], 1)
                        act.activation(kTc[:, :, 0:P], four(TB[0]), ACT.Copy).then_inc(S["past_kT"], 1)

                    def fox_keys():
                        act.wait_ge(S["k_tr"], 1)
                        act.activation(kTc[:, :, f_key], four(TB[0]), ACT.Copy).then_inc(S["kT_done"], 1)

                    def fox_s(h):
                        yield
                        act.wait_ge(S["s_max"], h + 1)
                        act.activation(pbuf[h % 2][:, 0:keys], pbuf[h % 2][:, 0:keys], ACT.Exp,
                                       bias=fneg[:, h:h + 1], accum_out=fsum[:, h:h + 1]).then_inc(S["p_exp"], 1)

                    def fox_o(h):
                        if h >= 1:
                            act.wait_ge(S["o_fox"], h)
                        for g, own in enumerate(halves):
                            act.wait_ge(S["p_tr"], n_halves * h + g + 1)
                            act.activation(pts[:, 4 * g:4 * g + len(own), :], four(TB[0])[:, 0:len(own)], ACT.Copy)\
                                .then_inc(S["pt_out"], 1)
                            yield

                    def fox_norm():
                        act.wait_ge(S["ss_fox"], 1)
                        act.activation(st2[:], st2[:], ACT.Sqrt, bias=eps[:], scale=1.0 / DHB)\
                            .then_inc(S["rms_fox"], 1)

                    def norm_ffn():
                        act.wait_ge(S["h1_ready"], 4)
                        if f_sample:
                            act.dma_start(x[DEC:P, :], x[0:DEC, :]).then_inc(S["x_twice"], 16)
                            act.wait_ge(S["x_twice"], 16)
                        rms(x[:], P, 4, tmp, S["rms_ffn"])

                    def wq(j):
                        name = f"wq{j}"
                        evac(name, [(qTp[:, 2 * j:2 * j + 2, :],
                                     AB[number[name] % 2][:, 0:256].rearrange("p (a c) -> p a c", a=2))])

                    def scores(g):
                        act.wait_ge(S["sc_mm"], g + 1)
                        act.activation(sc[:, 4 * g:4 * g + 4, :], four((SB + TB)[g]), ACT.Copy)\
                            .then_inc(S["sc_out"], 1)

                    def pick_gate():
                        act.wait_ge(S["top_v"], 1)
                        act.activation(gate_n[:], gate_n[:], ACT.Exp).then_inc(S["gate_e"], 1)

                    def hand_rows():
                        if peer:
                            wait_used(act, "u", sched.picks - 1)
                        act.wait_ge(S["xn_ready"], 1)
                        act.activation(xn_c[:], an[:], ACT.Copy)

                    stages = dict(tail_norm=tail_norm, tail_fin=tail_fin, norm_mix=norm_mix, silu_g=silu_g, gates=gates,
                                  gdn=gdn, state=state_u, gdn_norm=gdn_norm, fox_past=fox_past, fox_keys=fox_keys,
                                  fox_norm=fox_norm, norm_ffn=norm_ffn, pick_gate=pick_gate, hand_rows=hand_rows)
                    stages.update({f"gate{j}": (lambda j=j: tail_gate(j)) for j in range(4)})
                    stages.update({name: (lambda name=name: in_proj(name)) for name in IN_PIECES})
                    stages.update({f"conv{g}": (lambda g=g: conv(g)) for g in range(3)})
                    stages.update({f"inv{l}": (lambda l=l: inverse(l)) for l in range(LEVELS)})
                    stages.update({f"fox_s{h}": (lambda h=h: fox_s(h)) for h in range(HB)})
                    stages.update({f"fox_o{h}": (lambda h=h: fox_o(h)) for h in range(HB)})
                    stages.update({f"wq{j}": (lambda j=j: wq(j)) for j in range(HP)})
                    stages.update({f"scores{g}": (lambda g=g: scores(g)) for g in range(4)})
                    next_part = walker(stages)
                    for s in range(len(plan)):
                        if peer:
                            for k in [k for kind, k in sched.order[s] if kind == "v" and k in sched.tensor]:
                                m = sched.tensor[k]
                                act.wait_ge(S["w_ready"], k // TOP + 1)
                                if m >= DIAGS:
                                    wait_used(act, "v", sched.tensor_picks[m - DIAGS])
                                act.activation(diag[0:peer, m % DIAGS, 0:peer], ident[0:peer, 0:peer], ACT.Copy,
                                               scale=wgt[0:peer, k:k + 1]).then_inc(S["diag_ready"], 1)
                            if s and s % HEAD_SLOTS == 0 and s // HEAD_SLOTS <= sched.picks // TOP:
                                h = s // HEAD_SLOTS - 1
                                wait_used(act, "u", TOP * h + TOP - 1)
                                act.activation(wgt[0:peer, TOP * h:TOP * h + TOP],
                                               dots[0:peer, TOP * h:TOP * h + TOP], ACT.Gelu)\
                                    .then_inc(S["w_gelu"], 1)
                        for name in plan[s]:
                            next_part(name)
                    if front:
                        if peer:
                            act.wait_ge(S["h2_ready"], 1)
                        rows = slice(0, f_rows)
                        act.activation(h_c[rows, :], x[rows, :], ACT.Copy)

                @block.tensor
                def _(pe):
                    def transpose8(src, rows, banks, done):
                        for k in range(DK):
                            last = pe.transpose(banks[k // 4][:, (k % 4) * P:(k % 4) * P + rows],
                                                src[0:rows, k * P:(k + 1) * P], ident[0:rows, 0:rows])
                        last.then_inc(done, 1)

                    def transpose4(bank_, src, m0):
                        for m in range(4):
                            last = pe.transpose(bank_[:, m * P:(m + 1) * P], src[:, m0 + m, :], ident[:])
                        return last

                    def project(name, actT, rows, turned=False):
                        n = number[name]
                        what, c, w = PIECES[name]
                        k8 = 2 if what == "proj" else DK
                        wt = wring[:, n % WRING, 0:k8 * w].rearrange("p (k n) -> p k n", k=k8)
                        if n >= WRING:
                            pe.wait_ge(w_loaded[n % WRING], 16 * (n // WRING))
                        if n >= 2:
                            pe.wait_ge(proj_out[n % 2], n // 2)
                        b = AB[n % 2]
                        if turned:
                            for m in range(w // P):
                                for k in range(DK):
                                    last = pe.matmul(b[:, m * P:m * P + rows], wt[:, k, m * P:(m + 1) * P],
                                                     actT[:, k, 0:rows], start=(k == 0), stop=(k == DK - 1))
                        else:
                            for k in range(k8):
                                last = pe.matmul(b[0:rows, 0:w], actT[:, k, 0:rows], wt[:, k, :],
                                                 start=(k == 0), stop=(k == k8 - 1))
                        last.then_inc(S["proj_done"], 1)

                    def tail_norm():
                        pe.wait_ge(S["p_loaded"], 16)
                        for k in range(2):
                            last = pe.transpose(TB[0][:, k * P:k * P + t_rows], prow[0:t_rows, k * P:(k + 1) * P],
                                                ident[0:t_rows, 0:t_rows])
                        last.then_inc(S["pT_tr"], 1)
                        yield
                        pe.wait_ge(S["t_ready"], 1)
                        transpose8(tn, t_rows, SB, S["t_tr"])

                    def tail_gate(j):
                        pe.wait_ge(S["tT_ready"], 2)
                        project(f"gate{j}", tT, t_rows)

                    def tail_proj(g):
                        pe.wait_ge(S["pT_ready"], 1)
                        project(f"proj{g}", pT, t_rows)

                    def norm_mix():
                        yield
                        pe.wait_ge(S["a_ready"], 1)
                        transpose8(an, P, AB, S["a_tr"])

                    def in_proj(name):
                        if name == "conv_in0":
                            pe.wait_ge(S["aT_ready"], 2)
                        project(name, aT, P, PIECES[name][0] in ("conv", "fox_q"))

                    def conv(g):
                        yield
                        pe.wait_ge(S["c_silu"], g + 1)
                        if g == 0 and tail:
                            pe.wait_ge(S["tT_ready"], 2)
                            pe.wait_ge(S["pT_ready"], 1)
                        if g == 2 and f_sample:
                            pe.wait_ge(S["past_kT"], 1)
                        transpose4((SB + TB)[g], cT, 4 * g).then_inc(S["c_tr"], 1)

                    def gdn():
                        yield
                        yield
                        pe.wait_ge(S["qkb_ready"], 1)
                        pe.wait_ge(S["ctok_v"], 1)
                        transpose4(SB[0], ctok, 0)
                        transpose4(SB[1], ctok, 4)
                        if f_sample:
                            pe.wait_ge(S["aux_ready"], 1)
                        transpose4(TB[1], kb, 0).then_inc(S["qkb_tr"], 1)
                        for h in range(HA):
                            last = pe.matmul(TB[0][:, h * P:(h + 1) * P], latri[:, h, :], tri_le[:],
                                             start=True, stop=True)
                        last.then_inc(S["dec_mm"], 1)
                        yield
                        pe.wait_ge(S["kbT_out"], 1)
                        for m, lhs in enumerate((tri_le, tri_gt, ones)):
                            last = pe.matmul(TB[1][:, 4 * m:4 * m + 4], lhs[:], la[:], start=True, stop=True)
                        last.then_inc(S["dec_mm"], 1)
                        pe.wait_ge(S["qT_out"], 1)
                        for h in range(HA):
                            pe.matmul(SB[0][:, h * P:(h + 1) * P], cT[:, 4 + h, :], cT[:, 8 + h, :], start=True, stop=True)
                        for h in range(HA):
                            last = pe.matmul(SB[1][:, h * P:(h + 1) * P], cT[:, 4 + h, :], cT[:, h, :],
                                             start=True, stop=True)
                        last.then_inc(S["kk_mm"], 1)

                    def inverse(l):
                        pe.wait_ge(S["inv_ct"], l + 1)
                        if l == 0:
                            wait_out(pe, *[name for name in names if name in IN_PIECES][-2:])
                            transpose4(AB[0], ct[0], 0).then_inc(S["x_mm"], 1)
                            return
                        pe.wait_ge(S["t_out"], l)
                        for h in range(HA):
                            last = pe.matmul(AB[0][:, h * P:(h + 1) * P], ct[l % 2][:, h, :], tinv[:, h, :],
                                             start=True, stop=True)
                        last.then_inc(S["x_mm"], 1)
                        yield
                        pe.wait_ge(S["x_out"], l)
                        if l < LEVELS - 1:
                            for h in range(HA):
                                pe.matmul(AB[0][:, h * P:(h + 1) * P], ttinv[:, h, :], xx[:, h, :],
                                          start=True, stop=True)
                        for h in range(HA):
                            last = pe.matmul(AB[1][:, h * P:(h + 1) * P], xx[:, h, :], ttinv[:, h, :],
                                             start=True, stop=True)
                        last.then_inc(S["d_mm"], 1)

                    def state_u():
                        if f_sample:
                            pe.wait_ge(S["prefix_loaded"], 16 * CW)
                        pe.wait_ge(S["t_out"], LEVELS)
                        for h in range(HA):
                            pe.matmul(AB[0][:, h * P:(h + 1) * P], cT[:, 4 + h, :], state[:, h, :], start=True, stop=True)
                        for h in range(HA):
                            last = pe.matmul(AB[1][:, h * P:(h + 1) * P], cT[:, h, :], state[:, h, :],
                                             start=True, stop=True)
                        last.then_inc(S["state_mm"], 1)
                        yield
                        yield
                        pe.wait_ge(S["r_ready"], 1)
                        for h in range(HA):
                            last = pe.matmul(AB[0][:, h * P:(h + 1) * P], ttinv[:, h, :], rr[:, h, :],
                                             start=True, stop=True)
                        last.then_inc(S["u_mm"], 1)
                        yield
                        pe.wait_ge(S["u_out"], 1)
                        pe.wait_ge(S["qs_out"], 1)
                        for h in range(HA):
                            pe.matmul(AB[0][:, h * P:(h + 1) * P], attnT[:, h, :], uu[:, h, :], start=True, stop=True)
                        for h in range(HA):
                            last = pe.matmul(AB[1][:, h * P:(h + 1) * P], kb[:, h, :], uu[:, h, :],
                                             start=True, stop=True)
                        last.then_inc(S["o_mm"], 1)

                    def fox_past():
                        if not f_sample:
                            return
                        yield
                        pe.wait_ge(S["lf_past_ready"], 1)
                        pe.matmul(TB[1][:, 0:P], lf40[:], tri_le[:], start=True, stop=True).then_inc(S["c_mm"], 1)
                        pe.wait_ge(S["past_loaded"], 48)
                        if tail:
                            pe.wait_ge(S["pT_ready"], 1)
                        for m in range(4):
                            last = pe.transpose(TB[0][:, m * P:(m + 1) * P], kst[:, m * P:(m + 1) * P], ident[:])
                        last.then_inc(S["past_k_tr"], 1)

                    def fox_keys():
                        wait_out(pe, "fox_k0", "fox_k1")
                        pe.wait_ge(S["dec_exp"], 2)
                        for m in range(4):
                            last = pe.transpose(TB[0][:, m * P:(m + 1) * P], kst[:, m * P:(m + 1) * P], ident[:])
                        last.then_inc(S["k_tr"], 1)
                        pe.wait_ge(S["lf_ready"], 1)
                        pe.matmul(TB[1][:, 0:P], lf40[:], tri_le[:], start=True, stop=True).then_inc(S["c_mm"], 1)

                    def fox_s(h):
                        if h == 0:
                            wait_out(pe, "fox_q0", "fox_q1")
                            pe.wait_ge(S["kT_done"], 1)
                            pe.wait_ge(S["aux_ready"], 2 if f_sample else 1)
                            pe.wait_ge(S["mt_ready"], 1)
                        else:
                            pe.wait_ge(S["s_max"], h)
                        for g, own in enumerate(halves):
                            c = slice(P * own[0], P * own[-1] + P)
                            w = P * len(own)
                            pe.matmul(SB[g][:, 0:w], fqT[:, h, :], kTc[:, h // 2, c], start=True, stop=False)
                            last = pe.matmul(SB[g][:, 0:w], faux[:, h, :], aux[:, c], start=False, stop=True)
                        last.then_inc(S["s_mm"], 1)

                    def fox_o(h):
                        pe.wait_ge(S["p_exp"], h + 1)
                        for g, own in enumerate(halves):
                            n = n_halves * h + g
                            if n >= 1:
                                pe.wait_ge(S["pt_out"], n)
                            for m in own:
                                last = pe.transpose(TB[0][:, (m % 4) * P:(m % 4 + 1) * P],
                                                    pbuf[h % 2][:, m * P:(m + 1) * P], ident[:])
                            last.then_inc(S["p_tr"], 1)
                            yield
                        if n_halves == 1:
                            yield
                        pe.wait_ge(S["pt_out"], n_halves * h + n_halves)
                        if h == 0:
                            pe.wait_ge(S["aux_ready"], 2 if f_sample else 1)
                            wait_out(pe, "fox_v0", "fox_v1")
                        for m in range(blocks):
                            last = pe.matmul(TB[1][:, h * DHB:(h + 1) * DHB], pts[:, m, :],
                                             vc[:, m, h * DHB:(h + 1) * DHB], start=(m == 0), stop=(m == blocks - 1))
                        last.then_inc(S["o_fox"], 1)

                    def mix_turn():
                        pe.wait_ge(S["oA_ready"], 1)
                        pe.wait_ge(S["oB_ready"], 1)
                        transpose8(mix, P, TB, S["mix_tr"])

                    def out_proj(j):
                        if j == 0:
                            pe.wait_ge(S["mixT_ready"], 2)
                        project(f"out{j}", aT, P)

                    def norm_ffn():
                        yield
                        yield
                        pe.wait_ge(S["xn_ready"], 1)
                        transpose8(an, P, TB, S["xn_tr"])

                    def wq(j):
                        if j == 0:
                            pe.wait_ge(S["xnT_ready"], 2)
                        project(f"wq{j}", aT, P, True)

                    def scores(g):
                        wait_out(pe, f"wq{2 * g}", f"wq{2 * g + 1}")
                        for m in range(4):
                            last = pe.matmul((SB + TB)[g][:, m * P:(m + 1) * P], qTp[:, 4 * g + m, :],
                                             keysT[:, m % 2, :], start=True, stop=True)
                        last.then_inc(S["sc_mm"], 1)

                    stages = dict(tail_norm=tail_norm, norm_mix=norm_mix, gdn=gdn, state=state_u, fox_past=fox_past,
                                  fox_keys=fox_keys, mix_turn=mix_turn, norm_ffn=norm_ffn)
                    stages.update({f"gate{j}": (lambda j=j: tail_gate(j)) for j in range(4)})
                    stages.update({f"proj{g}": (lambda g=g: tail_proj(g)) for g in range(2)})
                    stages.update({name: (lambda name=name: in_proj(name)) for name in IN_PIECES})
                    stages.update({f"conv{g}": (lambda g=g: conv(g)) for g in range(3)})
                    stages.update({f"inv{l}": (lambda l=l: inverse(l)) for l in range(LEVELS)})
                    stages.update({f"fox_s{h}": (lambda h=h: fox_s(h)) for h in range(HB)})
                    stages.update({f"fox_o{h}": (lambda h=h: fox_o(h)) for h in range(HB)})
                    stages.update({f"out{j}": (lambda j=j: out_proj(j)) for j in range(4)})
                    stages.update({f"wq{j}": (lambda j=j: wq(j)) for j in range(HP)})
                    stages.update({f"scores{g}": (lambda g=g: scores(g)) for g in range(4)})
                    next_part = walker(stages)
                    for s in range(len(plan)):
                        for name in plan[s]:
                            next_part(name)
                        if peer:
                            for kind, k in sched.order[s]:
                                if kind == "v" and k in sched.tensor:
                                    n = sched.number[kind, k]
                                    r = n % RING
                                    m = sched.tensor[k]
                                    wait_landed(pe, n)
                                    pe.wait_ge(S["diag_ready"], m + 1)
                                    for g in range(2):
                                        last = pe.matmul(YB[g][0:peer, :], diag[0:peer, m % DIAGS, 0:peer],
                                                         ring[0:peer, r, 512 * g:512 * g + 512],
                                                         start=(m == 0), stop=(m == len(sched.tensor) - 1))
                                    last.then_inc(consumed[r], 1)
                    if peer and sched is FOLDED:
                        pe.wait_ge(S["sum_ready"], 1)
                        for g in range(2):
                            for half in range(2):
                                last = pe.matmul(SB[g][0:DEC, :], ident[:, DEC * half:DEC * half + DEC],
                                                 h_c[:, 512 * g:512 * g + 512], start=(half == 0), stop=(half == 1))
                        last.then_inc(S["folded"], 1)

                @block.vector
                def _(v):
                    step = Chain(v, S["dve_step"])

                    def norm(dst, src, rows, c, wait, ready, gain=None):
                        v.wait_ge(wait, 1)
                        inv = st[0:rows, c + 2:c + 3]
                        step(v.reciprocal(inv, st[0:rows, c:c + 1]))
                        if gain is None:
                            v.tensor_scalar(dst, src, inv, None, ALU.mult).then_inc(ready, 1)
                        else:
                            v.scalar_tensor_tensor(out=dst, in0=src, scalar=inv, in1=gain,
                                                   op0=ALU.mult, op1=ALU.mult).then_inc(ready, 1)

                    def turned(dst, rows, banks, wait, ready, gain=None):
                        v.wait_ge(wait, 1)
                        for g in range(2):
                            src = four(banks[g])[:, :, 0:rows]
                            d = dst[:, 4 * g:4 * g + 4, 0:rows]
                            if gain is None:
                                v.tensor_copy(d, src).then_inc(ready, 1)
                            else:
                                v.tensor_tensor(d, src, bcast(gain[:, 4 * g:4 * g + 4], rows), ALU.mult)\
                                    .then_inc(ready, 1)

                    def tail_norm():
                        yield
                        v.wait_ge(S["pT_tr"], 1)
                        v.tensor_copy(pT[:, :, 0:t_rows], TB[0][:, 0:2 * P].rearrange("p (a c) -> p a c", a=2)
                                      [:, :, 0:t_rows]).then_inc(S["pT_ready"], 1)
                        norm(tn[0:t_rows, :], h2[0:t_rows, :], t_rows, 8, S["rms_ple"], S["t_ready"])
                        yield
                        turned(tT, t_rows, SB, S["t_tr"], S["tT_ready"], g_ple)

                    def tail_proj(g):
                        yield
                        name = f"proj{g}"
                        n = number[name]
                        wait_out(v, f"gate{2 * g}", f"gate{2 * g + 1}")
                        v.wait_ge(S["proj_done"], n + 1)
                        c = slice(512 * g, 512 * g + 512)
                        step(v.tensor_tensor(sg[0:t_rows, c], AB[n % 2][0:t_rows, :], sg[0:t_rows, c], ALU.mult))
                        v.tensor_tensor(h2[0:t_rows, c], h2[0:t_rows, c], sg[0:t_rows, c], ALU.add)\
                            .then_inc(S["h3_ready"], 1)
                        v.engine_nop().then_inc(proj_out[n % 2], 1)

                    def tail_fin():
                        yield
                        norm(tn[0:t_rows, :], h2[0:t_rows, :], t_rows, 12, S["rms_fin"], S["y_ready"], g_fin[0:t_rows, :])

                    def norm_mix():
                        if f_sample:
                            v.memset(x[DEC:P, :], 0.0).then_inc(S["halo_done"], 1)
                        yield
                        norm(an[:], x[:], P, 0, S["rms_mix"], S["a_ready"])
                        yield
                        turned(aT, P, AB, S["a_tr"], S["aT_ready"], g_mix)

                    def conv(g):
                        wait_out(v, f"conv_in{2 * g}", f"conv_in{2 * g + 1}")
                        b = slice(4 * g, 4 * g + 4)
                        scratch = part(2 * g, 512, a=4)
                        step(v.tensor_tensor(cT[:, b, :], zT[:, b, 0:P], bcast(taps[:, 0, b], P), ALU.mult))
                        for j in range(1, CW):
                            step(v.tensor_tensor(scratch, zT[:, b, j:j + P], bcast(taps[:, j, b], P), ALU.mult))
                            if j < CW - 1:
                                step(v.tensor_tensor(cT[:, b, :], cT[:, b, :], scratch, ALU.add))
                        v.tensor_tensor(cT[:, b, :], cT[:, b, :], scratch, ALU.add).then_inc(S["conv_in"], 1)
                        if not f_sample:
                            step(v.tensor_copy(zT[:, b, 0:CW - 1], zT[:, b, P:P + CW - 1]))
                        yield
                        if g < 2:
                            yield
                            v.wait_ge(S["c_tr"], g + 1)
                            step(v.tensor_copy(ctok[:, b, :], four(SB[g])))

                    def gates():
                        wait_out(v, "ba_g", "fox_v1")
                        step(v.tensor_tensor(y12[:, 0:HA], zba[:, HA:], bias12[:, 0:HA], ALU.add))
                        step(v.tensor_tensor(y12[:, HA:], zf[:], bias12[:, HA:], ALU.add))
                        step(v.tensor_scalar(y12[:, HA:], y12[:, HA:], -1.0, None, ALU.mult))
                        v.scalar_tensor_tensor(out=e12[:], in0=y12[:], scalar=-1.0, in1=y12[:],
                                               op0=ALU.mult, op1=ALU.max).then_inc(S["y_gate"], 1)
                        yield
                        v.wait_ge(S["e_gate"], 1)
                        step(v.scalar_tensor_tensor(out=y12[:], in0=y12[:], scalar=0.0, in1=l12[:],
                                                    op0=ALU.max, op1=ALU.add))
                        step(v.tensor_tensor(la[:], y12[:, 0:HA], neg_a[:], ALU.mult))
                        if f_sample:
                            v.wait_ge(S["c_mm"], 1)
                        step(v.tensor_scalar(logf[:], y12[:, HA:], -1.0, None, ALU.mult))
                        step(v.tensor_scalar(bex[:], bex[:], 1.0, None, ALU.add))
                        step(v.reciprocal(beta[:], bex[:]))
                        if f_sample:
                            step(v.tensor_scalar(beta[:], beta[:], valid[:], None, ALU.mult))
                            step(v.tensor_scalar(la[:], la[:], valid[:], None, ALU.mult))
                        step(v.tensor_copy(lf40[:, 32:40], logf[:]))
                        v.tensor_scalar(lf40[:, 0:HB], logf[:], -1.0, None, ALU.mult).then_inc(S["lf_ready"], 1)

                    def gdn():
                        sq = tmp[:].rearrange("p (a c) -> p a c", a=8)
                        step(v.tensor_tensor(sq, ctok[:, 0:8, :], ctok[:, 0:8, :], ALU.mult))
                        v.tensor_reduce(st2[:], sq, AX.X, ALU.add).then_inc(S["ss_gdn"], 1)
                        yield
                        v.wait_ge(S["lf_ready"], 1)
                        step(v.tensor_tensor(latri, over(tri_gt[:], HA), bcast(la[:], P), ALU.mult))
                        v.wait_ge(S["rms_gdn"], 1)
                        step(v.reciprocal(st2[:], st2[:]))
                        step(v.tensor_scalar(st2[:, 0:4], st2[:, 0:4], P ** -0.5, None, ALU.mult))
                        step(v.tensor_tensor(ctok[:, 0:8, :], ctok[:, 0:8, :], bcast(st2[:], P), ALU.mult))
                        v.tensor_tensor(kb, ctok[:, 4:8, :], bcast(beta[:], P), ALU.mult).then_inc(S["qkb_ready"], 1)
                        yield
                        yield
                        v.wait_ge(S["qkb_tr"], 1)
                        v.tensor_copy(cT[:, 8:12, :], four(TB[1])).then_inc(S["kbT_out"], 1)
                        v.wait_ge(S["dec_exp"], 1)
                        step(v.tensor_tensor(dec, dec, over(tri_le[:], HA), ALU.mult))
                        yield
                        v.wait_ge(S["dec_exp"], 2)
                        step(v.tensor_tensor(kb, ctok[:, 4:8, :], bcast(ge[:, 4:8], P), ALU.mult))
                        step(v.tensor_scalar(neg_eg[:], ge[:, 0:4], -1.0, None, ALU.mult))
                        v.wait_ge(S["kk_mm"], 1)
                        v.tensor_tensor(mt, four(SB[0]), dec, ALU.mult)
                        v.tensor_tensor(attnT, four(SB[1]), dec, ALU.mult).then_inc(S["mt_ready"], 1)

                    def inverse(l):
                        if l == 0:
                            yield
                            v.wait_ge(S["inv_ct"], 1)
                            v.tensor_tensor(ttinv, over(ident[:], HA), ct[0], ALU.subtract)
                            v.wait_ge(S["x_mm"], 1)
                            v.tensor_tensor(tinv, over(ident[:], HA), four(AB[0]), ALU.subtract)\
                                .then_inc(S["t_out"], 1)
                            return
                        yield
                        yield
                        v.wait_ge(S["d_mm"], l)
                        v.wait_ge(S["t_out"], l)
                        if l < LEVELS - 1:
                            v.tensor_tensor(tinv, tinv, four(AB[0]), ALU.subtract)
                        v.tensor_tensor(ttinv, ttinv, four(AB[1]), ALU.subtract).then_inc(S["t_out"], 1)

                    def state_u():
                        yield
                        v.wait_ge(S["state_mm"], 1)
                        for h in range(HA):
                            last = v.scalar_tensor_tensor(out=rr[:, h, :], in0=AB[0][:, h * P:(h + 1) * P],
                                                          scalar=neg_eg[:, h:h + 1], in1=ctok[:, 8 + h, :],
                                                          op0=ALU.mult, op1=ALU.add)
                        step(last)
                        v.tensor_tensor(rr, rr, bcast(beta[:], P), ALU.mult).then_inc(S["r_ready"], 1)
                        oA = mix[:, 0:512].rearrange("p (a c) -> p a c", a=HA)
                        v.tensor_tensor(oA, four(AB[1]), bcast(ge[:, 0:4], P), ALU.mult).then_inc(S["qs_out"], 1)
                        yield
                        yield
                        yield
                        v.wait_ge(S["o_mm"], 1)
                        v.wait_ge(S["qs_out"], 1)
                        step(v.tensor_tensor(oA, oA, four(AB[0]), ALU.add))
                        for h in range(HA):
                            last = v.scalar_tensor_tensor(out=state[:, h, :], in0=state[:, h, :],
                                                          scalar=ge[:, 8 + h:9 + h], in1=AB[1][:, h * P:(h + 1) * P],
                                                          op0=ALU.mult, op1=ALU.add)
                        last.then_inc(S["s_ready"], 1)

                    def gdn_norm():
                        o = mix[:, 0:512].rearrange("p (a c) -> p a c", a=HA)
                        sq = tmp[:, 0:512].rearrange("p (a c) -> p a c", a=HA)
                        step(v.tensor_tensor(sq, o, o, ALU.mult))
                        v.tensor_reduce(st4[:], sq, AX.X, ALU.add).then_inc(S["ssn_gdn"], 1)
                        yield
                        v.wait_ge(S["rmsn_gdn"], 1)
                        step(v.reciprocal(st4[:], st4[:]))
                        step(v.tensor_tensor(o, o, bcast(st4[:], P), ALU.mult))
                        step(v.tensor_tensor(o, o, over(g_gdn[:], HA), ALU.mult))
                        v.wait_ge(S["silu_go"], 1)
                        v.tensor_tensor(o, o, zg[:].rearrange("p (a c) -> p a c", a=HA), ALU.mult)\
                            .then_inc(S["oA_ready"], 1)

                    def cumulate(key, n):
                        v.wait_ge(S["c_mm"], n)
                        step(v.tensor_scalar(c40[:], TB[1][:, 0:P], carry[:], None, ALU.add))
                        step(v.tensor_copy(carry[:], c40[:, P - 1:P]))
                        return v.tensor_copy(aux[0:HB, key], c40[0:HB, :])

                    def fox_past():
                        if not f_sample:
                            return
                        v.wait_ge(S["past_loaded"], 48)
                        step(v.memset(carry[:], 0.0))
                        step(v.memset(pos[:], float(P)))
                        step(v.tensor_copy(lf40[:, 32:40], logf[:]))
                        v.tensor_scalar(lf40[:, 0:HB], logf[:], -1.0, None, ALU.mult)\
                            .then_inc(S["lf_past_ready"], 1)
                        yield
                        yield
                        cumulate(slice(0, P), 1).then_inc(S["aux_ready"], 1)
                        v.wait_ge(S["aux_ready"], 1)

                    def fox_keys():
                        yield
                        step(cumulate(f_key, 2 if f_sample else 1))
                        step(v.memset(c40[0:HB, :], 1.0))
                        if tail:
                            v.wait_ge(S["y_stored"], 16)
                        v.tensor_tensor(faux, over(c40[:], HB), bcast(sel[:], P), ALU.mult)\
                            .then_inc(S["aux_ready"], 1)
                        v.wait_ge(S["cm_iota"], 1)
                        step(v.tensor_scalar(cm[:, 0:keys], cm[:, 0:keys], pos[:], NEG, ALU.is_gt, ALU.mult))
                        step(v.tensor_scalar(pos[:], pos[:], float(P), None, ALU.add))

                    def fox_s(h):
                        yield
                        v.wait_ge(S["s_mm"], h + 1)
                        if h >= 2:
                            v.wait_ge(S["p_tr"], n_halves * (h - 1))
                        for g, own in enumerate(halves):
                            c = slice(P * own[0], P * own[-1] + P)
                            last = v.tensor_tensor_reduce(out=pbuf[h % 2][:, c], in0=SB[g][:, 0:P * len(own)],
                                                          in1=cm[:, c], scale=1.0, scalar=NEG * 10,
                                                          op0=ALU.add, op1=ALU.max, accum_out=fst[:, g:g + 1])
                        step(last)
                        if n_halves == 2:
                            step(v.tensor_tensor(fst[:, 0:1], fst[:, 0:1], fst[:, 1:2], ALU.max))
                        v.tensor_scalar(fneg[:, h:h + 1], fst[:, 0:1], -1.0, None, ALU.mult).then_inc(S["s_max"], 1)
                        v.wait_ge(S["s_max"], h + 1)

                    def fox_norm():
                        v.wait_ge(S["o_fox"], HB)
                        v.wait_ge(S["p_exp"], HB)
                        step(v.reciprocal(finv[:], fsum[:]))
                        o = mix[:, 512:].rearrange("p (a c) -> p a c", a=HB)
                        sq = tmp[:, 0:512].rearrange("p (a c) -> p a c", a=HB)
                        step(v.tensor_tensor(o, TB[1][:].rearrange("p (a c) -> p a c", a=HB), bcast(finv[:], DHB), ALU.mult))
                        step(v.tensor_tensor(sq, o, o, ALU.mult))
                        v.tensor_reduce(st2[:], sq, AX.X, ALU.add).then_inc(S["ss_fox"], 1)
                        yield
                        v.wait_ge(S["rms_fox"], 1)
                        step(v.reciprocal(st2[:], st2[:]))
                        step(v.tensor_tensor(o, o, bcast(st2[:], DHB), ALU.mult))
                        v.tensor_tensor(o, o, over(g_fox[:], HB), ALU.mult).then_inc(S["oB_ready"], 1)

                    def mix_turn():
                        yield
                        turned(aT, P, TB, S["mix_tr"], S["mixT_ready"])

                    def out_proj(j):
                        yield
                        n = number[f"out{j}"]
                        v.wait_ge(S["proj_done"], n + 1)
                        v.tensor_tensor(x[:, 256 * j:256 * j + 256], x[:, 256 * j:256 * j + 256],
                                        AB[n % 2][:, 0:256], ALU.add).then_inc(S["h1_ready"], 1)
                        v.engine_nop().then_inc(proj_out[n % 2], 1)

                    def norm_ffn():
                        yield
                        norm(an[:], x[:], P, 4, S["rms_ffn"], S["xn_ready"], g_ffn[:])
                        yield
                        yield
                        turned(aT, P, TB, S["xn_tr"], S["xnT_ready"])

                    def top16(trios, width):
                        work = [eq[:, n, 0:width] for n in range(len(trios))]
                        for values, vals, _ in trios:
                            last = v.max(vals[:, 0:8], values)
                        step(last)
                        for values, vals, idxs in trios:
                            v.max_index(idxs[:, 0:8], vals[:, 0:8], values)
                        for (values, vals, _), w in zip(trios, work):
                            last = v.match_replace(w, vals[:, 0:8], values, NEG * 100)
                        step(last)
                        for (_, vals, _), w in zip(trios, work):
                            last = v.max(vals[:, 8:16], w)
                        step(last)
                        for (_, vals, idxs), w in zip(trios, work):
                            last = v.max_index(idxs[:, 8:16], vals[:, 8:16], w)
                        step(last)

                    def pick_halves(h):
                        if h % 2 == 0:
                            v.wait_ge(S["sc_out"], h // 2 + 1)
                        top16([(sc[:, m, :], sv[:, m, :], si[:, m, :]) for m in (2 * h, 2 * h + 1)], KEYS)

                    def pick_pairs(n):
                        heads = (2 * n, 2 * n + 1)
                        for h in heads:
                            last = v.tensor_tensor(cand[:, h, :].rearrange("p (a b) -> p a b", a=TOP),
                                                   bcast(sv[:, 2 * h, :], TOP), over(sv[:, 2 * h + 1, :], TOP), ALU.add)
                        step(last)
                        top16([(cand[:, h, :], cv[:, h, :], ci[:, h, :]) for h in heads], TOP * TOP)

                    def pick_gate():
                        g3 = gate_n[:].rearrange("p (h k) -> p h k", h=HP)
                        v.tensor_tensor(g3, cv[:], cv[:, :, 0:1].to_broadcast([P, HP, TOP]), ALU.subtract)\
                            .then_inc(S["top_v"], 1)
                        step(v.tensor_copy(sif[:], si[:]))
                        step(v.tensor_scalar(cd[:], ci[:], 15, None, ALU.bitwise_and))
                        step(v.tensor_copy(cf[:], cd[:]))
                        for h in range(HP):
                            last = v.tensor_tensor(eq2[:, h, :].rearrange("p (a b) -> p a b", a=TOP),
                                                   bcast(cf[:, h, :], TOP), over(iota16[:], TOP), ALU.is_equal)
                        last.then_inc(S["eq2_ready"], 1)
                        v.wait_ge(S["eq2_ready"], 1)
                        yield
                        step(v.tensor_scalar(cd[:], ci[:], 4, None, ALU.logical_shift_right))
                        step(v.tensor_copy(cf[:], cd[:]))
                        for h in range(HP):
                            last = v.tensor_tensor(eq[:, h, :].rearrange("p (a b) -> p a b", a=TOP),
                                                   bcast(cf[:, h, :], TOP), over(iota16[:], TOP), ALU.is_equal)
                        step(last)
                        yield
                        for h in range(HP):
                            e3 = eq[:, h, :].rearrange("p (a b) -> p a b", a=TOP)
                            last = v.tensor_tensor(e3, e3, over(sif[:, 2 * h, :], TOP), ALU.mult)
                        step(last)
                        yield
                        step(v.tensor_reduce(ef[:, 0, :, :], eq.rearrange("p h (a b) -> p h a b", a=TOP), AX.X, ALU.add))
                        v.wait_ge(S["eq2_times"], 1)
                        step(v.tensor_reduce(ef[:, 1, :, :], eq2.rearrange("p h (a b) -> p h a b", a=TOP), AX.X, ALU.add))
                        yield
                        step(v.scalar_tensor_tensor(out=ef[:, 0, :, :], in0=ef[:, 0, :, :], scalar=float(KEYS),
                                                    in1=ef[:, 1, :, :], op0=ALU.mult, op1=ALU.add))
                        if f_sample:
                            half = HP // 2
                            i3 = idx_n[:].rearrange("p (h k) -> p h k", h=HP)
                            v.tensor_copy(i3[0:DEC], ef[0:DEC, 0, :, :])
                            v.tensor_copy(i3[DEC:P, 0:half], ef[DEC:P, 0, half:HP, :])
                        else:
                            v.tensor_copy(idx_n[:].rearrange("p (h k) -> p h k", h=HP), ef[:, 0, :, :])
                        v.wait_ge(S["gate_e"], 1)
                        step(v.tensor_reduce(st2[:], g3, AX.X, ALU.add))
                        step(v.reciprocal(st2[:], st2[:]))
                        if f_sample:
                            step(v.tensor_tensor(g3, g3, bcast(st2[:], TOP), ALU.mult))
                            v.tensor_copy(g3[DEC:P, 0:half], g3[DEC:P, half:HP]).then_inc(S["gate_done"], 1)
                        else:
                            v.tensor_tensor(g3, g3, bcast(st2[:], TOP), ALU.mult).then_inc(S["gate_done"], 1)

                    stages = dict(tail_norm=tail_norm, tail_fin=tail_fin, norm_mix=norm_mix, gates=gates, gdn=gdn,
                                  state=state_u, gdn_norm=gdn_norm, fox_past=fox_past, fox_keys=fox_keys,
                                  fox_norm=fox_norm, mix_turn=mix_turn, norm_ffn=norm_ffn, pick_gate=pick_gate)
                    stages.update({f"proj{g}": (lambda g=g: tail_proj(g)) for g in range(2)})
                    stages.update({f"conv{g}": (lambda g=g: conv(g)) for g in range(3)})
                    stages.update({f"inv{l}": (lambda l=l: inverse(l)) for l in range(LEVELS)})
                    stages.update({f"fox_s{h}": (lambda h=h: fox_s(h)) for h in range(HB)})
                    stages.update({f"out{j}": (lambda j=j: out_proj(j)) for j in range(4)})
                    stages.update({f"halves{h}": (lambda h=h: pick_halves(h)) for h in range(HP)})
                    stages.update({f"pairs{n}": (lambda n=n: pick_pairs(n)) for n in range(HP // 2)})
                    next_part = walker(stages)
                    last_add = None
                    for s in range(len(plan)):
                        for name in plan[s]:
                            next_part(name)
                        if not peer:
                            continue
                        if s and s % HEAD_SLOTS == 0 and s // HEAD_SLOTS <= sched.picks // TOP:
                            h = s // HEAD_SLOTS - 1
                            v.wait_ge(S["w_gelu"], h + 1)
                            c = slice(TOP * h, TOP * h + TOP)
                            v.tensor_tensor(wgt[0:peer, c], wgt[0:peer, c], gate_c[0:peer, c], ALU.mult)\
                                .then_inc(S["w_ready"], 1)
                        for kind, k in sched.order[s]:
                            n = sched.number[kind, k]
                            r = n % RING
                            row = ring[0:peer, r, :]
                            if kind == "u":
                                wait_landed(v, n)
                                v.tensor_tensor_reduce(out=row, in0=row, in1=xn_c[0:peer, :], scale=1.0, scalar=0.0,
                                                       op0=ALU.mult, op1=ALU.add, accum_out=dots[0:peer, k:k + 1])\
                                    .then_inc(consumed[r], 1)
                            elif k not in sched.tensor:
                                wait_landed(v, n)
                                v.wait_ge(S["w_ready"], k // TOP + 1)
                                if last_add is not None:
                                    wait_used(v, *last_add)
                                v.scalar_tensor_tensor(out=h_c[0:peer, :], in0=row, scalar=wgt[0:peer, k:k + 1],
                                                       in1=h_c[0:peer, :], op0=ALU.mult, op1=ALU.add)\
                                    .then_inc(consumed[r], 1)
                                last_add = (kind, k)
                    if peer:
                        wait_used(v, *last_add)
                        wait_used(v, "v", sched.tensor_picks[-1])
                        dst = h_c if sched is FOLDED else h2
                        for g in range(2):
                            c = slice(512 * g, 512 * g + 512)
                            last = v.tensor_tensor(dst[0:peer, c], h_c[0:peer, c], YB[g][0:peer, :], ALU.add)
                        if sched is FOLDED:
                            last.then_inc(S["sum_ready"], 1)
                            v.wait_ge(S["folded"], 1)
                            for g in range(2):
                                last = v.tensor_copy(h2[0:DEC, 512 * g:512 * g + 512], SB[g][0:DEC, :])
                        last.then_inc(S["h2_ready"], 1)
                    if front and f_sample:
                        v.wait_ge(S["h2_ready"], 1)
                        v.memset(h_c[DEC:P, :], 0.0)
                    if front:
                        v.wait_ge(S["gate_done"], 1)
                        v.tensor_copy(idx_c[:], idx_n[:])
                        v.tensor_copy(gate_c[:], gate_n[:])
            nc.all_engine_barrier(sems_to_clear=range(numbers[0], numbers[-1] + 1))

        body(front=(0, P, 0, False), blocks=1, plan=[FIRST_PLAN])
        body(front=(1, P, 1, False), peer=P, blocks=2)
        with nc.Fori(2, TILES // 2) as i:
            body(front=(i, P, i, False), peer=P, tail=(i - 2, P, False), blocks=TILES // 2)
        with nc.Fori(TILES // 2, TILES) as i:
            body(front=(i, P, i, False), peer=P, tail=(i - 2, P, False), blocks=TILES)
        gates = ("gate0", "gate1", "gate2")
        body(front=(0, DEC, 1, True), peer=P, tail=(TILES - 2, P, False), blocks=2, upcoming=gates)
        body(peer=P, tail=(TILES - 1, P, False), first=gates, upcoming=gates, sched=FOLDED)
        body(tail=(0, DEC, True), first=gates, upcoming=())


def first_plan():
    ins = [[f"conv_in{j}"] for j in range(6)] + [[n] for n in
           ("fox_v1", "ba_g", "fox_v0", "fox_k0", "fox_k1", "fox_q0", "fox_q1", "g")]
    between = {1: ["conv0"], 3: ["conv0", "conv1"], 4: ["conv0"], 5: ["conv1", "conv2"], 6: ["conv1"], 7: ["conv2"],
               8: ["gates", "conv2", "gates", "gdn"], 9: ["gdn"], 11: ["gdn"], 12: ["gdn"], 13: ["gdn", "fox_keys", "fox_keys"]}
    plan = ["norm_mix"] * 3
    for n, own in enumerate(ins):
        plan += own + between.get(n, [])
    fox = []
    for h in range(HB):
        fox += [f"fox_s{h}", f"fox_s{h}", f"fox_o{h}", f"fox_o{h}", f"fox_o{h}"]
    gdn = ["inv0", "inv0"] + [f"inv{l}" for l in range(1, LEVELS) for _ in range(3)] + ["state"] * 5 + ["gdn_norm"] * 2
    per = -(-len(fox) // (len(gdn) - 6))
    for n, name in enumerate(gdn):
        plan += [name] + fox[max(n - 2, 0) * per:max(n - 1, 0) * per]
        if n == 4:
            plan += ["silu_g"]
    plan += ["fox_norm"] * 2 + ["mix_turn"] * 2
    for j in range(4):
        plan += [f"out{j}"] + ([f"out{j - 1}"] if j else [])
    plan += ["out3"] + ["norm_ffn"] * 4
    for j in range(HP):
        plan += [f"wq{j}"]
        if j % 2:
            g = j // 2
            plan += [f"scores{g}", f"halves{2 * g}", f"halves{2 * g + 1}", f"pairs{g}"]
    return plan + ["pick_gate"] * 6 + ["hand_rows"]


def make_plan():
    plan = [[] for _ in range(FULL.slots)]

    def at(slot, *names):
        plan[slot].extend(names)

    def spread(name, *slots):
        for s in slots:
            at(s, name)

    spread("tail_norm", 0, 1, 2)
    spread("norm_mix", 0, 1, 2)
    spread("fox_past", 3, 4, 5)
    for j in range(6):
        at(3 + j, f"conv_in{j}")
    for g in range(3):
        spread(f"conv{g}", 5 + 2 * g, 6 + 2 * g, 7 + 2 * g)
    at(9, "ba_g")
    at(10, "fox_v1")
    spread("gates", 11, 12)
    for j in range(4):
        at(11 + j, f"gate{j}")
    spread("gdn", 12, 13, 14, 15, 16)
    at(15, "proj0")
    at(16, "proj0", "proj1", "fox_v0")
    at(17, "proj1", "fox_k0")
    spread("tail_fin", 18, 19, 20)
    at(18, "fox_k1")
    at(19, "fox_q0")
    at(20, "fox_q1")
    spread("fox_keys", 20, 21)
    at(21, "g")
    at(22, "silu_g")
    s = 22
    spread("inv0", s, s + 1)
    for l in range(1, LEVELS):
        spread(f"inv{l}", s + 2 * l - 1, s + 2 * l, s + 2 * l + 1)
    s += 2 * LEVELS
    spread("state", s, s + 2, s + 3, s + 4, s + 5)
    spread("gdn_norm", s + 6, s + 7)
    start = [21 + (9 * h + 2) // 4 for h in range(HB)] + [99]
    for h in range(HB):
        s = start[h]
        spread(f"fox_s{h}", *([s] if s != start[h - 1] + 2 else []), s + 1)
        at(s + 2, f"fox_o{h}")
        if start[h + 1] == s + 2:
            at(s + 2, f"fox_s{h + 1}")
        spread(f"fox_o{h}", s + 2, s + 3)
    spread("fox_norm", s + 5, s + 6)
    spread("mix_turn", s + 7, s + 8)
    s += 9
    for j in range(4):
        spread(f"out{j}", s + (2 * j) // 3, s + (2 * j) // 3 + 1)
    s += 3
    spread("norm_ffn", s, s + 1, s + 2, s + 3)
    s += 3
    for j in range(HP):
        at(s + j, f"wq{j}")
        if j % 2:
            at(s + j, f"scores{j // 2}")
            at(s + j + 1, f"halves{j - 1}")
            at(s + j + 2, f"halves{j}")
            at(s + j + 3, f"pairs{j // 2}")
    s += HP + 3
    spread("pick_gate", s, s + 1, s + 2, s + 3, s + 4, s + 5)
    at(HP * HEAD_SLOTS + 1, "hand_rows")
    assert s + 5 < FULL.slots, s
    return plan


PLAN = make_plan()
FIRST_PLAN = first_plan()

_INS = ["x_prompt", "x_sample", "p_prompt", "p_sample", "cache_conv", "state_gdn", "cache_fox_k", "cache_fox_v",
        "cache_fox_logf", "w_in", "conv_w", "a_log", "dt_bias", "gdn_onorm", "b_f", "fox_onorm", "w_out", "norm_mix",
        "norm_ffn", "peer_wq", "peer_keys", "peer_u", "peer_v", "norm_ple", "w_ple_proj", "w_ple_gate", "norm_final"]
_OUTS = [("y_prompt", (1, SEQ, D)), ("y_sample", (1, DEC, D)),
         ("conv_prompt", (1, 1, CW - 1, CONV)), ("gdn_prompt", (1, 1, HA, P, P)),
         ("k_prompt", (1, 1, SEQ, HB, DHB)), ("v_prompt", (1, 1, SEQ, HB, DHB)), ("logf_prompt", (1, 1, SEQ, HB)),
         ("conv_sample", (1, 1, CW - 1, CONV)), ("gdn_sample", (1, 1, HA, P, P)),
         ("k_sample", (1, 1, DEC, HB, DHB)), ("v_sample", (1, 1, DEC, HB, DHB)), ("logf_sample", (1, 1, DEC, HB))]


def kernel(**inputs):
    import numpy as _np
    import concourse.bacc as _bacc
    from concourse.bass_utils import run_bass_kernel_spmd as _run

    nc = _bacc.Bacc("TRN2", target_bir_lowering=False, num_devices=1)
    arrays, t, out = {}, {}, {}
    for name in _INS:
        a = _np.ascontiguousarray(inputs[name])
        arrays[name] = a
        t[name] = nc.dram_tensor(name, a.shape, F32, kind="ExternalInput").ap()
    t["peer_u"] = t["peer_u"].rearrange("a e d -> (a e) d")
    t["peer_v"] = t["peer_v"].rearrange("a e d -> (a e) d")
    for name, shape in _OUTS:
        out[name] = nc.dram_tensor("out_" + name, shape, F32, kind="ExternalOutput").ap()
    build(nc, t, out)
    r = _run(nc, [arrays], core_ids=[0])
    return tuple(r.results[0]["out_" + name] for name, _ in _OUTS)
```
